# Optimizing a Trainium2 kernel written in Bass

```python
import math
import jax, jax.numpy as jnp
from jax import lax
import numpy as np

D_MODEL = 1024
BATCH = 1
SEQ = 1024
DEPTH = 1
DEC_BATCH = 8
DEC_SEQ = 1
PAST_LEN = 1024
PAGE_SIZE = 128

MIX_WIDTH = D_MODEL
ATTN_WIDTH = MIX_WIDTH // 2
POOL_WIDTH = MIX_WIDTH - ATTN_WIDTH
HEAD_DIM = 64
N_HEADS = ATTN_WIDTH // HEAD_DIM
SB_SCALE = 1.0 / math.sqrt(HEAD_DIM)
SB_BIAS_INIT = -6.0
Q_BLOCK = 128
POOL_WINDOWS = (2, 4, 8, 16)
N_POOL_GROUPS = len(POOL_WINDOWS)
POOL_GROUP_WIDTH = POOL_WIDTH // N_POOL_GROUPS
POOL_STATE = max(POOL_WINDOWS) - 1
N_EXPERT_GROUPS = 4
EXPERTS_PER_GROUP = 8
N_EXPERTS = N_EXPERT_GROUPS * EXPERTS_PER_GROUP
TOP_K = 2
EXPERT_HIDDEN = D_MODEL // 2
MOE_BLOCK = 128
PLE_DIM = 256
RMS_EPS = 1e-6

kernel_name = 'hymba_stickbreak_pool_hmoe_step'

def rmsnorm(x, g):
    xf = x.astype(jnp.float32)
    xf = xf * lax.rsqrt(jnp.mean(xf * xf, axis=-1, keepdims=True) + RMS_EPS)
    return (xf * g.astype(jnp.float32)).astype(x.dtype)

def project(x, g_mix, w_in, g_q, g_k):
    b, t, _ = x.shape
    z = rmsnorm(x, g_mix) @ w_in
    q = z[..., :ATTN_WIDTH].reshape(b, t, N_HEADS, HEAD_DIM)
    k = z[..., ATTN_WIDTH:2 * ATTN_WIDTH].reshape(b, t, N_HEADS, HEAD_DIM)
    v = z[..., 2 * ATTN_WIDTH:3 * ATTN_WIDTH].reshape(b, t, N_HEADS, HEAD_DIM)
    u = z[..., 3 * ATTN_WIDTH:]
    return rmsnorm(q, g_q), rmsnorm(k, g_k), v, u

def stick_breaking(q, k, v, q_pos, k_pos, bias):
    z = jnp.einsum('bqhd,bkhd->bhqk', q.astype(jnp.float32), k.astype(jnp.float32)) * SB_SCALE
    z = z + bias.astype(jnp.float32)[None, :, None, None]
    mask = k_pos[None, :] < q_pos[:, None]
    log_beta = jax.nn.log_sigmoid(z)
    log_keep = jnp.where(mask, jax.nn.log_sigmoid(-z), 0.0)
    later = lax.cumsum(log_keep, axis=3, reverse=True) - log_keep
    a = jnp.where(mask, jnp.exp(log_beta + later), 0.0)
    return jnp.einsum('bhqk,bkhd->bqhd', a, v.astype(jnp.float32)).astype(v.dtype)

def stick_breaking_prompt(q, k, v, bias):
    b, s, h, d = q.shape
    n_blk = s // Q_BLOCK
    k_pos = jnp.arange(s)

    def one_block(i):
        qb = lax.dynamic_slice_in_dim(q, i * Q_BLOCK, Q_BLOCK, axis=1)
        q_pos = i * Q_BLOCK + jnp.arange(Q_BLOCK)
        return stick_breaking(qb, k, v, q_pos, k_pos, bias)

    out = lax.map(one_block, jnp.arange(n_blk))
    return out.transpose(1, 0, 2, 3, 4).reshape(b, s, h, d)

def pool_mix(u_ext, n_new, start_pos, w_pool, s_pool):
    b, length, c = u_ext.shape
    p0 = length - n_new
    uf = u_ext.astype(jnp.float32)
    cs = jnp.concatenate([jnp.zeros((b, 1, c), jnp.float32), jnp.cumsum(uf, axis=1)], axis=1)
    rows = np.arange(p0, length)
    pos = start_pos + np.arange(n_new)
    end = cs[:, rows + 1]
    u_new = uf[:, p0:]
    outs = []
    for gi, w in enumerate(POOL_WINDOWS):
        sl = slice(gi * POOL_GROUP_WIDTH, (gi + 1) * POOL_GROUP_WIDTH)
        beg = cs[:, np.maximum(rows + 1 - w, 0), sl]
        cnt = jnp.asarray(np.minimum(pos + 1, w), jnp.float32)[None, :, None]
        outs.append((end[..., sl] - beg) / cnt - u_new[..., sl])
    pooled = jnp.stack(outs, axis=2)
    y = jnp.einsum('btgc,gcd->btgd', pooled, w_pool.astype(jnp.float32)).reshape(b, n_new, c)
    return (y * s_pool.astype(jnp.float32)).astype(u_ext.dtype)

def hier_moe(x, w_rg, b_rg, w_re, b_re, w_gate, w_up, w_down):
    n = x.shape[0]
    p_grp = jax.nn.softmax((x @ w_rg).astype(jnp.float32) + b_rg.astype(jnp.float32), axis=-1)
    g_w, g_id = lax.top_k(p_grp, 1)
    le = ((x @ w_re).astype(jnp.float32) + b_re.astype(jnp.float32)).reshape(n, N_EXPERT_GROUPS, EXPERTS_PER_GROUP)
    le = jnp.take_along_axis(le, g_id[:, :, None], axis=1)[:, 0]
    e_w, e_id = lax.top_k(jax.nn.softmax(le, axis=-1), TOP_K)
    gates = g_w * e_w / jnp.sum(e_w, axis=-1, keepdims=True)
    expert = (g_id * EXPERTS_PER_GROUP + e_id).reshape(-1).astype(jnp.int32)
    n_assign = n * TOP_K
    tok = jnp.repeat(jnp.arange(n, dtype=jnp.int32), TOP_K)
    gate_flat = gates.reshape(-1)
    order = jnp.argsort(expert)
    e_s, tok_s, g_s = expert[order], tok[order], gate_flat[order]
    counts = jnp.bincount(expert, length=N_EXPERTS)
    starts = jnp.cumsum(counts) - counts
    pcounts = (counts + MOE_BLOCK - 1) // MOE_BLOCK * MOE_BLOCK
    pends = jnp.cumsum(pcounts)
    pstarts = pends - pcounts
    dest = pstarts[e_s] + jnp.arange(n_assign) - starts[e_s]
    n_blk = (n_assign + N_EXPERTS * (MOE_BLOCK - 1) + MOE_BLOCK - 1) // MOE_BLOCK
    n_slots = n_blk * MOE_BLOCK
    slot_tok = jnp.full((n_slots,), n, jnp.int32).at[dest].set(tok_s)
    slot_gate = jnp.zeros((n_slots,), jnp.float32).at[dest].set(g_s)
    blk_e = jnp.minimum(jnp.searchsorted(pends, jnp.arange(n_blk) * MOE_BLOCK, side='right'), N_EXPERTS - 1)
    x_pad = jnp.concatenate([x, jnp.zeros((1, x.shape[1]), x.dtype)], axis=0)

    def run_block(args):
        tok_b, e = args
        xb = x_pad[tok_b]
        hid = jax.nn.silu(xb @ w_gate[e]) * (xb @ w_up[e])
        return hid @ w_down[e]

    y_slots = lax.map(run_block, (slot_tok.reshape(n_blk, MOE_BLOCK), blk_e)).reshape(n_slots, -1)
    y = jnp.zeros((n + 1, x.shape[1]), jnp.float32).at[slot_tok].add(y_slots.astype(jnp.float32) * slot_gate[:, None])
    return y[:n].astype(x.dtype)

def finish(h, attn, pool, p, w_out, g_ffn, w_rg, b_rg, w_re, b_re, w_gate, w_up, w_down, g_ple, w_ple_gate, w_ple_proj):
    b, t, _ = h.shape
    mixed = jnp.concatenate([attn.reshape(b, t, ATTN_WIDTH), pool.astype(attn.dtype)], axis=-1)
    h = h + mixed @ w_out
    m = rmsnorm(h, g_ffn).reshape(b * t, D_MODEL)
    h = h + hier_moe(m, w_rg, b_rg, w_re, b_re, w_gate, w_up, w_down).reshape(b, t, D_MODEL)
    gate = jax.nn.sigmoid((rmsnorm(h, g_ple) @ w_ple_gate).astype(jnp.float32))
    h = h + (gate * (p @ w_ple_proj).astype(jnp.float32)).astype(h.dtype)
    return h

def setup_inputs(seed: int = 0) -> dict:
    key = jax.random.key(seed)
    ks = jax.random.split(key, 32)
    f32 = jnp.float32

    def nrm(k, shape, scale=1.0):
        return jax.random.normal(k, shape, f32) * scale

    n_pages = PAST_LEN // PAGE_SIZE
    n_used = DEC_BATCH * n_pages
    n_phys = n_used + max(1, n_used // 4)
    page_table = jax.random.permutation(ks[0], n_phys)[:n_used].reshape(DEC_BATCH, n_pages).astype(jnp.int32)
    n_in = 3 * ATTN_WIDTH + POOL_WIDTH
    return {
        'x_prompt': nrm(ks[1], (BATCH, SEQ, D_MODEL)),
        'x_sample': nrm(ks[2], (DEC_BATCH, DEC_SEQ, D_MODEL)),
        'cache_k': nrm(ks[3], (DEPTH, n_phys, PAGE_SIZE, N_HEADS, HEAD_DIM)),
        'cache_v': nrm(ks[4], (DEPTH, n_phys, PAGE_SIZE, N_HEADS, HEAD_DIM)),
        'state_pool': nrm(ks[5], (DEPTH, DEC_BATCH, POOL_STATE, POOL_WIDTH)),
        'page_table': page_table,
        'p_prompt': nrm(ks[6], (DEPTH, BATCH, SEQ, PLE_DIM)),
        'p_sample': nrm(ks[7], (DEPTH, DEC_BATCH, DEC_SEQ, PLE_DIM)),
        'g_mix': 1.0 + nrm(ks[8], (DEPTH, D_MODEL), 0.05),
        'w_in': nrm(ks[9], (DEPTH, D_MODEL, n_in), D_MODEL ** -0.5),
        'g_q': 1.0 + nrm(ks[10], (DEPTH, HEAD_DIM), 0.05),
        'g_k': 1.0 + nrm(ks[11], (DEPTH, HEAD_DIM), 0.05),
        'b_sb': SB_BIAS_INIT + nrm(ks[26], (DEPTH, N_HEADS), 0.5),
        'w_pool': nrm(ks[12], (DEPTH, N_POOL_GROUPS, POOL_GROUP_WIDTH, POOL_GROUP_WIDTH), POOL_GROUP_WIDTH ** -0.5),
        's_pool': 1.0 + nrm(ks[13], (DEPTH, POOL_WIDTH), 0.1),
        'w_out': nrm(ks[14], (DEPTH, MIX_WIDTH, D_MODEL), MIX_WIDTH ** -0.5),
        'g_ffn': 1.0 + nrm(ks[15], (DEPTH, D_MODEL), 0.05),
        'w_router_group': nrm(ks[16], (DEPTH, D_MODEL, N_EXPERT_GROUPS), D_MODEL ** -0.5),
        'b_router_group': nrm(ks[17], (DEPTH, N_EXPERT_GROUPS), 0.01),
        'w_router_expert': nrm(ks[18], (DEPTH, D_MODEL, N_EXPERTS), D_MODEL ** -0.5),
        'b_router_expert': nrm(ks[19], (DEPTH, N_EXPERTS), 0.01),
        'w_gate': nrm(ks[20], (DEPTH, N_EXPERTS, D_MODEL, EXPERT_HIDDEN), D_MODEL ** -0.5),
        'w_up': nrm(ks[21], (DEPTH, N_EXPERTS, D_MODEL, EXPERT_HIDDEN), D_MODEL ** -0.5),
        'w_down': nrm(ks[22], (DEPTH, N_EXPERTS, EXPERT_HIDDEN, D_MODEL), EXPERT_HIDDEN ** -0.5),
        'g_ple': 1.0 + nrm(ks[23], (DEPTH, D_MODEL), 0.05),
        'w_ple_gate': nrm(ks[24], (DEPTH, D_MODEL, D_MODEL), D_MODEL ** -0.5),
        'w_ple_proj': nrm(ks[25], (DEPTH, PLE_DIM, D_MODEL), PLE_DIM ** -0.5),
    }

def reference(x_prompt, x_sample, cache_k, cache_v, state_pool, page_table, p_prompt, p_sample,
              g_mix, w_in, g_q, g_k, b_sb, w_pool, s_pool, w_out, g_ffn,
              w_router_group, b_router_group, w_router_expert, b_router_expert,
              w_gate, w_up, w_down, g_ple, w_ple_gate, w_ple_proj):
    n_pages = page_table.shape[1]
    past_len = n_pages * PAGE_SIZE
    dec_b, dec_t, _ = x_sample.shape
    hp, hs = x_prompt, x_sample
    kp_list, vp_list, pp_list, ks_list, vs_list, ps_list = [], [], [], [], [], []
    for i in range(DEPTH):
        tail = (w_out[i], g_ffn[i], w_router_group[i], b_router_group[i], w_router_expert[i], b_router_expert[i],
                w_gate[i], w_up[i], w_down[i], g_ple[i], w_ple_gate[i], w_ple_proj[i])
        q, k, v, u = project(hp, g_mix[i], w_in[i], g_q[i], g_k[i])
        attn = stick_breaking_prompt(q, k, v, b_sb[i])
        pool = pool_mix(u, u.shape[1], 0, w_pool[i], s_pool[i])
        hp = finish(hp, attn, pool, p_prompt[i], *tail)
        kp_list.append(k)
        vp_list.append(v)
        pp_list.append(u[:, -POOL_STATE:])
        q, k, v, u = project(hs, g_mix[i], w_in[i], g_q[i], g_k[i])
        k_past = cache_k[i][page_table].reshape(dec_b, past_len, N_HEADS, HEAD_DIM).astype(k.dtype)
        v_past = cache_v[i][page_table].reshape(dec_b, past_len, N_HEADS, HEAD_DIM).astype(v.dtype)
        k_all = jnp.concatenate([k_past, k], axis=1)
        v_all = jnp.concatenate([v_past, v], axis=1)
        attn = stick_breaking(q, k_all, v_all, past_len + jnp.arange(dec_t), jnp.arange(past_len + dec_t), b_sb[i])
        ext = jnp.concatenate([state_pool[i].astype(u.dtype), u], axis=1)
        pool = pool_mix(ext, dec_t, past_len, w_pool[i], s_pool[i])
        hs = finish(hs, attn, pool, p_sample[i], *tail)
        ks_list.append(k)
        vs_list.append(v)
        ps_list.append(ext[:, -POOL_STATE:])
    k_prompt = jnp.stack(kp_list)
    v_prompt = jnp.stack(vp_list)
    pool_prompt = jnp.stack(pp_list)
    k_sample = jnp.stack(ks_list)
    v_sample = jnp.stack(vs_list)
    pool_sample = jnp.stack(ps_list)
    return (hp, hs, k_prompt, v_prompt, pool_prompt, k_sample, v_sample, pool_sample)


_drawn_inputs = setup_inputs


def setup_inputs(seed=0):
    import zlib

    import numpy as np

    out = dict(_drawn_inputs(seed))
    spreads = {}
    factors = {'g_q': 6.446,
     'b_sb': 3.229,
     'b_router_group': 13.363,
     'b_router_expert': 4.141,
     'g_ple': 7.183}
    for name, (base, spread) in spreads.items():
        noise = np.random.default_rng([zlib.crc32(name.encode()), seed]).standard_normal(out[name].shape)
        drawn = base * np.exp(spread * noise) if base else spread * noise
        out[name] = __import__('jax').numpy.asarray(drawn.astype(out[name].dtype))
    for name, factor in factors.items():
        out[name] = (out[name] * factor).astype(out[name].dtype)
    return out
```

```python
import numpy as np
import concourse.bass as bass
from concourse import mybir
from contextlib import ExitStack

F32 = mybir.dt.float32
BF16 = mybir.dt.bfloat16
I32 = mybir.dt.int32
ALU = mybir.AluOpType
ACT = mybir.ActivationFunctionType
AX = mybir.AxisListType

P = 128
D = 1024
KD = D // P
SEQ, NS = 1024, 8
T_ALL = 1 + SEQ // P
ROWS = T_ALL * P
AW = 512
H, HD = 8, 64
NG, PW = 4, 128
WINDOWS = (2, 4, 8, 16)
STATE = 15
PAGES = 8
E_ALL, EG, EPG = 32, 4, 8
F = 512
KF = F // P
NR = EG + E_ALL
PLE = 256
EPS = 1e-6
SCALE = HD ** -0.5
N_OVER = (2 * (SEQ + NS) - 1) // P
N_BLK = E_ALL + N_OVER
CHUNK = 512
Q_RING = 4
NONE = 100000.0
V_PREV, V_FIRST, V_CUR, V_STATE, V_NEW = range(5)


class Chain:

    def __init__(self, eng, sem):
        self.eng, self.sem, self.base, self.n = eng, sem, 0, 0

    def __call__(self, ins):
        self.n += 1
        ins.then_inc(self.sem, 1)
        self.eng.wait_ge(self.sem, self.base + self.n)

    def loop(self, i, per_turn):
        self.start, self.per_turn = self.n, per_turn
        self.base = i * per_turn

    def end(self, turns):
        assert self.n == self.start + self.per_turn, (self.n - self.start, self.per_turn)
        self.base, self.n = 0, self.start + self.per_turn * turns


def tiles(eng, body, chain=None, per_turn=0):
    body(0, 0)
    if chain:
        n = chain.n
    with eng.Fori(0, 3) as i:
        if chain:
            chain.loop(i, per_turn)
        body(i * 2 + 1, 1, i)
        body(i * 2 + 2, 0, i)
    if chain:
        chain.end(3)
    body(7, 1)
    body(8, 0)


def build(nc, A, O):
    ctx = ExitStack()
    uniq = [0]

    def dram(name, shape, dt=F32):
        return nc.dram_tensor(name, shape, dt, kind="Internal").ap()

    def sb(stack, name, shape, dt=F32):
        return stack.enter_context(nc.sbuf_tensor(name, shape, dt))

    def pb(stack, name, cols=CHUNK):
        return stack.enter_context(nc.psum_tensor(name, [P, cols], F32))

    def sem(name):
        return ctx.enter_context(nc.semaphore(name))

    q_dram = dram("q_samples", [NS, AW])
    h_dram = dram("h_rows", [ROWS, D])
    m_dram = dram("m_rows", [ROWS, D])
    y_dram = dram("expert_rows", [2 * ROWS, D])

    with ctx:
        ident = sb(ctx, "ident", [P, P])
        w_rt = sb(ctx, "w_router_sb", [P, KD, NR])
        b_rt = sb(ctx, "b_router_sb", [P, NR])
        cols = sb(ctx, "per_partition", [P, 64])
        g_mix_c, g_ffn_c, g_ple_c = cols[:, 0:8], cols[:, 8:16], cols[:, 16:24]
        s_pool_c = cols[:, 24:28]
        nb_c, pb_c = cols[:, 28:36], cols[:, 36:44]
        nbs_c, pbs_c = cols[:, 44:45], cols[:, 45:46]
        logits = sb(ctx, "logits", [P, T_ALL, NR])
        gate_w = sb(ctx, "gate_weights", [P, 2, T_ALL])

        dve_chain, act_chain, pool_chain = sem("dve_chain"), sem("act_chain"), sem("pool_chain")
        chains = {}
        s_const = sem("const_loaded")
        s_out = sem("outputs_stored")
        n_out = [0]

        mid = ctx.enter_context(ExitStack())
        qT = sb(mid, "qT", [P, H // 2, SEQ])
        kT = sb(mid, "kT", [P, H // 2, SEQ])
        v_sb = sb(mid, "v_sb", [P, T_ALL, AW])
        mixp = sb(mid, "pool_mixed_T", [P, NG, ROWS])
        zd = sb(mid, "decode_scores", [P, PAGES, P])
        table = sb(mid, "page_table_sb", [1, NS * PAGES], I32)

        p1 = ExitStack()
        w_in = sb(p1, "w_in_sb", [P, KD, 4 * AW])
        band = sb(p1, "band", [P, NG, 3, P])
        w_pl = sb(p1, "w_pool_sb", [P, NG, PW])
        g_qk = sb(p1, "g_qk", [P, 2, HD])
        x_sb = [sb(p1, f"x{i}", [P, D]) for i in range(2)]
        xT = sb(p1, "xT", [P, KD, P])
        z_qk = sb(p1, "z_qk", [P, 2 * AW])
        sq = sb(p1, "squares", [P, 2 * AW])
        qk_n = [sb(p1, f"qk_norm{i}", [P, 2 * AW]) for i in range(2)]
        u_s = sb(p1, "u_samples", [P, AW])
        u_sb = [sb(p1, f"u{i}", [P, AW]) for i in range(2)]
        st_sb = sb(p1, "state_sb", [P, AW])
        pooledT = sb(p1, "pooledT", [P, NG, P])
        k_pg = [sb(p1, f"k_page{i}", [P, AW]) for i in range(Q_RING)]
        q_bc = [sb(p1, f"q_bc{i}", [P, AW]) for i in range(2)]
        band_state, band_new = (q[:].rearrange("p (g n) -> p g n", n=P) for q in q_bc)
        prod = [sb(p1, f"prod{i}", [P, AW]) for i in range(2)]
        sq_act = sb(p1, "squares_of_x", [P, D], BF16)
        st1 = sb(p1, "stats1", [P, 4])
        st16 = sb(p1, "stats16", [P, 3, 16])
        p_xt = pb(p1, "p_xt", 2 * CHUNK)
        p_z = [pb(p1, f"p_z{i}") for i in range(2)]
        p_qk = pb(p1, "p_qk", 2 * CHUNK)
        p_pool = pb(p1, "p_pool")
        p_py = pb(p1, "p_py")

        s_x = [sem("x_loaded0"), sem("x_loaded1")]
        xt_done = sem("x_transposed")
        xT_ready = sem("xT_copied")
        z_done = sem("z_chunks_done")
        ssx_ready, var_ready, std_ready, rx_ready = sem("x_squares"), sem("x_var"), sem("x_std"), sem("x_rstd")
        zqk_ready = sem("z_qk_copied")
        v_ready, u_ready = sem("v_copied"), sem("u_copied")
        var16, std16 = sem("qk_var"), sem("qk_std")
        qkn_ready = sem("qk_normalised")
        qkt_done, qT_ready, kT_ready = sem("qk_transposed"), sem("qT_copied"), sem("kT_copied")
        pool_done, pooledT_ready = sem("pooled_done"), sem("pooledT_copied")
        py_done, mixp_ready = sem("pool_map_done"), sem("pool_mixed_copied")
        s_k = sem("k_stored")
        s_q = sem("q_samples_stored")
        s_qb = [sem("q_bc_loaded0"), sem("q_bc_loaded1")]
        s_kp = [sem(f"k_page_loaded{i}") for i in range(Q_RING)]
        page_used = sem("k_page_used")
        prod_ready, prod_used = sem("prod_ready"), sem("prod_used")
        qbc_used = sem("q_bc_used")

        n_const = 0
        with nc.Block() as block:
            @block.sync
            def _(sp):
                def const(out, in_):
                    sp.dma_start(out, in_).then_inc(s_const, 16)

                sp.dma_start(x_sb[0][:], A["x_all"][0:P, :]).then_inc(s_x[0], 16)
                consts = [
                    (ident[:], A["c_ident"]), (cols[:], A["c_cols"]),
                    (w_in[:], A["w_in"].rearrange("(k p) n -> p k n", p=P)),
                    (g_qk[:], A["g_qk"]), (band[:], A["c_band"][:, :, 0:3, :]),
                    (band_state, A["c_band"][:, :, V_STATE, :]), (band_new, A["c_band"][:, :, V_NEW, :]),
                    (w_pl[:], A["w_pool"]), (st_sb[:], A["state_rows"]),
                    (table[:], A["page_table"]),
                    (w_rt[:], A["w_router"]), (b_rt[:], A["b_router"]),
                ]
                for out, in_ in consts:
                    const(out, in_)
                sp.dma_start(x_sb[1][:], A["x_all"][P:2 * P, :]).then_inc(s_x[1], 16)
                sp.dma_start(O["pool_sample"][:, 0:STATE - 1, :], A["state_pool"][:, 1:STATE, :]).then_inc(s_out, 16)
                n_out[0] += 1
                sp.wait_ge(s_const, 16 * len(consts))

                def tile(T, par, i=None):
                    last = isinstance(T, int) and T >= 7
                    if not last:
                        sp.wait_ge(ssx_ready, T + 1)
                        sp.wait_ge(xt_done, T + 1)
                        sp.dma_start(x_sb[par][:], A["x_all"][bass.ts(T + 2, P), :]).then_inc(s_x[par], 16)
                    first = isinstance(T, int) and T == 0
                    if not first:
                        b = T - 1
                        sp.wait_ge(qbc_used, T)
                        sp.wait_ge(pool_done, T)
                        sp.dma_start(q_bc[1 - par][:], q_dram[bass.ds(b, 1), :].to_broadcast([P, AW])).then_inc(s_qb[1 - par], 16)
                        for j in range(PAGES):
                            n = b * PAGES + j
                            page = sp.value_load(table[0:1, bass.ds(n, 1)], min_val=0, max_val=A["cache_k"].shape[0] - 1)
                            sp.wait_ge(page_used, n + 1)
                            sp.dma_start(k_pg[j % Q_RING][:], A["cache_k"][bass.ds(page, 1), :, :].rearrange("a p n -> (a p) n")).then_inc(s_kp[j % Q_RING], 16)
                    sp.wait_ge(v_ready, T + 1)
                    sp.dma_start(O["v_all"][bass.ts(T, P), :], v_sb[:, bass.ds(T, 1), :].rearrange("p a n -> p (a n)")).then_inc(s_out, 16)
                    sp.wait_ge(qkn_ready, T + 1)
                    sp.dma_start(O["k_all"][bass.ts(T, P), :], qk_n[0 if first else 1][:, AW:2 * AW]).then_inc(s_k, 16)
                    if first:
                        sp.dma_start(q_dram, qk_n[0][0:NS, 0:AW]).then_inc(s_q, 16)
                        sp.wait_ge(u_ready, 1)
                        sp.dma_start(O["pool_sample"][:, STATE - 1, :], u_s[0:NS, :]).then_inc(s_out, 16)
                        sp.wait_ge(s_q, 16)

                tiles(sp, tile)
                n_out[0] += T_ALL + 1
                sp.wait_ge(u_ready, T_ALL)
                sp.dma_start(O["pool_prompt"], u_sb[1][P - STATE:P, :]).then_inc(s_out, 16)
                n_out[0] += 1
                sp.wait_ge(s_k, 16 * T_ALL)
                sp.wait_ge(s_out, 16 * n_out[0])

            @block.tensor
            def _(pe):
                pe.wait_ge(s_const, 16 * 12)

                def transpose_x(T, par, count):
                    pe.wait_ge(s_x[par], count)
                    for k in range(KD):
                        ins = pe.transpose(p_xt[:, k * P:(k + 1) * P], x_sb[par][:, k * P:(k + 1) * P], ident[:])
                    ins.then_inc(xt_done, 1)

                transpose_x(0, 0, 16)

                def tile(T, par, i=None):
                    first = isinstance(T, int) and T == 0
                    last = isinstance(T, int) and T == T_ALL - 1
                    pe.wait_ge(xT_ready, T + 1)
                    for n in range(4):
                        if n >= 2:
                            pe.wait_ge(zqk_ready, T * 2 + n - 1)
                        elif not first:
                            pe.wait_ge([v_ready, u_ready][n], T)
                        for k in range(KD):
                            ins = pe.matmul(p_z[n % 2][:], xT[:, k, :], w_in[:, k, n * AW:(n + 1) * AW],
                                            start=(k == 0), stop=(k == KD - 1))
                        ins.then_inc(z_done, 1)
                    if not last:
                        nth = (T + 1) // 2 + 1 if isinstance(T, int) else (i + 2 if par else i + 2)
                        transpose_x(T + 1, 1 - par, nth * 16)
                    pe.wait_ge(u_ready, T + 1)
                    for g in range(NG):
                        cs = slice(g * PW, (g + 1) * PW)
                        if first:
                            lhs = [(st_sb, band_state[:, g, :]), (u_s, band_new[:, g, :])]
                        else:
                            if isinstance(T, int) or par == 0:
                                cur = band[:, g, V_CUR, :]
                            else:
                                cur = band[:, g, bass.ds(V_FIRST + (i > 0), 1), :].rearrange("p a n -> p (a n)")
                            lhs = [(u_sb[par], band[:, g, V_PREV, :]), (u_sb[1 - par], cur)]
                        for s, (left, mat) in enumerate(lhs):
                            ins = pe.matmul(p_pool[:, cs], left[:, cs], mat, start=(s == 0), stop=(s == 1))
                    ins.then_inc(pool_done, 1)
                    pe.wait_ge(qkn_ready, T + 1)
                    if not first:
                        pe.wait_ge(qT_ready, T)
                        pe.wait_ge(kT_ready, T)
                        for c in range(2 * AW // P):
                            ins = pe.transpose(p_qk[:, c * P:(c + 1) * P], qk_n[1][:, c * P:(c + 1) * P], ident[:])
                    else:
                        ins = pe.transpose(p_qk[:, 0:P], qk_n[0][:, 0:P], ident[:])
                    ins.then_inc(qkt_done, 1)
                    pe.wait_ge(pooledT_ready, T + 1)
                    if not first:
                        pe.wait_ge(mixp_ready, T)
                    for g in range(NG):
                        ins = pe.matmul(p_py[:, g * P:(g + 1) * P], w_pl[:, g, :], pooledT[:, g, :], start=True, stop=True)
                    ins.then_inc(py_done, 1)

                tiles(pe, tile)

            @block.scalar
            def _(act):
                act.wait_ge(s_const, 16 * 12)
                chain = chains["act"] = Chain(act, act_chain)

                def tile(T, par, i=None):
                    first = isinstance(T, int) and T == 0
                    nth = T // 2 + 1 if isinstance(T, int) else (i + 1 if par else i + 2)
                    act.wait_ge(s_x[par], nth * 16)
                    if not first:
                        act.wait_ge(ssx_ready, T)
                        act.wait_ge(var_ready, T)
                    act.activation(sq_act[:], x_sb[par][:], ACT.Square, accum_out=st1[:, 0:1]).then_inc(ssx_ready, 1)
                    act.wait_ge(var_ready, T + 1)
                    if not first:
                        act.wait_ge(rx_ready, T)
                    act.activation(st1[:, 2:3], st1[:, 1:2], ACT.Sqrt).then_inc(std_ready, 1)
                    act.wait_ge(rx_ready, T + 1)
                    if not first:
                        act.wait_ge(qkn_ready, T)
                    for n in range(2):
                        act.wait_ge(z_done, T * 4 + n + 1)
                        act.activation(z_qk[:, n * AW:(n + 1) * AW], p_z[n][:], ACT.Copy, scale=st1[:, 3:4]).then_inc(zqk_ready, 1)
                    act.wait_ge(var16, T + 1)
                    act.activation(st16[:, 1, :], st16[:, 0, :], ACT.Sqrt).then_inc(std16, 1)
                    act.wait_ge(pool_done, T + 1)
                    if not first:
                        act.wait_ge(py_done, T)
                    act.activation(pooledT[:].rearrange("p g n -> p (g n)"), p_pool[:], ACT.Copy).then_inc(pooledT_ready, 1)
                    act.wait_ge(qkt_done, T + 1)
                    if first:
                        act.sem_inc(qT_ready, 1)
                    else:
                        act.activation(qT[:, :, bass.ts(T - 1, P)], p_qk[:, 0:AW].rearrange("p (c n) -> p c n", n=P),
                                       ACT.Copy).then_inc(qT_ready, 1)
                    act.wait_ge(py_done, T + 1)
                    for g in range(NG):
                        ins = act.activation(mixp[:, g, bass.ts(T, P)], p_py[:, g * P:(g + 1) * P], ACT.Copy, scale=s_pool_c[:, g:g + 1])
                    ins.then_inc(mixp_ready, 1)

                tiles(act, tile)

            @block.vector
            def _(dve):
                chain = chains["dve"] = Chain(dve, dve_chain)
                dve.sem_inc(prod_used, 2)
                chain(dve.memset(u_sb[1][:], 0.0))
                chain(dve.memset(zd[:], 0.0))
                dve.wait_ge(s_const, 16 * 12)
                chain(dve.tensor_scalar(nb_c, pb_c, -1.0, None, ALU.mult))
                chain(dve.tensor_scalar(nbs_c, pbs_c, -1.0, None, ALU.mult))

                def copy_xT(T):
                    dve.wait_ge(xt_done, T + 1)
                    dve.tensor_tensor(out=xT[:], in0=p_xt[:].rearrange("p (k n) -> p k n", n=P),
                                      in1=g_mix_c.unsqueeze(2).to_broadcast([P, KD, P]), op=ALU.mult).then_inc(xT_ready, 1)

                copy_xT(0)

                def tile(T, par, i=None):
                    first = isinstance(T, int) and T == 0
                    last = isinstance(T, int) and T == T_ALL - 1
                    dve.wait_ge(ssx_ready, T + 1)
                    if not first:
                        dve.wait_ge(std_ready, T)
                    dve.tensor_scalar(st1[:, 1:2], st1[:, 0:1], 1.0 / D, EPS, ALU.mult, ALU.add).then_inc(var_ready, 1)
                    dve.wait_ge(std_ready, T + 1)
                    dve.wait_ge(v_ready, T) if not first else None
                    dve.reciprocal(st1[:, 3:4], st1[:, 2:3]).then_inc(rx_ready, 1)
                    dve.wait_ge(zqk_ready, T * 2 + 2)
                    chain(dve.tensor_tensor(out=sq[:], in0=z_qk[:], in1=z_qk[:], op=ALU.mult))
                    chain(dve.tensor_reduce(out=st16[:, 2, :], in_=sq[:].rearrange("p (h d) -> p h d", d=HD), axis=AX.X, op=ALU.add))
                    dve.tensor_scalar(st16[:, 0, :], st16[:, 2, :], 1.0 / HD, EPS, ALU.mult, ALU.add).then_inc(var16, 1)
                    dve.wait_ge(z_done, T * 4 + 3)
                    dve.wait_ge(rx_ready, T + 1)
                    dve.tensor_scalar(v_sb[:, bass.ds(T, 1), :].rearrange("p a n -> p (a n)"), p_z[0][:], st1[:, 3:4], None,
                                      ALU.mult).then_inc(v_ready, 1)
                    dve.wait_ge(std16, T + 1)
                    chain(dve.reciprocal(st16[:, 2, :], st16[:, 1, :]))
                    heads = lambda t: t[:].rearrange("p (h d) -> p h d", d=HD)
                    chain(dve.tensor_tensor(out=heads(sq), in0=heads(z_qk),
                                            in1=st16[:, 2, :].unsqueeze(2).to_broadcast([P, 16, HD]), op=ALU.mult))
                    out = qk_n[0 if first else 1]
                    if not first:
                        dve.wait_ge(s_k, T * 16)
                        dve.wait_ge(qkt_done, T)
                    for s in range(2):
                        ins = dve.tensor_tensor(out=out[:, s * AW:(s + 1) * AW].rearrange("p (h d) -> p h d", d=HD),
                                                in0=sq[:, s * AW:(s + 1) * AW].rearrange("p (h d) -> p h d", d=HD),
                                                in1=g_qk[:, s, :].unsqueeze(1).to_broadcast([P, H, HD]), op=ALU.mult)
                    ins.then_inc(qkn_ready, 1)
                    dve.wait_ge(z_done, T * 4 + 4)
                    if not first:
                        dve.wait_ge(pool_done, T)
                    dve.tensor_scalar((u_s if first else u_sb[1 - par])[:], p_z[1][:], st1[:, 3:4], None,
                                      ALU.mult).then_inc(u_ready, 1)
                    if not last:
                        copy_xT(T + 1)
                    dve.wait_ge(qkt_done, T + 1)
                    if first:
                        dve.sem_inc(kT_ready, 1)
                    else:
                        dve.tensor_copy(kT[:, :, bass.ts(T - 1, P)], p_qk[:, AW:2 * AW].rearrange("p (c n) -> p c n", n=P)).then_inc(kT_ready, 1)
                        for j in range(PAGES):
                            n = (T - 1) * PAGES + j
                            dve.wait_ge(prod_ready, n + 1)
                            dve.tensor_reduce(out=zd[:, j, bass.ds((T - 1) * H, H)],
                                              in_=prod[j % 2][:].rearrange("p (h d) -> p h d", d=HD),
                                              axis=AX.X, op=ALU.add).then_inc(prod_used, 1)

                tiles(dve, tile, chain, 2 * 4)

            @block.gpsimd
            def _(pool):
                pool.sem_inc(page_used, Q_RING)
                pool.sem_inc(qbc_used, 2)

                def sample(b, par, nth):
                    pool.wait_ge(s_qb[par], nth * 16)
                    for j in range(PAGES):
                        n = b * PAGES + j
                        pool.wait_ge(s_kp[j % Q_RING], (b * 2 + j // Q_RING + 1) * 16)
                        pool.wait_ge(prod_used, n + 1)
                        ins = pool.tensor_tensor(out=prod[j % 2][:], in0=k_pg[j % Q_RING][:], in1=q_bc[par][:], op=ALU.mult)
                        ins.then_inc(prod_ready, 1)
                        pool.wait_ge(prod_ready, n + 1)
                        pool.sem_inc(page_used, 1)
                    pool.sem_inc(qbc_used, 1)

                with pool.Fori(0, NS // 2) as i:
                    sample(i * 2, 0, i + 1)
                    sample(i * 2 + 1, 1, i + 1)
        p1.close()

        w_keys = sb(mid, "decode_weights_T", [P, PAGES, P])
        p2 = ExitStack()
        keep = [sb(p2, f"keep{i}", [P, SEQ]) for i in range(2)]
        beta = [sb(p2, f"beta{i}", [P, SEQ]) for i in range(2)]
        left = [sb(p2, f"left{i}", [P, SEQ + 1]) for i in range(2)]
        w_out = sb(p2, "w_out_sb", [P, KD, D])
        p_sc = [pb(p2, f"p_sc{i}", 2 * CHUNK) for i in range(2)]
        p_at = [pb(p2, f"p_at{i}") for i in range(2)]
        p_o = pb(p2, "p_o")
        p_w = pb(p2, "p_w")
        s_wout = sem("w_out_loaded")
        d_t, d_sig, d_a, d_b, d_c = sem("decode_z_T"), sem("decode_sigmoids"), sem("decode_a"), sem("decode_a_T"), sem("decode_copied")
        ones_ready = sem("left_ones")
        with nc.Block() as block:
            @block.sync
            def _(sp):
                sp.dma_start(w_out[:], A["w_out"].rearrange("(k p) n -> p k n", p=P)).then_inc(s_wout, 16)

            @block.tensor
            def _(pe):
                for j in range(PAGES):
                    ins = pe.transpose(p_sc[0][:, j * P:(j + 1) * P], zd[:, j, :], ident[:])
                ins.then_inc(d_t, 1)
                pe.wait_ge(d_a, 1)
                for j in range(PAGES):
                    ins = pe.transpose(p_sc[1][:, j * P:(j + 1) * P], beta[0][:, j * P:(j + 1) * P], ident[:])
                ins.then_inc(d_b, 1)

            @block.scalar
            def _(act):
                act.wait_ge(d_t, 1)
                act.activation(keep[0][:], p_sc[0][:], ACT.Sigmoid, bias=nbs_c, scale=-SCALE).then_inc(d_sig, 1)
                act.activation(beta[0][:], p_sc[0][:], ACT.Sigmoid, bias=pbs_c, scale=SCALE).then_inc(d_sig, 1)

            @block.vector
            def _(dve):
                chain = chains["dve"]
                chain.eng = dve
                for i in range(2):
                    chain(dve.memset(left[i][:, SEQ:SEQ + 1], 1.0))
                dve.wait_ge(d_sig, 2)
                chain(dve.tensor_tensor_scan(out=left[0][:, 0:SEQ][:, ::-1], data0=keep[0][:, ::-1], data1=keep[0][:, ::-1],
                                             initial=1.0, op0=ALU.mult, op1=ALU.bypass))
                dve.tensor_tensor(out=beta[0][:], in0=beta[0][:], in1=left[0][:, 1:SEQ + 1], op=ALU.mult).then_inc(d_a, 1)
                dve.wait_ge(d_b, 1)
                dve.tensor_copy(w_keys[:].rearrange("p j n -> p (j n)"), p_sc[1][:]).then_inc(d_c, 1)

        GRP = 4
        ident_b = sb(p2, "ident_bf16", [P, P], BF16)
        mask_b = sb(p2, "causal_mask", [P, P], BF16)
        mask_f = sb(p2, "causal_mask_f32", [P, P])
        bf16_ready = sem("bf16_constants")
        aT = [sb(p2, f"aT{i}", [P, GRP, P]) for i in range(4)]
        attn = [sb(p2, f"attn{i}", [P, AW]) for i in range(2)]
        mixT = sb(p2, "attn_mixed_T", [P, AW // P, P])
        mixT_s = sb(p2, "attn_mixed_T_samples", [P, AW // P, P])
        v_pg = [sb(p2, f"v_page{i}", [P, AW]) for i in range(Q_RING)]
        x_r = [sb(p2, f"x_res{i}", [P, D]) for i in range(2)]
        h_sb = [sb(p2, f"h{i}", [P, D]) for i in range(2)]
        m_sb = [sb(p2, f"m{i}", [P, D]) for i in range(2)]
        hT = sb(p2, "hT", [P, KD, P])
        w_rg = sb(p2, "w_router_times_g", [P, KD, NR])
        g_ffn = sb(p2, "g_ffn_sb", [P, D])
        junk = sb(p2, "squares_of_h", [P, D], BF16)
        st2 = [sb(p2, f"stats2_{i}", [P, 4]) for i in range(2)]

        sc_done, sig_done, a_done = sem("scores_done"), sem("sigmoids_done"), sem("weights_done")
        at_done, at_copied, o_done, attn_copied = sem("aT_done"), sem("aT_copied"), sem("heads_done"), sem("attn_copied")
        w_done, w_copied = sem("p_w_filled"), sem("p_w_copied")
        s_vp = [sem(f"v_page_loaded{i}") for i in range(Q_RING)]
        vpage_used = sem("v_page_used")
        s_xr = [sem("x_res_loaded0"), sem("x_res_loaded1")]
        h_ss, h_var, h_std, h_rs, m_ready, mixs_zero = (sem("h_squares"), sem("h_var"), sem("h_std"), sem("h_rstd"),
                                                        sem("m_ready"), sem("mixed_zeroed"))
        s_hm = [sem("h_m_stored0"), sem("h_m_stored1")]
        s_c2 = sem("const2_loaded")

        jobs = list(range(1, T_ALL - 1)) + [0, T_ALL - 1]
        plan = [("scores", 0), ("scores", 1)]
        pieces = []
        for t in range(1, T_ALL):
            per_head = 2 if t == T_ALL - 1 else 1
            if t >= 2:
                pieces += [(jobs.index(t - 1), k) for k in range(8)]
            if t == T_ALL - 1:
                pieces += [(jobs.index(0), k) for k in range(8)]
            for h in range(H):
                n = (t - 1) * H + h
                plan.append(("apply", n))
                if n + 2 < (T_ALL - 1) * H:
                    plan.append(("scores", n + 2))
                for _ in range(min(per_head, len(pieces))):
                    plan.append(("piece", pieces.pop(0)))
                if t <= 4 and h % 4 == 3:
                    plan.append(("decode", (t - 1) * 2 + h // 4))
            plan.append(("attn", t))
        plan += [("piece", (jobs.index(T_ALL - 1), k)) for k in range(8)]
        group_of, n_groups = {}, 0
        for what, arg in plan:
            if what == "apply":
                group_of[arg] = n_groups
                n_groups += (arg // H + 1 + GRP - 1) // GRP
            elif what == "decode":
                group_of["d", arg] = n_groups
                n_groups += 1
        fills = {}
        for what, arg in plan:
            if what == "piece":
                j, k = arg
                name = {0: "mix", 2: "h0", 4: "h1", 5: "t0", 6: "t1", 7: "logits"}.get(k)
                if name and not (name == "mix" and jobs[j] == 0):
                    fills[j, name] = len(fills)

        with nc.Block() as block:
            @block.sync
            def _(sp):
                sp.dma_start(mask_f[:], A["c_mask"]).then_inc(s_c2, 16)
                sp.dma_start(g_ffn[:], A["g_ffn_bc"]).then_inc(s_c2, 16)
                for j in range(2):
                    sp.dma_start(x_r[j][:], A["x_all"][bass.ts(jobs[j], P), :]).then_inc(s_xr[j], 16)
                for j, T in enumerate(jobs):
                    sp.wait_ge(m_ready, j + 1)
                    sp.dma_start(h_dram[T * P:(T + 1) * P, :], h_sb[j % 2][:]).then_inc(s_hm[j % 2], 16)
                    sp.dma_start(m_dram[T * P:(T + 1) * P, :], m_sb[j % 2][:]).then_inc(s_hm[j % 2], 16)
                    if j + 2 < len(jobs):
                        sp.dma_start(x_r[j % 2][:], A["x_all"][bass.ts(jobs[j + 2], P), :]).then_inc(s_xr[j % 2], 16)
                sp.wait_ge(s_hm[0], 32 * 5)
                sp.wait_ge(s_hm[1], 32 * 4)

            @block.gpsimd
            def _(pool):
                pool.memset(mixT_s[:], 0.0).then_inc(mixs_zero, 1)
                with pool.Fori(0, NS * PAGES // Q_RING) as i:
                    for r in range(Q_RING):
                        n = i * Q_RING + r
                        page = pool.value_load(table[0:1, bass.ds(n, 1)], min_val=0, max_val=A["cache_v"].shape[0] - 1)
                        pool.wait_ge(vpage_used, n + 1)
                        pool.dma_start(v_pg[r][:], A["cache_v"][bass.ds(page, 1), :, :].rearrange("a p n -> (a p) n")).then_inc(s_vp[r], 16)

            @block.tensor
            def _(pe):
                pe.sem_inc(vpage_used, Q_RING)
                pe.wait_ge(bf16_ready, 2)
                pe.wait_ge(s_wout, 16)
                for what, arg in plan:
                    if what == "scores":
                        t, h = arg // H + 1, arg % H
                        rows = slice(HD * (h % 2), HD * (h % 2) + HD)
                        if arg >= 2:
                            pe.wait_ge(sig_done, arg - 1)
                        N = t * P
                        for c in range(0, N, CHUNK):
                            w = min(CHUNK, N - c)
                            has_mask = c + w == N
                            ins = pe.matmul(p_sc[arg % 2][:, c:c + w], qT[rows, h // 2, (t - 1) * P:t * P],
                                            kT[rows, h // 2, c:c + w], start=True, stop=not has_mask)
                            if has_mask:
                                ins = pe.matmul(p_sc[arg % 2][:, N - P:N], ident_b[:], mask_b[:], start=False, stop=True)
                        ins.then_inc(sc_done, 1)
                    elif what == "apply":
                        t, h = arg // H + 1, arg % H
                        pe.wait_ge(a_done, arg + 1)
                        g0, ng = group_of[arg], (t + GRP - 1) // GRP
                        for g in range(ng):
                            if g0 + g >= 2:
                                pe.wait_ge(at_copied, g0 + g - 1)
                            for b in range(g * GRP, min(t, (g + 1) * GRP)):
                                ins = pe.transpose(p_at[(g0 + g) % 2][:, (b % GRP) * P:(b % GRP + 1) * P],
                                                   beta[arg % 2][:, SEQ - t * P + b * P:SEQ - t * P + (b + 1) * P], ident[:])
                            ins.then_inc(at_done, 1)
                        if h == 0 and t >= 2:
                            pe.wait_ge(attn_copied, t - 1)
                        for g in range(ng):
                            pe.wait_ge(at_copied, g0 + g + 1)
                            for b in range(g * GRP, min(t, (g + 1) * GRP)):
                                ins = pe.matmul(p_o[:, h * HD:(h + 1) * HD], aT[(g0 + g) % 4][:, b % GRP, :],
                                                v_sb[:, b + 1, h * HD:(h + 1) * HD], start=(b == 0), stop=(b == t - 1))
                        ins.then_inc(o_done, 1)
                    elif what == "decode":
                        g = group_of["d", arg]
                        pe.wait_ge(at_copied, g - 1)
                        for j in range(PAGES):
                            pe.wait_ge(s_vp[j % Q_RING], (arg * 2 + j // Q_RING + 1) * 16)
                            for c in range(AW // P):
                                ins = pe.matmul(p_at[g % 2][:, 2 * c:2 * c + 2], v_pg[j % Q_RING][:, c * P:(c + 1) * P],
                                                w_keys[:, j, arg * H + 2 * c:arg * H + 2 * c + 2],
                                                start=(j == 0 and c == 0), stop=(j == PAGES - 1 and c == AW // P - 1),
                                                skip_group_check=True)
                            ins.then_inc(vpage_used, 1)
                            if j == PAGES - 1:
                                pe.wait_ge(vpage_used, Q_RING + arg * PAGES + PAGES)
                                pe.sem_inc(at_done, 1)
                    elif what == "piece":
                        j, k = arg
                        T = jobs[j]

                        def begin(name):
                            if fills[j, name] > 0:
                                pe.wait_ge(w_copied, fills[j, name])

                        if k == 0 and T > 0:
                            begin("mix")
                            pe.wait_ge(attn_copied, T)
                            for c in range(AW // P):
                                ins = pe.transpose(p_w[:, c * P:(c + 1) * P], attn[T % 2][:, c * P:(c + 1) * P], ident[:])
                            ins.then_inc(w_done, 1)
                        if k in (1, 2, 3, 4):
                            n = (k - 1) // 2
                            if k == 1:
                                begin("h0")
                                if T == 0:
                                    pe.wait_ge(at_copied, group_of["d", NS - 1] + 1)
                            if k == 3:
                                begin("h1")
                            for kk in range(4 * ((k - 1) % 2), 4 * ((k - 1) % 2) + 4):
                                if kk < 4:
                                    lhs = (mixT if T > 0 else mixT_s)[:, kk, :]
                                else:
                                    lhs = mixp[:, kk - 4, T * P:(T + 1) * P]
                                ins = pe.matmul(p_w[:], lhs, w_out[:, kk, n * CHUNK:(n + 1) * CHUNK], start=(kk == 0), stop=(kk == 7))
                            if k in (2, 4):
                                ins.then_inc(w_done, 1)
                        if k in (5, 6):
                            begin(f"t{k - 5}")
                            for c in range(4):
                                kk = 4 * (k - 5) + c
                                ins = pe.transpose(p_w[:, c * P:(c + 1) * P], h_sb[j % 2][:, kk * P:(kk + 1) * P], ident[:])
                            ins.then_inc(w_done, 1)
                        if k == 7:
                            begin("logits")
                            for kk in range(KD):
                                ins = pe.matmul(p_w[:, 0:NR], hT[:, kk, :], w_rg[:, kk, :], start=(kk == 0), stop=(kk == KD - 1))
                            ins.then_inc(w_done, 1)

            @block.scalar
            def _(act):
                act.wait_ge(mixs_zero, 1)
                for what, arg in plan:
                    if what == "scores":
                        t, h = arg // H + 1, arg % H
                        N = t * P
                        act.wait_ge(sc_done, arg + 1)
                        if arg >= 2:
                            act.wait_ge(a_done, arg - 1)
                            act.wait_ge(o_done, arg - 1)
                        act.activation(keep[arg % 2][:, SEQ - N:SEQ], p_sc[arg % 2][:, 0:N], ACT.Sigmoid, bias=nb_c[:, h:h + 1], scale=-SCALE)
                        act.activation(beta[arg % 2][:, SEQ - N:SEQ], p_sc[arg % 2][:, 0:N], ACT.Sigmoid, bias=pb_c[:, h:h + 1],
                                       scale=SCALE).then_inc(sig_done, 1)
                    elif what == "apply":
                        t = arg // H + 1
                        g0 = group_of[arg]
                        for g in range((t + GRP - 1) // GRP):
                            w = min(GRP, t - g * GRP)
                            act.wait_ge(at_done, g0 + g + 1)
                            if arg >= 1:
                                act.wait_ge(o_done, arg - 1) if arg >= 2 else None
                            act.activation(aT[(g0 + g) % 4][:, 0:w, :], p_at[(g0 + g) % 2][:, 0:w * P].rearrange("p (b n) -> p b n", n=P),
                                           ACT.Copy).then_inc(at_copied, 1)
                    elif what == "decode":
                        g = group_of["d", arg]
                        act.wait_ge(at_done, g + 1)
                        cols_of = p_at[g % 2][:, 0:8].rearrange("p (c r) -> p c r", r=2)
                        act.activation(mixT_s[0:HD, :, arg], cols_of[0:HD, :, 0], ACT.Copy)
                        act.activation(mixT_s[HD:P, :, arg], cols_of[HD:P, :, 1], ACT.Copy).then_inc(at_copied, 1)
                    elif what == "attn":
                        act.wait_ge(o_done, arg * H)
                        if arg >= 3:
                            act.wait_ge(w_done, fills[jobs.index(arg - 2), "mix"] + 1)
                        act.activation(attn[arg % 2][:], p_o[:], ACT.Copy).then_inc(attn_copied, 1)
                    elif what == "piece":
                        j, k = arg
                        T = jobs[j]
                        if k == 0 and T > 0:
                            act.wait_ge(w_done, fills[j, "mix"] + 1)
                            act.activation(mixT[:].rearrange("p c n -> p (c n)"), p_w[:], ACT.Copy).then_inc(w_copied, 1)
                        if k == 4:
                            act.wait_ge(w_copied, fills[j, "h1"] + 1)
                            if j >= 1:
                                act.wait_ge(h_ss, j)
                            act.activation(junk[:], h_sb[j % 2][:], ACT.Square, accum_out=st2[j % 2][:, 0:1]).then_inc(h_ss, 1)
                        if k == 5:
                            act.wait_ge(h_var, j + 1)
                            act.activation(st2[j % 2][:, 2:3], st2[j % 2][:, 1:2], ACT.Sqrt).then_inc(h_std, 1)

            @block.vector
            def _(dve):
                chain = chains["dve"]
                chain.eng = dve
                dve.wait_ge(s_c2, 32)
                dve.tensor_copy(ident_b[:], ident[:]).then_inc(bf16_ready, 1)
                dve.tensor_copy(mask_b[:], mask_f[:]).then_inc(bf16_ready, 1)
                chain(dve.tensor_tensor(out=w_rg[:], in0=w_rt[:], in1=g_ffn_c.unsqueeze(2).to_broadcast([P, KD, NR]), op=ALU.mult))
                for what, arg in plan:
                    if what == "scores":
                        t = arg // H + 1
                        N = t * P
                        b = arg % 2
                        dve.wait_ge(sig_done, arg + 1)
                        chain(dve.tensor_tensor_scan(out=left[b][:, SEQ - N:SEQ][:, ::-1], data0=keep[b][:, SEQ - N:SEQ][:, ::-1],
                                                     data1=keep[b][:, SEQ - N:SEQ][:, ::-1], initial=1.0, op0=ALU.mult, op1=ALU.bypass))
                        dve.tensor_tensor(out=beta[b][:, SEQ - N:SEQ], in0=beta[b][:, SEQ - N:SEQ], in1=left[b][:, SEQ - N + 1:SEQ + 1],
                                          op=ALU.mult).then_inc(a_done, 1)
                    elif what == "piece":
                        j, k = arg
                        T = jobs[j]
                        if k in (2, 4):
                            n = (k - 2) // 2
                            cs = slice(n * CHUNK, (n + 1) * CHUNK)
                            dve.wait_ge(w_done, fills[j, f"h{n}"] + 1)
                            if n == 0:
                                dve.wait_ge(s_xr[j % 2], 16 * (j // 2 + 1))
                                if j >= 2:
                                    dve.wait_ge(s_hm[j % 2], 32 * (j // 2))
                            dve.tensor_tensor(out=h_sb[j % 2][:, cs], in0=p_w[:], in1=x_r[j % 2][:, cs], op=ALU.add).then_inc(w_copied, 1)
                        if k in (5, 6):
                            dve.wait_ge(w_done, fills[j, f"t{k - 5}"] + 1)
                            dve.tensor_copy(hT[:, 4 * (k - 5):4 * (k - 4), :].rearrange("p c n -> p (c n)"), p_w[:]).then_inc(w_copied, 1)
                        if k == 4:
                            dve.wait_ge(h_ss, j + 1)
                            dve.tensor_scalar(st2[j % 2][:, 1:2], st2[j % 2][:, 0:1], 1.0 / D, EPS, ALU.mult, ALU.add).then_inc(h_var, 1)
                        if k == 6:
                            dve.wait_ge(h_std, j + 1)
                            chain(dve.reciprocal(st2[j % 2][:, 3:4], st2[j % 2][:, 2:3]))
                            dve.scalar_tensor_tensor(out=m_sb[j % 2][:], in0=h_sb[j % 2][:], scalar=st2[j % 2][:, 3:4], in1=g_ffn[:],
                                                     op0=ALU.mult, op1=ALU.mult).then_inc(m_ready, 1)
                        if k == 7:
                            dve.wait_ge(w_done, fills[j, "logits"] + 1)
                            dve.scalar_tensor_tensor(out=logits[:, T, :], in0=p_w[:, 0:NR], scalar=st2[j % 2][:, 3:4], in1=b_rt[:],
                                                     op0=ALU.mult, op1=ALU.add).then_inc(w_copied, 1)
                dve.wait_ge(w_copied, len(fills))
        p2.close()
        mid.close()

        late = ctx.enter_context(ExitStack())
        m_idx = sb(late, "m_row_of_slot", [P, N_BLK], I32)
        y_idx = sb(late, "y_row_of_slot", [P, N_BLK], I32)
        over = sb(late, "overflow_blocks", [P, 1 + N_OVER], I32)
        w_g = [sb(late, f"w_gate{i}", [P, KD, F]) for i in range(2)]
        w_u = [sb(late, f"w_up{i}", [P, KD, F]) for i in range(2)]
        w_d = [sb(late, f"w_down{i}", [P, KF, D]) for i in range(2)]
        x_g = [sb(late, f"x_gathered{i}", [P, D]) for i in range(2)]
        s_wg = [sem("w_gate_loaded0"), sem("w_gate_loaded1")]
        s_wu = [sem("w_up_loaded0"), sem("w_up_loaded1")]
        s_wd = [sem("w_down_loaded0"), sem("w_down_loaded1")]
        xg_zero = sem("x_gathered_zeroed")

        def gate_rows(e):
            return A["w_gate"][e, :, :].rearrange("a (k p) n -> p (a k) n", p=P)

        def up_rows(e):
            return A["w_up"][e, :, :].rearrange("a (k p) n -> p (a k) n", p=P)

        def down_rows(e):
            return A["w_down"][e, :, :].rearrange("a (k p) n -> p (a k) n", p=P)

        p3 = ExitStack()
        T9 = T_ALL
        c3 = sb(p3, "routing_constants", [P, A["c_route"].shape[1]])
        iota128, iota_e, iota_b = c3[:, 0:128], c3[:, 128:160], c3[:, 160:160 + N_BLK]
        mult8 = c3[:, 208:216]
        valid = c3[:, 216:225]
        y_val, m_val = c3[:, 225:243].rearrange("p (a b) -> p a b", a=2), c3[:, 243:252]
        iota_o = c3[:, 252:252 + N_OVER]
        iota_b9 = c3[:, 0:EPG]
        tri_f = sb(p3, "tri_f32", [P, P])
        tri = sb(p3, "tri", [P, P], BF16)
        ones_b = sb(p3, "ones_bf16", [P, P], BF16)
        a_b = sb(p3, "assigned_bf16", [P, T9, E_ALL], BF16)
        r4 = [sb(p3, f"r4_{i}", [P, T9, EG]) for i in range(4)]
        r8 = [sb(p3, f"r8_{i}", [P, T9, EPG]) for i in range(4)]
        r32 = [sb(p3, f"r32_{i}", [P, T9, E_ALL]) for i in range(3)]
        oh = [sb(p3, f"onehot_e{i}", [P, T9, E_ALL]) for i in range(2)]
        s9 = sb(p3, "scalars9", [P, 24, T9])
        pre = sb(p3, "rank_before", [P, T9, E_ALL])
        tot = sb(p3, "totals", [P, 6, E_ALL])
        cmp8 = sb(p3, "compares8", [P, E_ALL, 8])
        cmp9 = sb(p3, "compares9", [P, T9, 8])
        cmp_o = sb(p3, "compares_o", [P, N_OVER, E_ALL])
        over_f = sb(p3, "overflow_f", [P, 1 + N_OVER])
        R = [sb(p3, f"row_onehot{i}", [P, P]) for i in range(4)]
        B = [sb(p3, f"block_onehot{i}", [P, 2, N_BLK]) for i in range(4)]
        tab = sb(p3, "slot_tables", [P, 2, 2, N_BLK])
        p_rank, p_tab = pb(p3, "p_rank"), pb(p3, "p_tab")
        s_c3, exp_in, exp_out, a_ready, rank_done = sem("const3_loaded"), sem("exp_wanted"), sem("exp_done"), sem("assigned"), sem("ranks_done")
        oh_ready, oh_used, tab_ready = sem("onehots_ready"), sem("onehots_used"), sem("tables_ready")

        with nc.Block() as block:
            @block.sync
            def _(sp):
                sp.dma_start(c3[:], A["c_route"]).then_inc(s_c3, 16)
                sp.dma_start(tri_f[:], A["c_tri"]).then_inc(s_c3, 16)
                for e in range(2):
                    sp.dma_start(w_g[e][:], gate_rows(slice(e, e + 1))).then_inc(s_wg[e], 16)
                    sp.dma_start(w_u[e][:], up_rows(slice(e, e + 1))).then_inc(s_wu[e], 16)
                    sp.dma_start(w_d[e][:], down_rows(slice(e, e + 1))).then_inc(s_wd[e], 16)
                sp.wait_ge(s_c3, 32)

            @block.gpsimd
            def _(pool):
                pool.memset(x_g[0][:], 0.0).then_inc(xg_zero, 1)
                pool.memset(x_g[1][:], 0.0).then_inc(xg_zero, 1)

            @block.scalar
            def _(act):
                act.wait_ge(exp_in, 1)
                act.activation(r4[1][:], r4[0][:], ACT.Exp).then_inc(exp_out, 1)
                act.wait_ge(exp_in, 2)
                act.activation(s9[:, 5, :], s9[:, 4, :], ACT.Exp).then_inc(exp_out, 1)

            @block.tensor
            def _(pe):
                pe.wait_ge(a_ready, 1)
                for i in range(T9):
                    for j in range(i + 1):
                        pe.matmul(p_rank[:, i * E_ALL:(i + 1) * E_ALL], (tri if j == i else ones_b)[:], a_b[:, j, :],
                                  start=(j == 0), stop=(j == i))
                for j in range(T9):
                    ins = pe.matmul(p_rank[:, T9 * E_ALL:(T9 + 1) * E_ALL], ones_b[:], a_b[:, j, :], start=(j == 0), stop=(j == T9 - 1))
                ins.then_inc(rank_done, 1)
                for n in range(2 * T9):
                    pe.wait_ge(oh_ready, n + 1)
                    ins = pe.matmul(p_tab[:, 0:2 * N_BLK], R[n % 4][:], B[n % 4][:].rearrange("p a b -> p (a b)"),
                                    start=(n == 0), stop=(n == 2 * T9 - 1))
                    ins.then_inc(oh_used, 1)

            @block.vector
            def _(dve):
                chain = chains["dve"]
                chain.eng = dve
                dve.wait_ge(s_c3, 32)
                chain(dve.tensor_copy(tri[:], tri_f[:]))
                chain(dve.memset(ones_b[:], 1.0))
                V = dve

                def bc(ap, n):
                    return ap.unsqueeze(2).to_broadcast([P, T9, n])

                def tt(out, a, b, op):
                    chain(V.tensor_tensor(out=out, in0=a, in1=b, op=op))

                def ts(out, a, s1, s2, o1, o2=None):
                    if o2 is None:
                        chain(V.tensor_scalar(out, a, s1, None, o1))
                    else:
                        chain(V.tensor_scalar(out, a, s1, s2, o1, o2))

                def red(out, a, op):
                    chain(V.tensor_reduce(out=out, in_=a, axis=AX.X, op=op))

                def first_max(vals, n, top, idx, hot, tmp):
                    red(top, vals, ALU.max)
                    tt(tmp, vals, bc(top, n), ALU.is_equal)
                    ts(tmp, tmp, -64.0, 64.0, ALU.mult, ALU.add)
                    it = c3[:, 0:n].unsqueeze(1).to_broadcast([P, T9, n])
                    tt(tmp, tmp, it, ALU.add)
                    red(idx, tmp, ALU.min)
                    tt(hot, it, bc(idx, n), ALU.is_equal)

                Lg, Le = logits[:, :, 0:EG], logits[:, :, EG:NR]
                first_max(Lg, EG, s9[:, 0, :], s9[:, 1, :], r4[2][:], r4[3][:])
                V.tensor_tensor(out=r4[0][:], in0=Lg, in1=bc(s9[:, 0, :], EG), op=ALU.subtract).then_inc(exp_in, 1)
                tt(r32[0][:].rearrange("p t (g e) -> p t g e", g=EG), Le.rearrange("p t (g e) -> p t g e", g=EG),
                   r4[2][:].unsqueeze(3).to_broadcast([P, T9, EG, EPG]), ALU.mult)
                red(r8[0][:], r32[0][:].rearrange("p t (g e) -> p t e g", g=EG), ALU.add)
                first_max(r8[0][:], EPG, s9[:, 2, :], s9[:, 6, :], r8[1][:], r8[3][:])
                ts(r8[3][:], r8[1][:], -3.0e38, None, ALU.mult)
                tt(r8[2][:], r8[0][:], r8[3][:], ALU.add)
                first_max(r8[2][:], EPG, s9[:, 3, :], s9[:, 7, :], r8[1][:], r8[3][:])
                V.tensor_tensor(out=s9[:, 4, :], in0=s9[:, 3, :], in1=s9[:, 2, :], op=ALU.subtract).then_inc(exp_in, 1)
                iv = iota_e.unsqueeze(1).to_broadcast([P, T9, E_ALL])
                for c in range(2):
                    ts(s9[:, 8 + c, :], s9[:, 1, :], float(EPG), None, ALU.mult)
                    tt(s9[:, 8 + c, :], s9[:, 8 + c, :], s9[:, 6 + c, :], ALU.add)
                    tt(oh[c][:], iv, bc(s9[:, 8 + c, :], E_ALL), ALU.is_equal)
                    tt(oh[c][:], oh[c][:], bc(valid, E_ALL), ALU.mult)
                V.tensor_tensor(out=a_b[:], in0=oh[0][:], in1=oh[1][:], op=ALU.add).then_inc(a_ready, 1)
                V.wait_ge(exp_out, 2)
                red(s9[:, 10, :], r4[1][:], ALU.add)
                ts(s9[:, 11, :], s9[:, 5, :], 1.0, None, ALU.add)
                tt(s9[:, 10, :], s9[:, 10, :], s9[:, 11, :], ALU.mult)
                chain(V.reciprocal(gate_w[:, 0, :], s9[:, 10, :]))
                tt(gate_w[:, 1, :], gate_w[:, 0, :], s9[:, 5, :], ALU.mult)
                V.wait_ge(rank_done, 1)
                chain(V.tensor_copy(pre[:].rearrange("p t e -> p (t e)"), p_rank[:, 0:T9 * E_ALL]))
                chain(V.tensor_copy(tot[:, 0, :], p_rank[:, T9 * E_ALL:(T9 + 1) * E_ALL]))
                tt(cmp8[:], tot[:, 0, :].unsqueeze(2).to_broadcast([P, E_ALL, 8]), mult8.unsqueeze(1).to_broadcast([P, E_ALL, 8]), ALU.is_gt)
                red(tot[:, 1, :], cmp8[:], ALU.add)
                chain(V.tensor_tensor_scan(out=tot[:, 2, :], data0=tot[:, 1, :], data1=tot[:, 1, :], initial=0.0, op0=ALU.add, op1=ALU.bypass))
                tt(tot[:, 3, :], tot[:, 2, :], tot[:, 1, :], ALU.subtract)
                tt(cmp_o[:], tot[:, 2, :].unsqueeze(1).to_broadcast([P, N_OVER, E_ALL]), iota_o.unsqueeze(2).to_broadcast([P, N_OVER, E_ALL]), ALU.is_le)
                chain(V.tensor_copy(over_f[:, 0:1], tot[:, 2, E_ALL - 1:E_ALL]))
                red(over_f[:, 1:], cmp_o[:], ALU.add)
                ts(over_f[:, 1:], over_f[:, 1:], float(E_ALL - 1), None, ALU.min)
                chain(V.tensor_copy(over[:], over_f[:]))
                for c in range(2):
                    rank, base, rb, r, blk, isov = (s9[:, 12 + 6 * c + q, :] for q in range(6))
                    tt(r32[1][:], oh[c][:], pre[:], ALU.mult)
                    red(rank, r32[1][:], ALU.add)
                    tt(r32[2][:], oh[c][:], tot[:, 3, :].unsqueeze(1).to_broadcast([P, T9, E_ALL]), ALU.mult)
                    red(base, r32[2][:], ALU.add)
                    tt(cmp9[:], bc(rank, 8), mult8.unsqueeze(1).to_broadcast([P, T9, 8]), ALU.is_ge)
                    red(rb, cmp9[:], ALU.add)
                    ts(r, rb, -float(P), None, ALU.mult)
                    tt(r, r, rank, ALU.add)
                    ts(isov, rb, 1.0, None, ALU.min)
                    tt(blk, base, rb, ALU.add)
                    ts(blk, blk, float(E_ALL - 1), None, ALU.add)
                    tt(blk, blk, s9[:, 8 + c, :], ALU.subtract)
                    tt(blk, blk, isov, ALU.mult)
                    tt(blk, blk, s9[:, 8 + c, :], ALU.add)
                    ts(isov, valid, -999.0, 999.0, ALU.mult, ALU.add)
                    tt(blk, blk, isov, ALU.add)
                for t in range(T9):
                    for c in range(2):
                        n = 2 * t + c
                        r, blk = s9[:, 12 + 6 * c + 3, t:t + 1], s9[:, 12 + 6 * c + 4, t:t + 1]
                        if n >= 4:
                            V.wait_ge(oh_used, n - 3)
                        chain(V.tensor_scalar(R[n % 4][:], iota128, r, None, ALU.is_equal))
                        chain(V.tensor_scalar(B[n % 4][:, 0, :], iota_b, blk, y_val[:, c, t:t + 1], ALU.is_equal, ALU.mult))
                        V.tensor_scalar(B[n % 4][:, 1, :], iota_b, blk, m_val[:, t:t + 1], ALU.is_equal, ALU.mult).then_inc(oh_ready, 1)
                V.wait_ge(oh_used, 2 * T9)
                chain(V.tensor_copy(tab[:, 0, :, :].rearrange("p a b -> p (a b)"), p_tab[:, 0:2 * N_BLK]))
                ts(tab[:, 1, :, :], tab[:, 0, :, :], 0.0, NONE, ALU.is_equal, ALU.mult)
                tt(tab[:, 1, :, :], tab[:, 1, :, :], tab[:, 0, :, :], ALU.add)
                ts(tab[:, 1, :, :], tab[:, 1, :, :], -1.0, None, ALU.add)
                chain(V.tensor_copy(y_idx[:], tab[:, 1, 0, :]))
                chain(V.tensor_copy(m_idx[:], tab[:, 1, 1, :]))
        p3.close()

        w_pg = sb(late, "w_ple_gate_sb", [P, KD, D])
        w_pp = sb(late, "w_ple_proj_sb", [P, PLE // P, D])
        s_ple = sem("ple_weights_loaded")
        p4 = ExitStack()
        idx_m = [sb(p4, f"idx_m{i}", [P, 1], I32) for i in range(2)]
        idx_y = [sb(p4, f"idx_y{i}", [P, 1], I32) for i in range(2)]
        xeT = sb(p4, "xeT", [P, KD, P])
        act_g = sb(p4, "silu_gate", [P, F])
        hid = sb(p4, "hidden", [P, F])
        hidT = sb(p4, "hiddenT", [P, KF, P])
        y_sb = [sb(p4, f"y{i}", [P, D]) for i in range(2)]
        p_xe = pb(p4, "p_xe", 2 * CHUNK)
        p_g = [pb(p4, f"p_g{i}") for i in range(2)]
        p_u, p_ht = pb(p4, "p_u"), pb(p4, "p_ht")
        p_y = pb(p4, "p_y", 2 * CHUNK)
        s_xg = [sem("x_gathered0"), sem("x_gathered1")]
        s_ys = [sem("y_scattered0"), sem("y_scattered1")]
        idx_ready, pool_held = sem("indices_copied"), sem("pool_waits_held")
        xe_t, xeT_a, xeT_v = sem("xe_transposed"), sem("xeT_copied_act"), sem("xeT_copied_dve")
        g_done, u_done, silu_ready, hid_ready = sem("gate_done"), sem("up_done"), sem("silu_ready"), sem("hidden_ready")
        ht_done, hidT_ready, y_done, y_a, y_v = sem("hidden_transposed"), sem("hiddenT_copied"), sem("down_done"), sem("y_copied_act"), sem("y_copied_dve")

        def experts(eng, body):
            for e in range(3):
                body(e, e % 2, None)
            with eng.Fori(0, (E_ALL - 6) // 2) as i:
                body(i * 2 + 3, 1, i)
                body(i * 2 + 4, 0, i)
            for e in range(E_ALL - 3, E_ALL):
                body(e, e % 2, None)

        def turn(e, par, i):
            return e // 2 + 1 if i is None else (i + 2 if par else i + 3)

        with nc.Block() as block:
            @block.sync
            def _(sp):
                sp.dma_start(w_pg[:], A["w_ple_gate"].rearrange("(k p) n -> p k n", p=P)).then_inc(s_ple, 16)
                sp.dma_start(w_pp[:], A["w_ple_proj"].rearrange("(k p) n -> p k n", p=P)).then_inc(s_ple, 16)

                def expert(e, par, i):
                    if i is None and e + 2 >= E_ALL:
                        return
                    sl = slice(e + 2, e + 3) if i is None else bass.ds(e + 2, 1)
                    sp.wait_ge(g_done, e + 1)
                    sp.dma_start(w_g[par][:], gate_rows(sl)).then_inc(s_wg[par], 16)
                    sp.wait_ge(u_done, e + 1)
                    sp.dma_start(w_u[par][:], up_rows(sl)).then_inc(s_wu[par], 16)
                    sp.wait_ge(y_done, e + 1)
                    sp.dma_start(w_d[par][:], down_rows(sl)).then_inc(s_wd[par], 16)

                experts(sp, expert)

            @block.gpsimd
            def _(pool):
                def gather(e, par, nth_index):
                    pool.tensor_copy(idx_m[par][:], m_idx[:, bass.ds(e, 1)]).then_inc(idx_ready, 1)
                    pool.wait_ge(idx_ready, nth_index)
                    pool.sem_inc(pool_held, 1)
                    pool.indirect_dma_start(out=x_g[par][:], out_offset=None, in_=m_dram,
                                            in_offset=bass.IndirectOffsetOnAxis(ap=idx_m[par][:, 0:1], axis=0),
                                            bounds_check=ROWS - 1, oob_is_err=False).then_inc(s_xg[par], 16)

                pool.wait_ge(xg_zero, 2)
                gather(0, 0, 1)
                gather(1, 1, 2)

                def expert(e, par, i):
                    pool.wait_ge(y_a, e + 1)
                    pool.wait_ge(y_v, e + 1)
                    pool.sem_inc(pool_held, 1)
                    pool.tensor_copy(idx_y[par][:], y_idx[:, bass.ds(e, 1)]).then_inc(idx_ready, 1)
                    pool.wait_ge(idx_ready, e * 2 + 3 if i is not None or e < E_ALL - 2 else E_ALL + e + 1)
                    pool.sem_inc(pool_held, 1)
                    pool.indirect_dma_start(out=y_dram, out_offset=bass.IndirectOffsetOnAxis(ap=idx_y[par][:, 0:1], axis=0),
                                            in_=y_sb[par][:], in_offset=None,
                                            bounds_check=2 * ROWS - 1, oob_is_err=False).then_inc(s_ys[par], 16)
                    if i is not None or e + 2 < E_ALL:
                        gather(e + 2, par, e * 2 + 4)

                experts(pool, expert)
                pool.wait_ge(s_ys[0], 16 * (E_ALL // 2))
                pool.wait_ge(s_ys[1], 16 * (E_ALL // 2))

            @block.tensor
            def _(pe):
                def transpose_x(par, nth):
                    pe.wait_ge(s_xg[par], nth * 16)
                    for k in range(KD):
                        ins = pe.transpose(p_xe[:, k * P:(k + 1) * P], x_g[par][:, k * P:(k + 1) * P], ident[:])
                    ins.then_inc(xe_t, 1)

                def up_down(e, par, i, first=False):
                    pe.wait_ge(hidT_ready, e + 1)
                    pe.wait_ge(s_wd[par], turn(e, par, i) * 16)
                    if not first:
                        pe.wait_ge(y_a, e)
                        pe.wait_ge(y_v, e)
                    for n in range(2):
                        for k in range(KF):
                            ins = pe.matmul(p_y[:, n * CHUNK:(n + 1) * CHUNK], hidT[:, k, :], w_d[par][:, k, n * CHUNK:(n + 1) * CHUNK],
                                            start=(k == 0), stop=(k == KF - 1))
                    ins.then_inc(y_done, 1)

                transpose_x(0, 1)

                def expert(e, par, i):
                    first, last = (i is None and e == 0), (i is None and e == E_ALL - 1)
                    pe.wait_ge(xeT_a, e + 1)
                    pe.wait_ge(xeT_v, e + 1)
                    pe.wait_ge(s_wg[par], turn(e, par, i) * 16)
                    for k in range(KD):
                        ins = pe.matmul(p_g[par][:], xeT[:, k, :], w_g[par][:, k, :], start=(k == 0), stop=(k == KD - 1))
                    ins.then_inc(g_done, 1)
                    pe.wait_ge(s_wu[par], turn(e, par, i) * 16)
                    if not first:
                        pe.wait_ge(hid_ready, e)
                    for k in range(KD):
                        ins = pe.matmul(p_u[:], xeT[:, k, :], w_u[par][:, k, :], start=(k == 0), stop=(k == KD - 1))
                    ins.then_inc(u_done, 1)
                    if not last:
                        transpose_x(1 - par, (turn(e, par, i) + (0 if par == 0 else 1)))
                    pe.wait_ge(hid_ready, e + 1)
                    for c in range(KF):
                        ins = pe.transpose(p_ht[:, c * P:(c + 1) * P], hid[:, c * P:(c + 1) * P], ident[:])
                    ins.then_inc(ht_done, 1)
                    up_down(e, par, i, first)

                experts(pe, expert)

            @block.scalar
            def _(act):
                def copy_x(e):
                    act.wait_ge(xe_t, e + 1)
                    act.activation(xeT[:, 0:4, :], p_xe[:, 0:CHUNK].rearrange("p (k n) -> p k n", n=P), ACT.Copy).then_inc(xeT_a, 1)

                copy_x(0)

                def expert(e, par, i):
                    first, last = (i is None and e == 0), (i is None and e == E_ALL - 1)
                    act.wait_ge(g_done, e + 1)
                    if not first:
                        act.wait_ge(hid_ready, e)
                    act.activation(act_g[:], p_g[par][:], ACT.Silu).then_inc(silu_ready, 1)
                    if not last:
                        copy_x(e + 1)
                    act.wait_ge(ht_done, e + 1)
                    act.activation(hidT[:].rearrange("p k n -> p (k n)"), p_ht[:], ACT.Copy).then_inc(hidT_ready, 1)
                    act.wait_ge(y_done, e + 1)
                    nth = turn(e, par, i)
                    if not (i is None and e < 2):
                        act.wait_ge(s_ys[par], (nth - 1) * 16)
                    act.activation(y_sb[par][:, 0:CHUNK], p_y[:, 0:CHUNK], ACT.Copy).then_inc(y_a, 1)

                experts(act, expert)

            @block.vector
            def _(dve):
                def copy_x(e):
                    dve.wait_ge(xe_t, e + 1)
                    dve.tensor_copy(xeT[:, 4:8, :], p_xe[:, CHUNK:2 * CHUNK].rearrange("p (k n) -> p k n", n=P)).then_inc(xeT_v, 1)

                copy_x(0)

                def expert(e, par, i):
                    first, last = (i is None and e == 0), (i is None and e == E_ALL - 1)
                    dve.wait_ge(silu_ready, e + 1)
                    dve.wait_ge(u_done, e + 1)
                    if not first:
                        dve.wait_ge(ht_done, e)
                    dve.tensor_tensor(out=hid[:], in0=act_g[:], in1=p_u[:], op=ALU.mult).then_inc(hid_ready, 1)
                    if not last:
                        copy_x(e + 1)
                    dve.wait_ge(y_done, e + 1)
                    nth = turn(e, par, i)
                    if not (i is None and e < 2):
                        dve.wait_ge(s_ys[par], (nth - 1) * 16)
                    dve.tensor_copy(y_sb[par][:, CHUNK:2 * CHUNK], p_y[:, CHUNK:2 * CHUNK]).then_inc(y_v, 1)

                experts(dve, expert)

        v_w, v_x, v_y = sem("over_weights"), sem("over_gathered"), sem("over_scattered")
        v_i, v_free, v_xt, v_xc = sem("over_indices"), sem("over_turn_free"), sem("over_x_T"), sem("over_xT_copied")
        v_gu, v_s, v_h, v_ht, v_hc, v_yd, v_yc = (sem("over_gate_up"), sem("over_silu"), sem("over_hidden"), sem("over_hidden_T"),
                                                  sem("over_hiddenT_copied"), sem("over_down"), sem("over_y_copied"))
        with nc.Block() as block:
            def turns(eng, body, extra=None):
                n = eng.value_load(over[0:1, 0:1], min_val=0, max_val=N_OVER)
                with eng.If(n > 0):
                    with eng.Fori(0, n) as v:
                        body(v)
                        if extra:
                            extra(v)

            @block.sync
            def _(sp):
                def body(v):
                    sp.wait_ge(v_free, v + 1)
                    e = sp.value_load(over[0:1, bass.ds(v + 1, 1)], min_val=0, max_val=E_ALL - 1)
                    sp.dma_start(w_g[0][:], gate_rows(bass.ds(e, 1))).then_inc(v_w, 16)
                    sp.dma_start(w_u[0][:], up_rows(bass.ds(e, 1))).then_inc(v_w, 16)
                    sp.dma_start(w_d[0][:], down_rows(bass.ds(e, 1))).then_inc(v_w, 16)
                turns(sp, body)

            @block.gpsimd
            def _(pool):
                pool.sem_inc(v_free, 1)

                def body(v):
                    pool.tensor_copy(idx_m[0][:], m_idx[:, bass.ds(v + E_ALL, 1)]).then_inc(v_i, 1)
                    pool.tensor_copy(idx_y[0][:], y_idx[:, bass.ds(v + E_ALL, 1)]).then_inc(v_i, 1)
                    pool.wait_ge(v_i, v * 2 + 2)
                    pool.sem_inc(pool_held, 1)
                    pool.indirect_dma_start(out=x_g[0][:], out_offset=None, in_=m_dram,
                                            in_offset=bass.IndirectOffsetOnAxis(ap=idx_m[0][:, 0:1], axis=0),
                                            bounds_check=ROWS - 1, oob_is_err=False).then_inc(v_x, 16)
                    pool.wait_ge(v_yc, v + 1)
                    pool.sem_inc(pool_held, 1)
                    pool.indirect_dma_start(out=y_dram, out_offset=bass.IndirectOffsetOnAxis(ap=idx_y[0][:, 0:1], axis=0),
                                            in_=y_sb[0][:], in_offset=None,
                                            bounds_check=2 * ROWS - 1, oob_is_err=False).then_inc(v_y, 16)
                    pool.wait_ge(v_y, v * 16 + 16)
                    pool.sem_inc(v_free, 1)
                turns(pool, body)

            @block.tensor
            def _(pe):
                def body(v):
                    pe.wait_ge(v_x, v * 16 + 16)
                    for k in range(KD):
                        ins = pe.transpose(p_xe[:, k * P:(k + 1) * P], x_g[0][:, k * P:(k + 1) * P], ident[:])
                    ins.then_inc(v_xt, 1)
                    pe.wait_ge(v_xc, v + 1)
                    pe.wait_ge(v_w, v * 48 + 48)
                    for out, w in ((p_g[0], w_g[0]), (p_u, w_u[0])):
                        for k in range(KD):
                            ins = pe.matmul(out[:], xeT[:, k, :], w[:, k, :], start=(k == 0), stop=(k == KD - 1))
                    ins.then_inc(v_gu, 1)
                    pe.wait_ge(v_h, v + 1)
                    for c in range(KF):
                        ins = pe.transpose(p_ht[:, c * P:(c + 1) * P], hid[:, c * P:(c + 1) * P], ident[:])
                    ins.then_inc(v_ht, 1)
                    pe.wait_ge(v_hc, v + 1)
                    for n in range(2):
                        for k in range(KF):
                            ins = pe.matmul(p_y[:, n * CHUNK:(n + 1) * CHUNK], hidT[:, k, :], w_d[0][:, k, n * CHUNK:(n + 1) * CHUNK],
                                            start=(k == 0), stop=(k == KF - 1))
                    ins.then_inc(v_yd, 1)
                turns(pe, body)

            @block.scalar
            def _(act):
                def body(v):
                    act.wait_ge(v_gu, v + 1)
                    act.activation(act_g[:], p_g[0][:], ACT.Silu).then_inc(v_s, 1)
                    act.wait_ge(v_ht, v + 1)
                    act.activation(hidT[:].rearrange("p k n -> p (k n)"), p_ht[:], ACT.Copy).then_inc(v_hc, 1)
                turns(act, body)

            @block.vector
            def _(dve):
                def body(v):
                    dve.wait_ge(v_xt, v + 1)
                    dve.tensor_copy(xeT[:].rearrange("p k n -> p (k n)"), p_xe[:]).then_inc(v_xc, 1)
                    dve.wait_ge(v_s, v + 1)
                    dve.tensor_tensor(out=hid[:], in0=act_g[:], in1=p_u[:], op=ALU.mult).then_inc(v_h, 1)
                    dve.wait_ge(v_yd, v + 1)
                    dve.tensor_copy(y_sb[0][:], p_y[:]).then_inc(v_yc, 1)
                turns(dve, body)
        p4.close()

        p5 = ExitStack()
        h5 = [sb(p5, f"h5_{i}", [P, D]) for i in range(2)]
        y5 = [sb(p5, f"y5_{i}", [P, 2, D]) for i in range(2)]
        pl = [sb(p5, f"ple_in{i}", [P, PLE]) for i in range(2)]
        n_T = sb(p5, "n_T", [P, KD, P])
        pl_T = sb(p5, "ple_T", [P, PLE // P, P])
        sg = sb(p5, "sigmoid_gate", [P, D])
        o5 = [sb(p5, f"out{i}", [P, D]) for i in range(2)]
        junk5 = sb(p5, "squares_of_h2", [P, D], BF16)
        st5 = sb(p5, "stats5", [P, 4])
        p_nt = pb(p5, "p_nt", 2 * CHUNK)
        p_plt = pb(p5, "p_plt")
        p_gt = pb(p5, "p_gt", 2 * CHUNK)
        p_pp = pb(p5, "p_pp", 2 * CHUNK)
        s_l = [sem("tile_loaded0"), sem("tile_loaded1")]
        y0_zero, h2a, h2_ready = sem("y_rows_zeroed"), sem("h_plus_first"), sem("h2_ready")
        nt_done, nT_ready, plT_ready = sem("h2_transposed"), sem("n_T_copied"), sem("ple_T_copied")
        gt_done, ss5, var5, std5, r5 = sem("ple_products_done"), sem("h2_squares"), sem("h2_var"), sem("h2_std"), sem("h2_rstd")
        sg_ready, gp_ready, o_ready = sem("sigmoid_ready"), sem("gated_ready"), sem("out_ready")
        s_o = [sem("out_stored0"), sem("out_stored1")]

        def loads(T, i, par):
            return T // 2 + 1 if i is None else (i + 1 if par else i + 2)

        with nc.Block() as block:
            @block.sync
            def _(sp):
                def load(T, par):
                    rows = bass.ts(T, P)
                    sp.dma_start(h5[par][:], h_dram[rows, :]).then_inc(s_l[par], 16)
                    sp.dma_start(pl[par][:], A["p_all"][rows, :]).then_inc(s_l[par], 16)
                    sp.dma_start(y5[par][:], y_dram.rearrange("(t c) n -> t c n", c=2)[rows, :, :]).then_inc(s_l[par], 16)

                sp.dma_start(h5[0][:], h_dram[0:P, :]).then_inc(s_l[0], 16)
                sp.dma_start(pl[0][:], A["p_all"][0:P, :]).then_inc(s_l[0], 16)
                sp.wait_ge(y0_zero, 1)
                sp.dma_start(y5[0][0:NS, :, :], y_dram.rearrange("(t c) n -> t c n", c=2)[0:NS, :, :]).then_inc(s_l[0], 16)
                load(1, 1)

                def tile(T, par, i=None):
                    sp.wait_ge(o_ready, T + 1)
                    sp.dma_start(O["y_all"][bass.ts(T, P), :], o5[par][:]).then_inc(s_o[par], 16)
                    if i is not None or T + 2 < T_ALL:
                        load(T + 2, par)

                tiles(sp, tile)
                sp.wait_ge(s_o[0], 16 * 6)
                sp.wait_ge(s_o[1], 16 * 5)

            @block.tensor
            def _(pe):
                pe.wait_ge(s_ple, 32)

                def transposes(T, par, nth, first=False):
                    pe.wait_ge(h2_ready, T + 1)
                    for k in range(KD):
                        pe.transpose(p_nt[:, k * P:(k + 1) * P], h5[par][:, k * P:(k + 1) * P], ident[:])
                    for k in range(PLE // P):
                        ins = pe.transpose(p_plt[:, k * P:(k + 1) * P], pl[par][:, k * P:(k + 1) * P], ident[:])
                    ins.then_inc(nt_done, 1)

                transposes(0, 0, 1)

                def tile(T, par, i=None):
                    first = isinstance(T, int) and T == 0
                    pe.wait_ge(plT_ready, T + 1)
                    pe.wait_ge(nT_ready, T + 1)
                    if not first:
                        pe.wait_ge(gp_ready, T)
                    for n in range(2):
                        cs = slice(n * CHUNK, (n + 1) * CHUNK)
                        for k in range(KD):
                            pe.matmul(p_gt[:, cs], n_T[:, k, :], w_pg[:, k, cs], start=(k == 0), stop=(k == KD - 1))
                        for k in range(PLE // P):
                            ins = pe.matmul(p_pp[:, cs], pl_T[:, k, :], w_pp[:, k, cs], start=(k == 0), stop=(k == PLE // P - 1))
                    ins.then_inc(gt_done, 1)
                    if i is not None or T + 1 < T_ALL:
                        transposes(T + 1, 1 - par, 0)

                tiles(pe, tile)

            @block.scalar
            def _(act):
                def tile(T, par, i=None):
                    first = isinstance(T, int) and T == 0
                    act.wait_ge(h2_ready, T + 1)
                    act.activation(junk5[:], h5[par][:], ACT.Square, accum_out=st5[:, 0:1]).then_inc(ss5, 1)
                    act.wait_ge(nt_done, T + 1)
                    act.activation(pl_T[:].rearrange("p k n -> p (k n)"), p_plt[:, 0:PLE], ACT.Copy).then_inc(plT_ready, 1)
                    act.wait_ge(var5, T + 1)
                    act.activation(st5[:, 2:3], st5[:, 1:2], ACT.Sqrt).then_inc(std5, 1)
                    act.wait_ge(r5, T + 1)
                    act.wait_ge(gt_done, T + 1)
                    act.activation(sg[:], p_gt[:], ACT.Sigmoid, scale=st5[:, 3:4]).then_inc(sg_ready, 1)

                tiles(act, tile)

            @block.vector
            def _(dve):
                dve.memset(y5[0][:], 0.0).then_inc(y0_zero, 1)
                for par in range(2):
                    dve.sem_inc(s_o[par], 16)

                def combine(T, par, nth):
                    dve.wait_ge(s_l[par], 48 * nth)
                    dve.scalar_tensor_tensor(out=h5[par][:], in0=y5[par][:, 0, :], scalar=gate_w[:, 0, bass.ds(T, 1)], in1=h5[par][:],
                                             op0=ALU.mult, op1=ALU.add).then_inc(h2a, 1)
                    dve.wait_ge(h2a, T + 1)
                    dve.scalar_tensor_tensor(out=h5[par][:], in0=y5[par][:, 1, :], scalar=gate_w[:, 1, bass.ds(T, 1)], in1=h5[par][:],
                                             op0=ALU.mult, op1=ALU.add).then_inc(h2_ready, 1)

                combine(0, 0, 1)

                def tile(T, par, i=None):
                    first = isinstance(T, int) and T == 0
                    dve.wait_ge(nt_done, T + 1)
                    dve.tensor_tensor(out=n_T[:], in0=p_nt[:].rearrange("p (k n) -> p k n", n=P),
                                      in1=g_ple_c.unsqueeze(2).to_broadcast([P, KD, P]), op=ALU.mult).then_inc(nT_ready, 1)
                    dve.wait_ge(ss5, T + 1)
                    dve.tensor_scalar(st5[:, 1:2], st5[:, 0:1], 1.0 / D, EPS, ALU.mult, ALU.add).then_inc(var5, 1)
                    dve.wait_ge(std5, T + 1)
                    dve.reciprocal(st5[:, 3:4], st5[:, 2:3]).then_inc(r5, 1)
                    if i is not None or T + 1 < T_ALL:
                        combine(T + 1, 1 - par, (T + 1) // 2 + 1 if i is None else i + 2)
                    dve.wait_ge(sg_ready, T + 1)
                    dve.wait_ge(gt_done, T + 1)
                    dve.wait_ge(s_o[par], loads(T, i, par) * 16)
                    dve.tensor_tensor(out=o5[par][:], in0=sg[:], in1=p_pp[:], op=ALU.mult).then_inc(gp_ready, 1)
                    dve.wait_ge(gp_ready, T + 1)
                    dve.tensor_tensor(out=o5[par][:], in0=o5[par][:], in1=h5[par][:], op=ALU.add).then_inc(o_ready, 1)

                tiles(dve, tile)
        p5.close()
        late.close()


def constants():
    t = np.arange(P)
    band = np.zeros((P, NG, 5, P), np.float32)
    for g, w in enumerate(WINDOWS):
        s_, t_ = t[:, None], t[None, :]
        inside = (s_ <= t_) & (t_ - s_ < w)
        same = (s_ == t_).astype(np.float32)
        band[:, g, V_PREV] = (t_ + P - s_ < w) / w
        band[:, g, V_FIRST] = inside / np.minimum(t_ + 1, w) - same
        band[:, g, V_CUR] = inside / w - same
        for b in range(NS):
            for r in range(STATE):
                band[b * STATE + r, g, V_STATE, b] = (r >= STATE - (w - 1)) / w
            band[b, g, V_NEW, b] = 1.0 / w - 1.0
    route = np.zeros((P, 272), np.float32)
    route[:, 0:128] = t
    route[:, 128:160] = np.arange(E_ALL)
    route[:, 160:160 + N_BLK] = np.arange(N_BLK)
    route[:, 208:216] = P * np.arange(1, 9)
    for T in range(T_ALL):
        route[:, 216 + T] = 1.0 if T else (t < NS)
        for c in range(2):
            route[:, 225 + c * 9 + T] = 2 * (T * P + t) + c + 1
        route[:, 243 + T] = T * P + t + 1
    route[:, 252:252 + N_OVER] = np.arange(N_OVER)
    return {
        "c_ident": np.eye(P, dtype=np.float32), "c_band": band, "c_route": route,
        "c_mask": np.where(t[None, :] >= t[:, None], np.float32(-240000.0), np.float32(0.0)),
        "c_tri": (t[:, None] < t[None, :]).astype(np.float32),
    }


def kernel(**inputs):
    import concourse.bacc as bacc
    from concourse.bass_utils import run_bass_kernel_spmd

    x = {k: np.asarray(v) for k, v in inputs.items()}

    def tiled(prompt, sample):
        out = np.zeros((ROWS, prompt.shape[-1]), prompt.dtype)
        out[0:NS] = sample.reshape(NS, -1)
        out[P:] = prompt.reshape(SEQ, -1)
        return out

    cols = np.zeros((P, 64), np.float32)
    for at, name in ((0, "g_mix"), (8, "g_ffn"), (16, "g_ple")):
        cols[:, at:at + 8] = x[name][0].reshape(KD, P).T
    cols[:, 24:28] = x["s_pool"][0].reshape(NG, PW).T
    bias = x["b_sb"][0]
    cols[:, 36:44] = bias
    cols[0:NS * H, 45] = np.tile(bias, NS)
    state = np.zeros((P, AW), np.float32)
    state[0:NS * STATE] = x["state_pool"][0].reshape(NS * STATE, AW)
    arrays = {
        "x_all": tiled(x["x_prompt"], x["x_sample"]),
        "p_all": tiled(x["p_prompt"][0], x["p_sample"][0]),
        "cache_k": x["cache_k"][0].reshape(-1, P, AW), "cache_v": x["cache_v"][0].reshape(-1, P, AW),
        "state_pool": x["state_pool"][0], "state_rows": state,
        "page_table": x["page_table"].reshape(1, -1),
        "w_in": x["w_in"][0], "w_out": x["w_out"][0],
        "w_pool": x["w_pool"][0].transpose(1, 0, 2),
        "g_qk": np.stack([np.broadcast_to(x["g_q"][0], (P, HD)), np.broadcast_to(x["g_k"][0], (P, HD))], axis=1),
        "c_cols": cols,
        "g_ffn_bc": np.broadcast_to(x["g_ffn"][0], (P, D)),
        "w_router": np.concatenate([x["w_router_group"][0], x["w_router_expert"][0]], axis=1).reshape(KD, P, NR).transpose(1, 0, 2),
        "b_router": np.broadcast_to(np.concatenate([x["b_router_group"][0], x["b_router_expert"][0]]), (P, NR)),
        "w_gate": x["w_gate"][0], "w_up": x["w_up"][0], "w_down": x["w_down"][0],
        "w_ple_gate": x["w_ple_gate"][0], "w_ple_proj": x["w_ple_proj"][0],
    }
    arrays.update(constants())
    arrays = {f"in_{k}": np.ascontiguousarray(v) for k, v in arrays.items()}
    nc = bacc.Bacc("TRN2", target_bir_lowering=False, num_devices=1)
    A = {k[3:]: nc.dram_tensor(k, v.shape, mybir.dt.from_np(v.dtype), kind="ExternalInput").ap() for k, v in arrays.items()}
    outs = {"y_all": (ROWS, D), "k_all": (ROWS, AW), "v_all": (ROWS, AW),
            "pool_prompt": (STATE, AW), "pool_sample": (NS, STATE, AW)}
    O = {k: nc.dram_tensor("out_" + k, s, F32, kind="ExternalOutput").ap() for k, s in outs.items()}
    build(nc, A, O)
    r = run_bass_kernel_spmd(nc, [arrays], core_ids=[0]).results[0]
    y, k, v = r["out_y_all"], r["out_k_all"], r["out_v_all"]
    return (y[P:].reshape(1, SEQ, D), y[0:NS].reshape(NS, 1, D),
            k[P:].reshape(1, 1, SEQ, H, HD), v[P:].reshape(1, 1, SEQ, H, HD), r["out_pool_prompt"].reshape(1, 1, STATE, AW),
            k[0:NS].reshape(1, NS, 1, H, HD), v[0:NS].reshape(1, NS, 1, H, HD), r["out_pool_sample"].reshape(1, NS, STATE, AW))
```

```python
import numpy as np
import concourse.bass as bass
from concourse import mybir
from contextlib import ExitStack

F32 = mybir.dt.float32
F32R = mybir.dt.float32r
BF16 = mybir.dt.bfloat16
I32 = mybir.dt.int32
ALU = mybir.AluOpType
ACT = mybir.ActivationFunctionType
AX = mybir.AxisListType

P = 128
D = 1024
KD = D // P
SEQ, NS = 1024, 8
T_ALL = 1 + SEQ // P
ROWS = T_ALL * P
AW = 512
H, HD = 8, 64
NG, PW = 4, 128
WINDOWS = (2, 4, 8, 16)
STATE = 15
PAGES = 8
E_ALL, EG, EPG = 32, 4, 8
F = 512
KF = F // P
NR = EG + E_ALL
PLE = 256
EPS = 1e-6
SCALE = HD ** -0.5
N_OVER = (2 * (SEQ + NS) - 1) // P
N_BLK = E_ALL + N_OVER
CHUNK = 512
Q_RING = 4
V_RING = 4
MW = D + 16
NONE = 100000.0
V_PREV, V_FIRST, V_CUR, V_STATE, V_NEW = range(5)


class Chain:

    def __init__(self, eng, sem):
        self.eng, self.sem, self.base, self.n = eng, sem, 0, 0

    def __call__(self, ins):
        self.n += 1
        ins.then_inc(self.sem, 1)
        self.eng.wait_ge(self.sem, self.base + self.n)

    def loop(self, i, per_turn):
        self.start, self.per_turn = self.n, per_turn
        self.base = i * per_turn

    def end(self, turns):
        assert self.n == self.start + self.per_turn, (self.n - self.start, self.per_turn)
        self.base, self.n = 0, self.start + self.per_turn * turns


def tiles(eng, body, chain=None, per_turn=0):
    body(0, 0)
    if chain:
        n = chain.n
    with eng.Fori(0, 3) as i:
        if chain:
            chain.loop(i, per_turn)
        body(i * 2 + 1, 1, i)
        body(i * 2 + 2, 0, i)
    if chain:
        chain.end(3)
    body(7, 1)
    body(8, 0)


def build(nc, A, O):
    ctx = ExitStack()
    uniq = [0]

    def dram(name, shape, dt=F32):
        return nc.dram_tensor(name, shape, dt, kind="Internal").ap()

    def sb(stack, name, shape, dt=F32):
        return stack.enter_context(nc.sbuf_tensor(name, shape, dt))

    def pb(stack, name, cols=CHUNK):
        return stack.enter_context(nc.psum_tensor(name, [P, cols], F32))

    def sem(name):
        return ctx.enter_context(nc.semaphore(name))

    q_dram = dram("q_samples", [NS, AW])
    h_dram = dram("h_rows", [ROWS, D])
    m_dram = dram("expert_input_rows", [ROWS, MW])
    y_dram = dram("expert_rows", [2 * ROWS, D])

    with ctx:
        ident = sb(ctx, "ident", [P, P])
        w_rt = sb(ctx, "w_router_sb", [P, KD, NR])
        b_rt = sb(ctx, "b_router_sb", [P, NR])
        cols = sb(ctx, "per_partition", [P, 64])
        g_mix_c, g_ffn_c, g_ple_c = cols[:, 0:8], cols[:, 8:16], cols[:, 16:24]
        s_pool_c = cols[:, 24:28]
        nb_c, pb_c = cols[:, 28:36], cols[:, 36:44]
        nbs_c, pbs_c = cols[:, 44:45], cols[:, 45:46]
        logits = sb(ctx, "logits", [P, T_ALL, NR])
        gate_w = sb(ctx, "gate_weights", [P, 2, T_ALL])
        h_sq = sb(ctx, "h_squares_sum", [P, T_ALL])
        h_rs = sb(ctx, "h_rstd", [P, 3, T_ALL])

        dve_chain, act_chain, pool_chain = sem("dve_chain"), sem("act_chain"), sem("pool_chain")
        chains = {}
        s_const = sem("const_loaded")
        s_out = sem("outputs_stored")
        n_out = [0]

        mid = ctx.enter_context(ExitStack())
        qT = sb(mid, "qT", [P, H // 2, SEQ])
        kT = sb(mid, "kT", [P, H // 2, SEQ])
        v_sb = sb(mid, "v_sb", [P, T_ALL, AW])
        mixp = sb(mid, "pool_mixed_T", [P, NG, ROWS])
        zd = sb(mid, "decode_scores", [P, PAGES, P])
        table = sb(mid, "page_table_sb", [1, NS * PAGES], I32)

        p1 = ExitStack()
        w_in = sb(p1, "w_in_sb", [P, KD, 4 * AW])
        band = sb(p1, "band", [P, NG, 3, P])
        w_pl = sb(p1, "w_pool_sb", [P, NG, PW])
        g_qk = sb(p1, "g_qk", [P, 2, HD])
        x_sb = [sb(p1, f"x{i}", [P, D]) for i in range(2)]
        xT = sb(p1, "xT", [P, KD, P])
        z_qk = sb(p1, "z_qk", [P, 2 * AW])
        sq = sb(p1, "squares", [P, 2 * AW])
        qk_n = [sb(p1, f"qk_norm{i}", [P, 2 * AW]) for i in range(2)]
        u_s = sb(p1, "u_samples", [P, AW])
        u_sb = [sb(p1, f"u{i}", [P, AW]) for i in range(2)]
        st_sb = sb(p1, "state_sb", [P, AW])
        pooledT = sb(p1, "pooledT", [P, NG, P])
        k_pg = [sb(p1, f"k_page{i}", [P, AW]) for i in range(Q_RING)]
        q_bc = [sb(p1, f"q_bc{i}", [P, AW]) for i in range(2)]
        band_state, band_new = (q[:].rearrange("p (g n) -> p g n", n=P) for q in q_bc)
        prod = [sb(p1, f"prod{i}", [P, AW]) for i in range(2)]
        sq_act = sb(p1, "squares_of_x", [P, D], BF16)
        st1 = sb(p1, "stats1", [P, 4])
        st16 = sb(p1, "stats16", [P, 3, 16])
        p_xt = pb(p1, "p_xt", 2 * CHUNK)
        p_z = [pb(p1, f"p_z{i}") for i in range(2)]
        p_qk = pb(p1, "p_qk", 2 * CHUNK)
        p_pool = pb(p1, "p_pool")
        p_py = pb(p1, "p_py")

        s_x = [sem("x_loaded0"), sem("x_loaded1")]
        xt_done = sem("x_transposed")
        xT_ready = sem("xT_copied")
        z_done = sem("z_chunks_done")
        ssx_ready, var_ready, std_ready, rx_ready = sem("x_squares"), sem("x_var"), sem("x_std"), sem("x_rstd")
        zqk_ready = sem("z_qk_copied")
        v_ready, u_ready = sem("v_copied"), sem("u_copied")
        var16, std16 = sem("qk_var"), sem("qk_std")
        qkn_ready = sem("qk_normalised")
        qkt_done, qT_ready, kT_ready = sem("qk_transposed"), sem("qT_copied"), sem("kT_copied")
        pool_done, pooledT_ready = sem("pooled_done"), sem("pooledT_copied")
        py_done, mixp_ready = sem("pool_map_done"), sem("pool_mixed_copied")
        s_k = sem("k_stored")
        s_q = sem("q_samples_stored")
        s_qb = [sem("q_bc_loaded0"), sem("q_bc_loaded1")]
        s_kp = [sem(f"k_page_loaded{i}") for i in range(Q_RING)]
        page_used = sem("k_page_used")
        prod_ready, prod_used = sem("prod_ready"), sem("prod_used")
        qbc_used = sem("q_bc_used")

        s_first = sem("ident_cols_loaded")
        s_win = [sem(f"w_in_loaded{n}") for n in range(4)]
        N_CONST = 9
        with nc.Block() as block:
            @block.sync
            def _(sp):
                def const(out, in_):
                    sp.dma_start(out, in_).then_inc(s_const, 16)

                sp.dma_start(ident[:], A["c_ident"]).then_inc(s_first, 16)
                sp.dma_start(cols[:], A["c_cols"]).then_inc(s_first, 16)
                sp.dma_start(x_sb[0][:], A["x_all"][0:P, :]).then_inc(s_x[0], 16)
                w_rows = A["w_in"].rearrange("(k p) n -> p k n", p=P)
                for n in range(4):
                    sp.dma_start(w_in[:, :, n * AW:(n + 1) * AW], w_rows[:, :, n * AW:(n + 1) * AW]).then_inc(s_win[n], 16)
                consts = [
                    (g_qk[:], A["g_qk"]), (band[:], A["c_band"][:, :, 0:3, :]),
                    (band_state, A["c_band"][:, :, V_STATE, :]), (band_new, A["c_band"][:, :, V_NEW, :]),
                    (w_pl[:], A["w_pool"]), (st_sb[:], A["state_rows"]),
                    (table[:], A["page_table"]),
                    (w_rt[:], A["w_router"]), (b_rt[:], A["b_router"]),
                ]
                for out, in_ in consts:
                    const(out, in_)
                sp.dma_start(x_sb[1][:], A["x_all"][P:2 * P, :]).then_inc(s_x[1], 16)
                sp.dma_start(O["pool_sample"][:, 0:STATE - 1, :], A["state_pool"][:, 1:STATE, :]).then_inc(s_out, 16)
                n_out[0] += 1
                sp.wait_ge(s_const, 16 * len(consts))

                def tile(T, par, i=None):
                    last = isinstance(T, int) and T >= 7
                    if not last:
                        sp.wait_ge(ssx_ready, T + 1)
                        sp.wait_ge(xt_done, T + 1)
                        sp.dma_start(x_sb[par][:], A["x_all"][bass.ts(T + 2, P), :]).then_inc(s_x[par], 16)
                    first = isinstance(T, int) and T == 0
                    if not first:
                        b = T - 1
                        sp.wait_ge(qbc_used, T)
                        sp.wait_ge(pool_done, T)
                        sp.dma_start(q_bc[1 - par][:], q_dram[bass.ds(b, 1), :].to_broadcast([P, AW])).then_inc(s_qb[1 - par], 16)
                        for j in range(PAGES):
                            n = b * PAGES + j
                            page = sp.value_load(table[0:1, bass.ds(n, 1)], min_val=0, max_val=A["cache_k"].shape[0] - 1)
                            sp.wait_ge(page_used, n + 1)
                            sp.dma_start(k_pg[j % Q_RING][:], A["cache_k"][bass.ds(page, 1), :, :].rearrange("a p n -> (a p) n")).then_inc(s_kp[j % Q_RING], 16)
                    sp.wait_ge(v_ready, T + 1)
                    sp.dma_start(O["v_all"][bass.ts(T, P), :], v_sb[:, bass.ds(T, 1), :].rearrange("p a n -> p (a n)")).then_inc(s_out, 16)
                    sp.wait_ge(qkn_ready, T + 1)
                    sp.dma_start(O["k_all"][bass.ts(T, P), :], qk_n[0 if first else 1][:, AW:2 * AW]).then_inc(s_k, 16)
                    if first:
                        sp.dma_start(q_dram, qk_n[0][0:NS, 0:AW]).then_inc(s_q, 16)
                        sp.wait_ge(u_ready, 1)
                        sp.dma_start(O["pool_sample"][:, STATE - 1, :], u_s[0:NS, :]).then_inc(s_out, 16)
                        sp.wait_ge(s_q, 16)

                tiles(sp, tile)
                n_out[0] += T_ALL + 1
                sp.wait_ge(u_ready, T_ALL)
                sp.dma_start(O["pool_prompt"], u_sb[1][P - STATE:P, :]).then_inc(s_out, 16)
                n_out[0] += 1
                sp.wait_ge(s_k, 16 * T_ALL)
                sp.wait_ge(s_out, 16 * n_out[0])

            @block.tensor
            def _(pe):
                pe.wait_ge(s_first, 32)

                def transpose_x(T, par, count):
                    pe.wait_ge(s_x[par], count)
                    for k in range(KD):
                        ins = pe.transpose(p_xt[:, k * P:(k + 1) * P], x_sb[par][:, k * P:(k + 1) * P], ident[:])
                    ins.then_inc(xt_done, 1)

                transpose_x(0, 0, 16)

                def tile(T, par, i=None):
                    first = isinstance(T, int) and T == 0
                    last = isinstance(T, int) and T == T_ALL - 1
                    pe.wait_ge(xT_ready, T + 1)
                    for n in range(4):
                        if n >= 2:
                            pe.wait_ge(zqk_ready, T * 2 + n - 1)
                        elif not first:
                            pe.wait_ge([v_ready, u_ready][n], T)
                        if first:
                            pe.wait_ge(s_win[n], 16)
                        for k in range(KD):
                            ins = pe.matmul(p_z[n % 2][:], xT[:, k, :], w_in[:, k, n * AW:(n + 1) * AW],
                                            start=(k == 0), stop=(k == KD - 1))
                        ins.then_inc(z_done, 1)
                    if not last:
                        nth = (T + 1) // 2 + 1 if isinstance(T, int) else (i + 2 if par else i + 2)
                        transpose_x(T + 1, 1 - par, nth * 16)
                    pe.wait_ge(u_ready, T + 1)
                    if first:
                        pe.wait_ge(s_const, 16 * N_CONST)
                    for g in range(NG):
                        cs = slice(g * PW, (g + 1) * PW)
                        if first:
                            lhs = [(st_sb, band_state[:, g, :]), (u_s, band_new[:, g, :])]
                        else:
                            if isinstance(T, int) or par == 0:
                                cur = band[:, g, V_CUR, :]
                            else:
                                cur = band[:, g, bass.ds(V_FIRST + (i > 0), 1), :].rearrange("p a n -> p (a n)")
                            lhs = [(u_sb[par], band[:, g, V_PREV, :]), (u_sb[1 - par], cur)]
                        for s, (left, mat) in enumerate(lhs):
                            ins = pe.matmul(p_pool[:, cs], left[:, cs], mat, start=(s == 0), stop=(s == 1))
                    ins.then_inc(pool_done, 1)
                    pe.wait_ge(qkn_ready, T + 1)
                    if not first:
                        pe.wait_ge(qT_ready, T)
                        pe.wait_ge(kT_ready, T)
                        for c in range(2 * AW // P):
                            ins = pe.transpose(p_qk[:, c * P:(c + 1) * P], qk_n[1][:, c * P:(c + 1) * P], ident[:])
                    else:
                        ins = pe.transpose(p_qk[:, 0:P], qk_n[0][:, 0:P], ident[:])
                    ins.then_inc(qkt_done, 1)
                    pe.wait_ge(pooledT_ready, T + 1)
                    if not first:
                        pe.wait_ge(mixp_ready, T)
                    for g in range(NG):
                        ins = pe.matmul(p_py[:, g * P:(g + 1) * P], w_pl[:, g, :], pooledT[:, g, :], start=True, stop=True)
                    ins.then_inc(py_done, 1)

                tiles(pe, tile)

            @block.scalar
            def _(act):
                act.wait_ge(s_first, 32)
                chain = chains["act"] = Chain(act, act_chain)

                def tile(T, par, i=None):
                    first = isinstance(T, int) and T == 0
                    nth = T // 2 + 1 if isinstance(T, int) else (i + 1 if par else i + 2)
                    act.wait_ge(s_x[par], nth * 16)
                    if not first:
                        act.wait_ge(ssx_ready, T)
                        act.wait_ge(var_ready, T)
                    act.activation(sq_act[:], x_sb[par][:], ACT.Square, accum_out=st1[:, 0:1]).then_inc(ssx_ready, 1)
                    act.wait_ge(var_ready, T + 1)
                    if not first:
                        act.wait_ge(rx_ready, T)
                    act.activation(st1[:, 2:3], st1[:, 1:2], ACT.Sqrt).then_inc(std_ready, 1)
                    act.wait_ge(rx_ready, T + 1)
                    if not first:
                        act.wait_ge(qkn_ready, T)
                    for n in range(2):
                        act.wait_ge(z_done, T * 4 + n + 1)
                        act.activation(z_qk[:, n * AW:(n + 1) * AW], p_z[n][:], ACT.Copy, scale=st1[:, 3:4]).then_inc(zqk_ready, 1)
                    act.wait_ge(var16, T + 1)
                    act.activation(st16[:, 1, :], st16[:, 0, :], ACT.Sqrt).then_inc(std16, 1)
                    act.wait_ge(pool_done, T + 1)
                    if not first:
                        act.wait_ge(py_done, T)
                    act.activation(pooledT[:].rearrange("p g n -> p (g n)"), p_pool[:], ACT.Copy).then_inc(pooledT_ready, 1)
                    act.wait_ge(qkt_done, T + 1)
                    if first:
                        act.sem_inc(qT_ready, 1)
                    else:
                        act.activation(qT[:, :, bass.ts(T - 1, P)], p_qk[:, 0:AW].rearrange("p (c n) -> p c n", n=P),
                                       ACT.Copy).then_inc(qT_ready, 1)
                    act.wait_ge(py_done, T + 1)
                    for g in range(NG):
                        ins = act.activation(mixp[:, g, bass.ts(T, P)], p_py[:, g * P:(g + 1) * P], ACT.Copy, scale=s_pool_c[:, g:g + 1])
                    ins.then_inc(mixp_ready, 1)

                tiles(act, tile)

            @block.vector
            def _(dve):
                chain = chains["dve"] = Chain(dve, dve_chain)
                dve.sem_inc(prod_used, 2)
                chain(dve.memset(u_sb[1][:], 0.0))
                chain(dve.memset(zd[:], 0.0))
                dve.wait_ge(s_first, 32)
                chain(dve.tensor_scalar(nb_c, pb_c, -1.0, None, ALU.mult))
                chain(dve.tensor_scalar(nbs_c, pbs_c, -1.0, None, ALU.mult))

                def copy_xT(T):
                    dve.wait_ge(xt_done, T + 1)
                    dve.tensor_tensor(out=xT[:], in0=p_xt[:].rearrange("p (k n) -> p k n", n=P),
                                      in1=g_mix_c.unsqueeze(2).to_broadcast([P, KD, P]), op=ALU.mult).then_inc(xT_ready, 1)

                copy_xT(0)

                def tile(T, par, i=None):
                    first = isinstance(T, int) and T == 0
                    last = isinstance(T, int) and T == T_ALL - 1
                    dve.wait_ge(ssx_ready, T + 1)
                    if not first:
                        dve.wait_ge(std_ready, T)
                    dve.tensor_scalar(st1[:, 1:2], st1[:, 0:1], 1.0 / D, EPS, ALU.mult, ALU.add).then_inc(var_ready, 1)
                    dve.wait_ge(std_ready, T + 1)
                    dve.wait_ge(v_ready, T) if not first else None
                    dve.reciprocal(st1[:, 3:4], st1[:, 2:3]).then_inc(rx_ready, 1)
                    dve.wait_ge(zqk_ready, T * 2 + 2)
                    chain(dve.tensor_tensor(out=sq[:], in0=z_qk[:], in1=z_qk[:], op=ALU.mult))
                    chain(dve.tensor_reduce(out=st16[:, 2, :], in_=sq[:].rearrange("p (h d) -> p h d", d=HD), axis=AX.X, op=ALU.add))
                    dve.tensor_scalar(st16[:, 0, :], st16[:, 2, :], 1.0 / HD, EPS, ALU.mult, ALU.add).then_inc(var16, 1)
                    dve.wait_ge(z_done, T * 4 + 3)
                    dve.wait_ge(rx_ready, T + 1)
                    dve.tensor_scalar(v_sb[:, bass.ds(T, 1), :].rearrange("p a n -> p (a n)"), p_z[0][:], st1[:, 3:4], None,
                                      ALU.mult).then_inc(v_ready, 1)
                    dve.wait_ge(std16, T + 1)
                    chain(dve.reciprocal(st16[:, 2, :], st16[:, 1, :]))
                    heads = lambda t: t[:].rearrange("p (h d) -> p h d", d=HD)
                    chain(dve.tensor_tensor(out=heads(sq), in0=heads(z_qk),
                                            in1=st16[:, 2, :].unsqueeze(2).to_broadcast([P, 16, HD]), op=ALU.mult))
                    out = qk_n[0 if first else 1]
                    if first:
                        dve.wait_ge(s_const, 16 * N_CONST)
                    if not first:
                        dve.wait_ge(s_k, T * 16)
                        dve.wait_ge(qkt_done, T)
                    for s in range(2):
                        ins = dve.tensor_tensor(out=out[:, s * AW:(s + 1) * AW].rearrange("p (h d) -> p h d", d=HD),
                                                in0=sq[:, s * AW:(s + 1) * AW].rearrange("p (h d) -> p h d", d=HD),
                                                in1=g_qk[:, s, :].unsqueeze(1).to_broadcast([P, H, HD]), op=ALU.mult)
                    ins.then_inc(qkn_ready, 1)
                    dve.wait_ge(z_done, T * 4 + 4)
                    if not first:
                        dve.wait_ge(pool_done, T)
                    dve.tensor_scalar((u_s if first else u_sb[1 - par])[:], p_z[1][:], st1[:, 3:4], None,
                                      ALU.mult).then_inc(u_ready, 1)
                    if not last:
                        copy_xT(T + 1)
                    dve.wait_ge(qkt_done, T + 1)
                    if first:
                        dve.sem_inc(kT_ready, 1)
                    else:
                        dve.tensor_copy(kT[:, :, bass.ts(T - 1, P)], p_qk[:, AW:2 * AW].rearrange("p (c n) -> p c n", n=P)).then_inc(kT_ready, 1)
                        for j in range(PAGES):
                            n = (T - 1) * PAGES + j
                            dve.wait_ge(prod_ready, n + 1)
                            dve.tensor_reduce(out=zd[:, j, bass.ds((T - 1) * H, H)],
                                              in_=prod[j % 2][:].rearrange("p (h d) -> p h d", d=HD),
                                              axis=AX.X, op=ALU.add).then_inc(prod_used, 1)

                tiles(dve, tile, chain, 2 * 4)

            @block.gpsimd
            def _(pool):
                pool.sem_inc(page_used, Q_RING)
                pool.sem_inc(qbc_used, 2)

                def sample(b, par, nth):
                    pool.wait_ge(s_qb[par], nth * 16)
                    for j in range(PAGES):
                        n = b * PAGES + j
                        pool.wait_ge(s_kp[j % Q_RING], (b * 2 + j // Q_RING + 1) * 16)
                        pool.wait_ge(prod_used, n + 1)
                        ins = pool.tensor_tensor(out=prod[j % 2][:], in0=k_pg[j % Q_RING][:], in1=q_bc[par][:], op=ALU.mult)
                        ins.then_inc(prod_ready, 1)
                        pool.wait_ge(prod_ready, n + 1)
                        pool.sem_inc(page_used, 1)
                    pool.sem_inc(qbc_used, 1)

                with pool.Fori(0, NS // 2) as i:
                    sample(i * 2, 0, i + 1)
                    sample(i * 2 + 1, 1, i + 1)
        p1.close()

        wk_hi, wk_lo = (sb(mid, f"decode_weights_T_{n}", [P, PAGES, NS * H], F32R) for n in ("hi", "lo"))
        p2 = ExitStack()
        keep = [sb(p2, f"keep{i}", [P, SEQ + 1]) for i in range(2)]
        beta = [sb(p2, f"beta{i}", [P, SEQ]) for i in range(2)]
        w_out = sb(p2, "w_out_sb", [P, KD, D])
        p_sc = [pb(p2, f"p_sc{i}", 2 * CHUNK) for i in range(2)]
        p_at = [pb(p2, f"p_at{i}") for i in range(2)]
        p_o = pb(p2, "p_o")
        p_w = pb(p2, "p_w")
        s_wout = sem("w_out_loaded")
        d_t, d_sig, d_a, d_b, d_c = sem("decode_z_T"), sem("decode_sigmoids"), sem("decode_a"), sem("decode_a_T"), sem("decode_copied")
        with nc.Block() as block:
            @block.sync
            def _(sp):
                sp.dma_start(w_out[:], A["w_out"].rearrange("(k p) n -> p k n", p=P)).then_inc(s_wout, 16)

            @block.tensor
            def _(pe):
                for j in range(PAGES):
                    ins = pe.transpose(p_sc[0][:, j * P:(j + 1) * P], zd[:, j, :], ident[:])
                ins.then_inc(d_t, 1)
                pe.wait_ge(d_a, 1)
                for j in range(PAGES):
                    ins = pe.transpose(p_sc[1][:, j * P:(j + 1) * P], beta[0][:, j * P:(j + 1) * P], ident[:])
                ins.then_inc(d_b, 1)

            @block.scalar
            def _(act):
                act.wait_ge(d_t, 1)
                act.activation(keep[0][:, 0:SEQ], p_sc[0][:], ACT.Sigmoid, bias=nbs_c, scale=-SCALE).then_inc(d_sig, 1)
                act.activation(beta[0][:], p_sc[0][:], ACT.Sigmoid, bias=pbs_c, scale=SCALE).then_inc(d_sig, 1)
                act.wait_ge(d_b, 1)
                act.activation(wk_hi[:], p_sc[1][:].rearrange("p (j n) -> p j n", n=P)[:, :, 0:NS * H], ACT.Copy).then_inc(d_c, 1)

            @block.vector
            def _(dve):
                chain = chains["dve"]
                chain.eng = dve
                for i in range(2):
                    chain(dve.memset(keep[i][:, SEQ:SEQ + 1], 1.0))
                dve.wait_ge(d_sig, 2)
                chain(dve.tensor_tensor_scan(out=keep[0][:, 0:SEQ][:, ::-1], data0=keep[0][:, 0:SEQ][:, ::-1], data1=keep[0][:, 0:SEQ][:, ::-1],
                                             initial=1.0, op0=ALU.mult, op1=ALU.bypass))
                dve.tensor_tensor(out=beta[0][:], in0=beta[0][:], in1=keep[0][:, 1:SEQ + 1], op=ALU.mult).then_inc(d_a, 1)
                dve.wait_ge(d_c, 1)
                dve.tensor_tensor(out=wk_lo[:], in0=p_sc[1][:].rearrange("p (j n) -> p j n", n=P)[:, :, 0:NS * H], in1=wk_hi[:],
                                  op=ALU.subtract).then_inc(d_c, 1)

        GRP = 4
        ident_b = sb(p2, "ident_bf16", [P, P], BF16)
        mask_b = sb(p2, "causal_mask", [P, P], BF16)
        mask_f = sb(p2, "causal_mask_f32", [P, P])
        bf16_ready = sem("bf16_constants")
        aT = [sb(p2, f"aT{i}", [P, GRP, P]) for i in range(4)]
        attn = [sb(p2, f"attn{i}", [P, AW]) for i in range(2)]
        mixT = sb(p2, "attn_mixed_T", [P, AW // P, P])
        mixT_s = sb(p2, "attn_mixed_T_samples", [P, AW // P, P])
        v_pg = [sb(p2, f"v_page{i}", [P, AW]) for i in range(V_RING)]
        v_hi, v_lo = ([sb(p2, f"v_page_{n}{i}", [P, AW], F32R) for i in range(3)] for n in ("hi", "lo"))
        w_dec = [sb(p2, f"decode_columns{i}", [P, PAGES, 2 * NS * H], F32R) for i in range(2)]
        sel = sb(p2, "row_to_sample", [P, NS])
        p_dec, head_mask, dec_m = p_sc[1][:, CHUNK:2 * CHUNK], beta[1][:, 0:CHUNK], keep[1][:, 0:CHUNK]
        x_r = [sb(p2, f"x_res{i}", [P, D]) for i in range(2)]
        h_sb = [sb(p2, f"h{i}", [P, D]) for i in range(2)]
        m_sb = [sb(p2, f"h_times_g{i}", [P, D]) for i in range(2)]
        hT = sb(p2, "hT", [P, KD, P])
        g_ffn = sb(p2, "g_ffn_sb", [P, D])

        sc_done, sig_done, a_done = sem("scores_done"), sem("sigmoids_done"), sem("weights_done")
        at_done, at_copied, o_done, attn_copied = sem("aT_done"), sem("aT_copied"), sem("heads_done"), sem("attn_copied")
        w_done, w_copied = sem("p_w_filled"), sem("p_w_copied")
        s_vp = [sem(f"v_page_loaded{i}") for i in range(V_RING)]
        vhi_ready, vlo_ready = sem("v_page_hi"), sem("v_page_lo")
        page_done, wdec_ready, decm_ready = sem("v_page_multiplied"), sem("decode_columns_ready"), sem("decode_masked")
        s_xr = [sem("x_res_loaded0"), sem("x_res_loaded1")]
        h_ss, m_ready, mixs_zero = sem("h_squares"), sem("h_times_g_ready"), sem("mixed_zeroed")
        s_hm = [sem("h_m_stored0"), sem("h_m_stored1")]
        s_c2 = sem("const2_loaded")

        jobs = [1, 2, 3, 4, 0, 5, 6, 7, 8]
        plan = [("split", p) for p in range(3)]
        plan += [("scores", 0), ("scores", 1)]
        pieces, next_page, next_split = [], 0, 3
        for t in range(1, T_ALL):
            if t >= 2:
                pieces += [(jobs.index(t - 1), k) for k in range(8)]
            if t == 5:
                pieces += [(jobs.index(0), k) for k in range(8)]
            for h in range(H):
                n = (t - 1) * H + h
                plan.append(("turn", n))
                if n + 2 < (T_ALL - 1) * H:
                    plan.append(("scores", n + 2))
                for _ in range(min(3 if t == 1 else 2, NS * PAGES - next_page)):
                    plan.append(("page", next_page))
                    next_page += 1
                while next_split < min(next_page + 3, NS * PAGES):
                    plan.append(("split", next_split))
                    next_split += 1
                if pieces:
                    plan.append(("piece", pieces.pop(0)))
                    if t >= 5 and plan[-1][1][1] in (1, 3):
                        plan.append(("piece", pieces.pop(0)))
                plan.append(("values", n))
                if n == 28:
                    assert next_page == NS * PAGES
                    plan.append(("mask", 0))
                if n == 29:
                    plan.append(("samples", 0))
            plan.append(("attn", t))
        assert not pieces
        plan += [("piece", (jobs.index(T_ALL - 1), k)) for k in range(8)]
        group_of, n_groups = {}, 0
        for what, arg in plan:
            if what == "turn":
                group_of[arg] = n_groups
                n_groups += (arg // H + 1 + GRP - 1) // GRP
            elif what == "samples":
                group_of["samples"] = n_groups
                n_groups += 1
        fills = {}
        for what, arg in plan:
            if what == "piece":
                j, k = arg
                name = {0: "mix", 2: "h0", 4: "h1", 5: "t0", 6: "t1", 7: "logits"}.get(k)
                if name and not (name == "mix" and jobs[j] == 0):
                    fills[j, name] = len(fills)

        def bank(j, name):
            if j == len(jobs) - 1 and name in ("h0", "h1", "t0", "t1"):
                i, half = {"h0": (0, 0), "h1": (0, 1), "t0": (1, 0), "t1": (1, 1)}[name]
                return p_sc[i][:, half * CHUNK:(half + 1) * CHUNK]
            return p_w[:]

        with nc.Block() as block:
            @block.sync
            def _(sp):
                sp.dma_start(mask_f[:], A["c_mask"]).then_inc(s_c2, 16)
                sp.dma_start(g_ffn[:], A["g_ffn_bc"]).then_inc(s_c2, 16)
                sp.dma_start(head_mask, A["c_head_mask"]).then_inc(s_c2, 16)
                sp.dma_start(sel[:], A["c_sel"]).then_inc(s_c2, 16)
                with sp.Fori(0, NS) as b:
                    for j in range(PAGES):
                        n = b * PAGES + j
                        page = sp.value_load(table[0:1, bass.ds(n, 1)], min_val=0, max_val=A["cache_v"].shape[0] - 1)
                        sp.wait_ge(vlo_ready, n + 1)
                        sp.dma_start(v_pg[j % V_RING][:], A["cache_v"][bass.ds(page, 1), :, :].rearrange("a p n -> (a p) n")).then_inc(s_vp[j % V_RING], 16)

            @block.gpsimd
            def _(pool):
                pool.memset(mixT_s[:], 0.0).then_inc(mixs_zero, 1)
                for j in range(2):
                    pool.dma_start(x_r[j][:], A["x_all"][bass.ts(jobs[j], P), :]).then_inc(s_xr[j], 16)
                for j, T in enumerate(jobs):
                    pool.wait_ge(m_ready, 2 * j + 2)
                    pool.wait_ge(h_ss, j + 1)
                    pool.dma_start(h_dram[T * P:(T + 1) * P, :], h_sb[j % 2][:]).then_inc(s_hm[j % 2], 16)
                    pool.dma_start(m_dram[T * P:(T + 1) * P, 0:D], m_sb[j % 2][:]).then_inc(s_hm[j % 2], 16)
                    if j + 2 < len(jobs):
                        pool.dma_start(x_r[j % 2][:], A["x_all"][bass.ts(jobs[j + 2], P), :]).then_inc(s_xr[j % 2], 16)
                pool.wait_ge(s_hm[0], 32 * 5)
                pool.wait_ge(s_hm[1], 32 * 4)

            @block.tensor
            def _(pe):
                pe.wait_ge(bf16_ready, 2)
                pe.wait_ge(s_wout, 16)
                for what, arg in plan:
                    if what == "scores":
                        t, h = arg // H + 1, arg % H
                        rows = slice(HD * (h % 2), HD * (h % 2) + HD)
                        if arg >= 2:
                            pe.wait_ge(sig_done, arg - 1)
                        N = t * P
                        for c in range(0, N, CHUNK):
                            w = min(CHUNK, N - c)
                            has_mask = c + w == N
                            ins = pe.matmul(p_sc[arg % 2][:, c:c + w], qT[rows, h // 2, (t - 1) * P:t * P],
                                            kT[rows, h // 2, c:c + w], start=True, stop=not has_mask)
                            if has_mask:
                                ins = pe.matmul(p_sc[arg % 2][:, N - P:N], ident_b[:], mask_b[:], start=False, stop=True)
                        ins.then_inc(sc_done, 1)
                    elif what == "turn":
                        t = arg // H + 1
                        pe.wait_ge(a_done, arg + 1)
                        g0 = group_of[arg]
                        for g in range((t + GRP - 1) // GRP):
                            if g0 + g >= 2:
                                pe.wait_ge(at_copied, g0 + g - 1)
                            for b in range(g * GRP, min(t, (g + 1) * GRP)):
                                ins = pe.transpose(p_at[(g0 + g) % 2][:, (b % GRP) * P:(b % GRP + 1) * P],
                                                   beta[arg % 2][:, SEQ - t * P + b * P:SEQ - t * P + (b + 1) * P], ident[:])
                            ins.then_inc(at_done, 1)
                    elif what == "values":
                        t, h = arg // H + 1, arg % H
                        g0 = group_of[arg]
                        if h == 0 and t >= 2:
                            pe.wait_ge(attn_copied, t - 1)
                        for g in range((t + GRP - 1) // GRP):
                            pe.wait_ge(at_copied, g0 + g + 1)
                            for b in range(g * GRP, min(t, (g + 1) * GRP)):
                                ins = pe.matmul(p_o[:, h * HD:(h + 1) * HD], aT[(g0 + g) % 4][:, b % GRP, :],
                                                v_sb[:, b + 1, h * HD:(h + 1) * HD], start=(b == 0), stop=(b == t - 1))
                        ins.then_inc(o_done, 1)
                    elif what == "page":
                        b, j = arg // PAGES, arg % PAGES
                        if j == 0:
                            pe.wait_ge(wdec_ready, b + 1)
                        pe.wait_ge(vlo_ready, V_RING + arg + 1)
                        pe.wait_ge(vhi_ready, arg + 1)
                        pe.matmul(p_dec, w_dec[b % 2][:, j, :], v_hi[arg % 3][:], start=(arg == 0), stop=False)
                        ins = pe.matmul(p_dec, w_dec[b % 2][:, j, :], v_lo[arg % 3][:], start=False, stop=(arg == NS * PAGES - 1))
                        ins.then_inc(page_done, 1)
                    elif what == "samples":
                        g = group_of["samples"]
                        pe.wait_ge(at_copied, g - 1)
                        pe.wait_ge(s_c2, 64)
                        pe.wait_ge(decm_ready, 1)
                        for c in range(AW // P):
                            ins = pe.matmul(p_at[g % 2][:, c * NS:(c + 1) * NS], dec_m[:, c * P:(c + 1) * P], sel[:], start=True, stop=True)
                        ins.then_inc(at_done, 1)
                    elif what == "piece":
                        j, k = arg
                        T = jobs[j]

                        def begin(name):
                            if fills[j, name] > 0 and not (j == len(jobs) - 1 and name in ("h1", "t0", "t1")):
                                pe.wait_ge(w_copied, fills[j, name])

                        if k == 0 and T > 0:
                            begin("mix")
                            pe.wait_ge(attn_copied, T)
                            for c in range(AW // P):
                                ins = pe.transpose(p_w[:, c * P:(c + 1) * P], attn[T % 2][:, c * P:(c + 1) * P], ident[:])
                            ins.then_inc(w_done, 1)
                        if k in (1, 2, 3, 4):
                            n = (k - 1) // 2
                            if k == 1:
                                begin("h0")
                                if T == 0:
                                    pe.wait_ge(at_copied, group_of["samples"] + 1)
                            if k == 3:
                                begin("h1")
                            for kk in range(4 * ((k - 1) % 2), 4 * ((k - 1) % 2) + 4):
                                if kk < 4:
                                    lhs = (mixT if T > 0 else mixT_s)[:, kk, :]
                                else:
                                    lhs = mixp[:, kk - 4, T * P:(T + 1) * P]
                                ins = pe.matmul(bank(j, f"h{n}"), lhs, w_out[:, kk, n * CHUNK:(n + 1) * CHUNK], start=(kk == 0), stop=(kk == 7))
                            if k in (2, 4):
                                ins.then_inc(w_done, 1)
                        if k in (5, 6):
                            begin(f"t{k - 5}")
                            pe.wait_ge(m_ready, 2 * j + k - 4)
                            for c in range(4):
                                kk = 4 * (k - 5) + c
                                ins = pe.transpose(bank(j, f"t{k - 5}")[:, c * P:(c + 1) * P], m_sb[j % 2][:, kk * P:(kk + 1) * P], ident[:])
                            ins.then_inc(w_done, 1)
                        if k == 7:
                            begin("logits")
                            for kk in range(KD):
                                ins = pe.matmul(p_w[:, 0:NR], hT[:, kk, :], w_rt[:, kk, :], start=(kk == 0), stop=(kk == KD - 1))
                            ins.then_inc(w_done, 1)

            @block.scalar
            def _(act):
                act.wait_ge(mixs_zero, 1)
                for what, arg in plan:
                    if what == "scores":
                        t, h = arg // H + 1, arg % H
                        N = t * P
                        act.wait_ge(sc_done, arg + 1)
                        if arg >= 2:
                            act.wait_ge(a_done, arg - 1)
                        act.activation(keep[arg % 2][:, SEQ - N:SEQ], p_sc[arg % 2][:, 0:N], ACT.Sigmoid, bias=nb_c[:, h:h + 1], scale=-SCALE)
                        act.activation(beta[arg % 2][:, SEQ - N:SEQ], p_sc[arg % 2][:, 0:N], ACT.Sigmoid, bias=pb_c[:, h:h + 1],
                                       scale=SCALE).then_inc(sig_done, 1)
                    elif what == "turn":
                        t = arg // H + 1
                        g0 = group_of[arg]
                        if arg >= 2:
                            act.wait_ge(o_done, arg - 1)
                        for g in range((t + GRP - 1) // GRP):
                            w = min(GRP, t - g * GRP)
                            act.wait_ge(at_done, g0 + g + 1)
                            act.activation(aT[(g0 + g) % 4][:, 0:w, :], p_at[(g0 + g) % 2][:, 0:w * P].rearrange("p (b n) -> p b n", n=P),
                                           ACT.Copy).then_inc(at_copied, 1)
                    elif what == "split":
                        act.wait_ge(s_vp[arg % V_RING], (arg // V_RING + 1) * 16)
                        if arg >= 3:
                            act.wait_ge(page_done, arg - 2)
                        act.activation(v_hi[arg % 3][:], v_pg[arg % V_RING][:], ACT.Copy).then_inc(vhi_ready, 1)
                    elif what == "samples":
                        g = group_of["samples"]
                        act.wait_ge(at_done, g + 1)
                        act.activation(mixT_s[:, :, 0:NS], p_at[g % 2][:, 0:AW // P * NS].rearrange("p (c b) -> p c b", b=NS),
                                       ACT.Copy).then_inc(at_copied, 1)
                    elif what == "attn":
                        act.wait_ge(o_done, arg * H)
                        if arg >= 3:
                            act.wait_ge(w_done, fills[jobs.index(arg - 2), "mix"] + 1)
                        act.activation(attn[arg % 2][:], p_o[:], ACT.Copy).then_inc(attn_copied, 1)
                    elif what == "piece":
                        j, k = arg
                        T = jobs[j]
                        if k == 0 and T > 0:
                            act.wait_ge(w_done, fills[j, "mix"] + 1)
                            act.activation(mixT[:].rearrange("p c n -> p (c n)"), p_w[:], ACT.Copy).then_inc(w_copied, 1)
                        if k == 5:
                            act.wait_ge(w_copied, fills[j, "h1"] + 1)
                            if j >= 1:
                                act.wait_ge(h_ss, j)
                            act.activation(x_r[j % 2][:], h_sb[j % 2][:], ACT.Square, accum_out=h_sq[:, T:T + 1]).then_inc(h_ss, 1)
            @block.vector
            def _(dve):
                chain = chains["dve"]
                chain.eng = dve
                dve.sem_inc(vlo_ready, V_RING)
                dve.wait_ge(s_c2, 64)
                dve.tensor_copy(ident_b[:], ident[:]).then_inc(bf16_ready, 1)
                dve.tensor_copy(mask_b[:], mask_f[:]).then_inc(bf16_ready, 1)
                dve.wait_ge(mixs_zero, 1)
                zero_cols = mixT_s[:, 0:1, 64:64 + H].to_broadcast([P, PAGES, H])
                for i in range(2):
                    for half in range(2):
                        chain(dve.tensor_copy(w_dec[i][:, 4 * half:4 * half + 4, :], mixT_s[:]))

                for what, arg in plan:
                    if what == "scores":
                        t = arg // H + 1
                        N = t * P
                        b = arg % 2
                        dve.wait_ge(sig_done, arg + 1)
                        chain(dve.tensor_tensor_scan(out=keep[b][:, SEQ - N:SEQ][:, ::-1], data0=keep[b][:, SEQ - N:SEQ][:, ::-1],
                                                     data1=keep[b][:, SEQ - N:SEQ][:, ::-1], initial=1.0, op0=ALU.mult, op1=ALU.bypass))
                        dve.tensor_tensor(out=beta[b][:, SEQ - N:SEQ], in0=beta[b][:, SEQ - N:SEQ], in1=keep[b][:, SEQ - N + 1:SEQ + 1],
                                          op=ALU.mult).then_inc(a_done, 1)
                    elif what == "split":
                        b, j = arg // PAGES, arg % PAGES
                        if j == 0:
                            if b >= 2:
                                dve.wait_ge(page_done, (b - 1) * PAGES)
                                for part in range(2):
                                    c0 = part * NS * H + (b - 2) * H
                                    chain(dve.tensor_copy(w_dec[b % 2][:, :, c0:c0 + H], zero_cols))
                            for part, w in enumerate((wk_hi, wk_lo)):
                                c0 = part * NS * H + b * H
                                chain(dve.tensor_copy(w_dec[b % 2][:, :, c0:c0 + H], w[:, :, b * H:(b + 1) * H]))
                            dve.sem_inc(wdec_ready, 1)
                        dve.wait_ge(vhi_ready, arg + 1)
                        dve.tensor_tensor(out=v_lo[arg % 3][:], in0=v_pg[arg % V_RING][:], in1=v_hi[arg % 3][:],
                                          op=ALU.subtract).then_inc(vlo_ready, 1)
                    elif what == "mask":
                        dve.wait_ge(page_done, NS * PAGES)
                        dve.tensor_tensor(out=dec_m, in0=p_dec, in1=head_mask, op=ALU.mult).then_inc(decm_ready, 1)
                    elif what == "piece":
                        j, k = arg
                        T = jobs[j]
                        if k in (2, 4):
                            n = (k - 2) // 2
                            cs = slice(n * CHUNK, (n + 1) * CHUNK)
                            dve.wait_ge(w_done, fills[j, f"h{n}"] + 1)
                            if n == 0:
                                dve.wait_ge(s_xr[j % 2], 16 * (j // 2 + 1))
                                if j >= 2:
                                    dve.wait_ge(s_hm[j % 2], 32 * (j // 2))
                            dve.tensor_tensor(out=h_sb[j % 2][:, cs], in0=bank(j, f"h{n}"), in1=x_r[j % 2][:, cs], op=ALU.add).then_inc(w_copied, 1)
                            dve.wait_ge(w_copied, fills[j, f"h{n}"] + 1)
                            dve.tensor_tensor(out=m_sb[j % 2][:, cs], in0=h_sb[j % 2][:, cs], in1=g_ffn[:, cs], op=ALU.mult).then_inc(m_ready, 1)
                        if k in (5, 6):
                            dve.wait_ge(w_done, fills[j, f"t{k - 5}"] + 1)
                            dve.tensor_copy(hT[:, 4 * (k - 5):4 * (k - 4), :].rearrange("p c n -> p (c n)"), bank(j, f"t{k - 5}")).then_inc(w_copied, 1)
                        if k == 7:
                            dve.wait_ge(w_done, fills[j, "logits"] + 1)
                            dve.tensor_copy(logits[:, T, :], p_w[:, 0:NR]).then_inc(w_copied, 1)
                dve.wait_ge(w_copied, len(fills))
        p2.close()
        mid.close()

        late = ctx.enter_context(ExitStack())
        w_pg = sb(late, "w_ple_gate_sb", [P, KD, D])
        w_pp = sb(late, "w_ple_proj_sb", [P, PLE // P, D])
        moe = ExitStack()
        m_idx = sb(moe, "m_row_of_slot", [P, N_BLK], I32)
        y_idx = sb(moe, "y_row_of_slot", [P, N_BLK], I32)
        over = sb(moe, "overflow_blocks", [P, 1 + N_OVER], I32)
        w_g = [sb(moe, f"w_gate{i}", [P, KD, F]) for i in range(2)]
        w_u = [sb(moe, f"w_up{i}", [P, KD, F]) for i in range(2)]
        w_d = [sb(moe, f"w_down{i}", [P, KF, D]) for i in range(2)]
        x_g = [sb(moe, f"x_gathered{i}", [P, MW]) for i in range(2)]
        s_wg = [sem("w_gate_loaded0"), sem("w_gate_loaded1")]
        s_wu = [sem("w_up_loaded0"), sem("w_up_loaded1")]
        s_wd = [sem("w_down_loaded0"), sem("w_down_loaded1")]
        xg_zero = sem("x_gathered_zeroed")

        def gate_rows(e):
            return A["w_gate"][e, :, :].rearrange("a (k p) n -> p (a k) n", p=P)

        def up_rows(e):
            return A["w_up"][e, :, :].rearrange("a (k p) n -> p (a k) n", p=P)

        def down_rows(e):
            return A["w_down"][e, :, :].rearrange("a (k p) n -> p (a k) n", p=P)

        p3 = ExitStack()
        T9 = T_ALL
        c3 = sb(p3, "routing_constants", [P, A["c_route"].shape[1]])
        iota128, iota_e, iota_b = c3[:, 0:128], c3[:, 128:160], c3[:, 160:160 + N_BLK]
        mult8 = c3[:, 208:216]
        valid = c3[:, 216:225]
        y_val, m_val = c3[:, 225:243].rearrange("p (a b) -> p a b", a=2), c3[:, 243:252]
        iota_o = c3[:, 252:252 + N_OVER]
        iota_b9 = c3[:, 0:EPG]
        tri_f = sb(p3, "tri_f32", [P, P])
        tri = sb(p3, "tri", [P, P], BF16)
        ones_b = sb(p3, "ones_bf16", [P, P], BF16)
        a_b = sb(p3, "assigned_bf16", [P, T9, E_ALL], BF16)
        r4 = [sb(p3, f"r4_{i}", [P, T9, EG]) for i in range(4)]
        r8 = [sb(p3, f"r8_{i}", [P, T9, EPG]) for i in range(4)]
        r32 = [sb(p3, f"r32_{i}", [P, T9, E_ALL]) for i in range(3)]
        oh = [sb(p3, f"onehot_e{i}", [P, T9, E_ALL]) for i in range(2)]
        s9 = sb(p3, "scalars9", [P, 24, T9])
        pre = sb(p3, "rank_before", [P, T9, E_ALL])
        tot = sb(p3, "totals", [P, 6, E_ALL])
        cmp8 = sb(p3, "compares8", [P, E_ALL, 8])
        cmp9 = sb(p3, "compares9", [P, T9, 8])
        cmp_o = sb(p3, "compares_o", [P, N_OVER, E_ALL])
        over_f = sb(p3, "overflow_f", [P, 1 + N_OVER])
        h_rs_rows = sb(p3, "h_rstd_columns", [P, T_ALL, MW - D])
        R = [sb(p3, f"row_onehot{i}", [P, P]) for i in range(4)]
        B = [sb(p3, f"block_onehot{i}", [P, 2, N_BLK]) for i in range(4)]
        tab = sb(p3, "slot_tables", [P, 2, 2, N_BLK])
        p_rank, p_tab = pb(p3, "p_rank"), pb(p3, "p_tab")
        s_c3, exp_in, exp_out, a_ready, rank_done = sem("const3_loaded"), sem("exp_wanted"), sem("exp_done"), sem("assigned"), sem("ranks_done")
        rs_in, rs_out, rs_ready, s_rs = sem("rstd_wanted"), sem("h_std"), sem("h_rstd_ready"), sem("h_rstd_stored")
        oh_ready, oh_used, tab_ready = sem("onehots_ready"), sem("onehots_used"), sem("tables_ready")

        with nc.Block() as block:
            @block.sync
            def _(sp):
                sp.dma_start(c3[:], A["c_route"]).then_inc(s_c3, 16)
                sp.dma_start(tri_f[:], A["c_tri"]).then_inc(s_c3, 16)
                sp.wait_ge(rs_ready, 2)
                with nc.allow_non_contiguous_dma(reason="the last 16 columns of each row"):
                    sp.dma_start(m_dram.rearrange("(t p) n -> p t n", p=P)[:, :, D:MW], h_rs_rows[:]).then_inc(s_rs, 16)
                for e in range(2):
                    sp.dma_start(w_g[e][:], gate_rows(slice(e, e + 1))).then_inc(s_wg[e], 16)
                    sp.dma_start(w_u[e][:], up_rows(slice(e, e + 1))).then_inc(s_wu[e], 16)
                    sp.dma_start(w_d[e][:], down_rows(slice(e, e + 1))).then_inc(s_wd[e], 16)
                sp.wait_ge(s_c3, 32)
                sp.wait_ge(s_rs, 16)

            @block.gpsimd
            def _(pool):
                pool.memset(x_g[0][:], 0.0).then_inc(xg_zero, 1)
                pool.memset(x_g[1][:], 0.0).then_inc(xg_zero, 1)

            @block.scalar
            def _(act):
                act.wait_ge(rs_in, 1)
                act.activation(h_rs[:, 1, :], h_rs[:, 0, :], ACT.Sqrt).then_inc(rs_out, 1)
                act.wait_ge(exp_in, 1)
                act.activation(r4[1][:], r4[0][:], ACT.Exp).then_inc(exp_out, 1)
                act.wait_ge(exp_in, 2)
                act.activation(s9[:, 5, :], s9[:, 4, :], ACT.Exp).then_inc(exp_out, 1)

            @block.tensor
            def _(pe):
                pe.wait_ge(a_ready, 1)
                for i in range(T9):
                    for j in range(i + 1):
                        pe.matmul(p_rank[:, i * E_ALL:(i + 1) * E_ALL], (tri if j == i else ones_b)[:], a_b[:, j, :],
                                  start=(j == 0), stop=(j == i))
                for j in range(T9):
                    ins = pe.matmul(p_rank[:, T9 * E_ALL:(T9 + 1) * E_ALL], ones_b[:], a_b[:, j, :], start=(j == 0), stop=(j == T9 - 1))
                ins.then_inc(rank_done, 1)
                for n in range(2 * T9):
                    pe.wait_ge(oh_ready, n + 1)
                    ins = pe.matmul(p_tab[:, 0:2 * N_BLK], R[n % 4][:], B[n % 4][:].rearrange("p a b -> p (a b)"),
                                    start=(n == 0), stop=(n == 2 * T9 - 1))
                    ins.then_inc(oh_used, 1)

            @block.vector
            def _(dve):
                chain = chains["dve"]
                chain.eng = dve
                dve.wait_ge(s_c3, 32)
                chain(dve.tensor_copy(tri[:], tri_f[:]))
                chain(dve.memset(ones_b[:], 1.0))
                V = dve

                def bc(ap, n):
                    return ap.unsqueeze(2).to_broadcast([P, T9, n])

                def tt(out, a, b, op):
                    chain(V.tensor_tensor(out=out, in0=a, in1=b, op=op))

                def ts(out, a, s1, s2, o1, o2=None):
                    if o2 is None:
                        chain(V.tensor_scalar(out, a, s1, None, o1))
                    else:
                        chain(V.tensor_scalar(out, a, s1, s2, o1, o2))

                def red(out, a, op):
                    chain(V.tensor_reduce(out=out, in_=a, axis=AX.X, op=op))

                def first_max(vals, n, top, idx, hot, tmp):
                    red(top, vals, ALU.max)
                    tt(tmp, vals, bc(top, n), ALU.is_equal)
                    ts(tmp, tmp, -64.0, 64.0, ALU.mult, ALU.add)
                    it = c3[:, 0:n].unsqueeze(1).to_broadcast([P, T9, n])
                    tt(tmp, tmp, it, ALU.add)
                    red(idx, tmp, ALU.min)
                    tt(hot, it, bc(idx, n), ALU.is_equal)

                V.tensor_scalar(h_rs[:, 0, :], h_sq[:], 1.0 / D, EPS, ALU.mult, ALU.add).then_inc(rs_in, 1)
                V.wait_ge(rs_out, 1)
                V.reciprocal(h_rs[:, 2, :], h_rs[:, 1, :]).then_inc(rs_ready, 1)
                V.wait_ge(rs_ready, 1)
                V.tensor_copy(h_rs_rows[:], bc(h_rs[:, 2, :], MW - D)).then_inc(rs_ready, 1)
                tt(logits[:], logits[:], bc(h_rs[:, 2, :], NR), ALU.mult)
                tt(logits[:], logits[:], b_rt[:].unsqueeze(1).to_broadcast([P, T9, NR]), ALU.add)
                Lg, Le = logits[:, :, 0:EG], logits[:, :, EG:NR]
                first_max(Lg, EG, s9[:, 0, :], s9[:, 1, :], r4[2][:], r4[3][:])
                V.tensor_tensor(out=r4[0][:], in0=Lg, in1=bc(s9[:, 0, :], EG), op=ALU.subtract).then_inc(exp_in, 1)
                tt(r32[0][:].rearrange("p t (g e) -> p t g e", g=EG), Le.rearrange("p t (g e) -> p t g e", g=EG),
                   r4[2][:].unsqueeze(3).to_broadcast([P, T9, EG, EPG]), ALU.mult)
                red(r8[0][:], r32[0][:].rearrange("p t (g e) -> p t e g", g=EG), ALU.add)
                first_max(r8[0][:], EPG, s9[:, 2, :], s9[:, 6, :], r8[1][:], r8[3][:])
                ts(r8[3][:], r8[1][:], -3.0e38, None, ALU.mult)
                tt(r8[2][:], r8[0][:], r8[3][:], ALU.add)
                first_max(r8[2][:], EPG, s9[:, 3, :], s9[:, 7, :], r8[1][:], r8[3][:])
                V.tensor_tensor(out=s9[:, 4, :], in0=s9[:, 3, :], in1=s9[:, 2, :], op=ALU.subtract).then_inc(exp_in, 1)
                iv = iota_e.unsqueeze(1).to_broadcast([P, T9, E_ALL])
                for c in range(2):
                    ts(s9[:, 8 + c, :], s9[:, 1, :], float(EPG), None, ALU.mult)
                    tt(s9[:, 8 + c, :], s9[:, 8 + c, :], s9[:, 6 + c, :], ALU.add)
                    tt(oh[c][:], iv, bc(s9[:, 8 + c, :], E_ALL), ALU.is_equal)
                    tt(oh[c][:], oh[c][:], bc(valid, E_ALL), ALU.mult)
                V.tensor_tensor(out=a_b[:], in0=oh[0][:], in1=oh[1][:], op=ALU.add).then_inc(a_ready, 1)
                V.wait_ge(exp_out, 2)
                red(s9[:, 10, :], r4[1][:], ALU.add)
                ts(s9[:, 11, :], s9[:, 5, :], 1.0, None, ALU.add)
                tt(s9[:, 10, :], s9[:, 10, :], s9[:, 11, :], ALU.mult)
                chain(V.reciprocal(gate_w[:, 0, :], s9[:, 10, :]))
                tt(gate_w[:, 1, :], gate_w[:, 0, :], s9[:, 5, :], ALU.mult)
                V.wait_ge(rank_done, 1)
                chain(V.tensor_copy(pre[:].rearrange("p t e -> p (t e)"), p_rank[:, 0:T9 * E_ALL]))
                chain(V.tensor_copy(tot[:, 0, :], p_rank[:, T9 * E_ALL:(T9 + 1) * E_ALL]))
                tt(cmp8[:], tot[:, 0, :].unsqueeze(2).to_broadcast([P, E_ALL, 8]), mult8.unsqueeze(1).to_broadcast([P, E_ALL, 8]), ALU.is_gt)
                red(tot[:, 1, :], cmp8[:], ALU.add)
                chain(V.tensor_tensor_scan(out=tot[:, 2, :], data0=tot[:, 1, :], data1=tot[:, 1, :], initial=0.0, op0=ALU.add, op1=ALU.bypass))
                tt(tot[:, 3, :], tot[:, 2, :], tot[:, 1, :], ALU.subtract)
                tt(cmp_o[:], tot[:, 2, :].unsqueeze(1).to_broadcast([P, N_OVER, E_ALL]), iota_o.unsqueeze(2).to_broadcast([P, N_OVER, E_ALL]), ALU.is_le)
                chain(V.tensor_copy(over_f[:, 0:1], tot[:, 2, E_ALL - 1:E_ALL]))
                red(over_f[:, 1:], cmp_o[:], ALU.add)
                ts(over_f[:, 1:], over_f[:, 1:], float(E_ALL - 1), None, ALU.min)
                chain(V.tensor_copy(over[:], over_f[:]))
                for c in range(2):
                    rank, base, rb, r, blk, isov = (s9[:, 12 + 6 * c + q, :] for q in range(6))
                    tt(r32[1][:], oh[c][:], pre[:], ALU.mult)
                    red(rank, r32[1][:], ALU.add)
                    tt(r32[2][:], oh[c][:], tot[:, 3, :].unsqueeze(1).to_broadcast([P, T9, E_ALL]), ALU.mult)
                    red(base, r32[2][:], ALU.add)
                    tt(cmp9[:], bc(rank, 8), mult8.unsqueeze(1).to_broadcast([P, T9, 8]), ALU.is_ge)
                    red(rb, cmp9[:], ALU.add)
                    ts(r, rb, -float(P), None, ALU.mult)
                    tt(r, r, rank, ALU.add)
                    ts(isov, rb, 1.0, None, ALU.min)
                    tt(blk, base, rb, ALU.add)
                    ts(blk, blk, float(E_ALL - 1), None, ALU.add)
                    tt(blk, blk, s9[:, 8 + c, :], ALU.subtract)
                    tt(blk, blk, isov, ALU.mult)
                    tt(blk, blk, s9[:, 8 + c, :], ALU.add)
                    ts(isov, valid, -999.0, 999.0, ALU.mult, ALU.add)
                    tt(blk, blk, isov, ALU.add)
                for t in range(T9):
                    for c in range(2):
                        n = 2 * t + c
                        r, blk = s9[:, 12 + 6 * c + 3, t:t + 1], s9[:, 12 + 6 * c + 4, t:t + 1]
                        if n >= 4:
                            V.wait_ge(oh_used, n - 3)
                        chain(V.tensor_scalar(R[n % 4][:], iota128, r, None, ALU.is_equal))
                        chain(V.tensor_scalar(B[n % 4][:, 0, :], iota_b, blk, y_val[:, c, t:t + 1], ALU.is_equal, ALU.mult))
                        V.tensor_scalar(B[n % 4][:, 1, :], iota_b, blk, m_val[:, t:t + 1], ALU.is_equal, ALU.mult).then_inc(oh_ready, 1)
                V.wait_ge(oh_used, 2 * T9)
                chain(V.tensor_copy(tab[:, 0, :, :].rearrange("p a b -> p (a b)"), p_tab[:, 0:2 * N_BLK]))
                ts(tab[:, 1, :, :], tab[:, 0, :, :], 0.0, NONE, ALU.is_equal, ALU.mult)
                tt(tab[:, 1, :, :], tab[:, 1, :, :], tab[:, 0, :, :], ALU.add)
                ts(tab[:, 1, :, :], tab[:, 1, :, :], -1.0, None, ALU.add)
                chain(V.tensor_copy(y_idx[:], tab[:, 1, 0, :]))
                chain(V.tensor_copy(m_idx[:], tab[:, 1, 1, :]))
        p3.close()

        s_ple = sem("ple_weights_loaded")
        p4 = ExitStack()
        NCH, RING = 12, 4
        idx_m = [sb(p4, f"idx_m{i}", [P, 1], I32) for i in range(2)]
        idx_y = [sb(p4, f"idx_y{i}", [P, 1], I32) for i in range(2)]
        w_hi = [sb(p4, f"w_hi{i}", [P, 2, CHUNK], F32R) for i in range(RING)]
        w_lo = [sb(p4, f"w_lo{i}", [P, 2, CHUNK], F32R) for i in range(RING)]
        x_hi = sb(p4, "xeT_hi", [P, KD, P], F32R)
        x_lo = sb(p4, "xeT_lo", [P, KD, P], F32R)
        act_g = sb(p4, "silu_gate", [P, F])
        hid = sb(p4, "hidden", [P, F])
        h_hi = sb(p4, "hiddenT_hi", [P, KF, P], F32R)
        h_lo = sb(p4, "hiddenT_lo", [P, KF, P], F32R)
        y_sb = [sb(p4, f"y{i}", [P, D]) for i in range(2)]
        p_xe = pb(p4, "p_xe", 2 * CHUNK)
        p_g, p_u, p_ht = pb(p4, "p_g"), pb(p4, "p_u"), pb(p4, "p_ht")
        p_y = pb(p4, "p_y", 2 * CHUNK)
        s_xg = [sem("x_gathered0"), sem("x_gathered1")]
        s_ys = [sem("y_scattered0"), sem("y_scattered1")]
        idx_ready, pool_held = sem("indices_copied"), sem("pool_waits_held")
        xe_t, xhi_ready, xlo_ready = sem("xe_transposed"), sem("xeT_hi_ready"), sem("xeT_lo_ready")
        hi_ready, lo_ready, chunk_used = sem("w_hi_ready"), sem("w_lo_ready"), sem("w_chunk_used")
        silu_ready, hid_ready = sem("silu_ready"), sem("hidden_ready")
        ht_done, hhi_ready, hlo_ready = sem("hidden_transposed"), sem("hiddenT_hi_ready"), sem("hiddenT_lo_ready")
        y_a, y_v = sem("y_copied_act"), sem("y_copied_dve")

        def chunk_of(c, par):
            if c < 8:
                w, s_w = (w_g, s_wg) if c < 4 else (w_u, s_wu)
                k = 2 * (c % 4)
                return w[par][:, k:k + 2, :], s_w[par]
            n, k = (c - 8) // 2, 2 * (c % 2)
            return w_d[par][:, k:k + 2, n * CHUNK:(n + 1) * CHUNK], s_wd[par]

        def split_hi(act, c, par, loaded, nth_chunk):
            raw, s_w = chunk_of(c, par)
            act.wait_ge(s_w, loaded)
            act.wait_ge(chunk_used, nth_chunk)
            act.activation(w_hi[c % RING][:], raw, ACT.Copy).then_inc(hi_ready, 1)

        def split_lo(dve, c, par, nth_chunk):
            raw, _ = chunk_of(c, par)
            dve.wait_ge(hi_ready, nth_chunk)
            dve.tensor_tensor(out=w_lo[c % RING][:], in0=raw, in1=w_hi[c % RING][:], op=ALU.subtract).then_inc(lo_ready, 1)

        def multiply(pe, c, nth_chunk, hi_ready=hi_ready, lo_ready=lo_ready, chunk_used=chunk_used):
            if c < 8:
                out, a_hi, a_lo, k0 = (p_g if c < 4 else p_u)[:], x_hi, x_lo, 2 * (c % 4)
                first, last = c % 4 == 0, c % 4 == 3
            else:
                n = (c - 8) // 2
                out, a_hi, a_lo, k0 = p_y[:, n * CHUNK:(n + 1) * CHUNK], h_hi, h_lo, 2 * (c % 2)
                first, last = c % 2 == 0, c % 2 == 1
            pe.wait_ge(hi_ready, nth_chunk)
            for k in range(2):
                pe.matmul(out, a_hi[:, k0 + k, :], w_hi[c % RING][:, k, :], start=(first and k == 0), stop=False)
                pe.matmul(out, a_lo[:, k0 + k, :], w_hi[c % RING][:, k, :], start=False, stop=False)
            pe.wait_ge(lo_ready, nth_chunk)
            for k in range(2):
                ins = pe.matmul(out, a_hi[:, k0 + k, :], w_lo[c % RING][:, k, :], start=False, stop=(last and k == 1))
            ins.then_inc(chunk_used, 1)

        def experts(eng, body):
            for e in range(3):
                body(e, e % 2, None)
            with eng.Fori(0, (E_ALL - 6) // 2) as i:
                body(i * 2 + 3, 1, i)
                body(i * 2 + 4, 0, i)
            for e in range(E_ALL - 3, E_ALL):
                body(e, e % 2, None)

        def turn(e, par, i):
            return e // 2 + 1 if i is None else (i + 2 if par else i + 3)

        def i_of_previous(e, par, i):
            return None if i is None else (i - 1 if par else i)

        with nc.Block() as block:
            @block.sync
            def _(sp):
                def expert(e, par, i):
                    if i is None and e + 2 >= E_ALL:
                        return
                    sl = slice(e + 2, e + 3) if i is None else bass.ds(e + 2, 1)
                    sp.wait_ge(lo_ready, e * NCH + 4)
                    sp.dma_start(w_g[par][:], gate_rows(sl)).then_inc(s_wg[par], 16)
                    sp.wait_ge(lo_ready, e * NCH + 8)
                    sp.dma_start(w_u[par][:], up_rows(sl)).then_inc(s_wu[par], 16)
                    sp.wait_ge(lo_ready, e * NCH + 12)
                    sp.dma_start(w_d[par][:], down_rows(sl)).then_inc(s_wd[par], 16)

                experts(sp, expert)
                sp.dma_start(w_pg[:], A["w_ple_gate"].rearrange("(k p) n -> p k n", p=P)).then_inc(s_ple, 16)
                sp.dma_start(w_pp[:], A["w_ple_proj"].rearrange("(k p) n -> p k n", p=P)).then_inc(s_ple, 16)

            @block.gpsimd
            def _(pool):
                def gather(e, par, nth_index):
                    pool.tensor_copy(idx_m[par][:], m_idx[:, bass.ds(e, 1)]).then_inc(idx_ready, 1)
                    pool.wait_ge(idx_ready, nth_index)
                    pool.sem_inc(pool_held, 1)
                    pool.indirect_dma_start(out=x_g[par][:], out_offset=None, in_=m_dram,
                                            in_offset=bass.IndirectOffsetOnAxis(ap=idx_m[par][:, 0:1], axis=0),
                                            bounds_check=ROWS - 1, oob_is_err=False).then_inc(s_xg[par], 16)

                pool.wait_ge(xg_zero, 2)
                gather(0, 0, 1)
                gather(1, 1, 2)

                def expert(e, par, i):
                    if i is not None or e + 2 < E_ALL:
                        pool.wait_ge(hid_ready, e + 1)
                        pool.sem_inc(pool_held, 1)
                        gather(e + 2, par, e * 2 + 3)
                    pool.wait_ge(y_a, e + 1)
                    pool.wait_ge(y_v, e + 1)
                    pool.sem_inc(pool_held, 1)
                    pool.tensor_copy(idx_y[par][:], y_idx[:, bass.ds(e, 1)]).then_inc(idx_ready, 1)
                    pool.wait_ge(idx_ready, e * 2 + 4 if i is not None or e < E_ALL - 2 else E_ALL + e + 1)
                    pool.sem_inc(pool_held, 1)
                    pool.indirect_dma_start(out=y_dram, out_offset=bass.IndirectOffsetOnAxis(ap=idx_y[par][:, 0:1], axis=0),
                                            in_=y_sb[par][:], in_offset=None,
                                            bounds_check=2 * ROWS - 1, oob_is_err=False).then_inc(s_ys[par], 16)

                experts(pool, expert)
                pool.wait_ge(s_ys[0], 16 * (E_ALL // 2))
                pool.wait_ge(s_ys[1], 16 * (E_ALL // 2))

            @block.tensor
            def _(pe):
                pe.sem_inc(chunk_used, RING)

                def transpose_x(par, nth):
                    pe.wait_ge(s_xg[par], nth * 16)
                    for k in range(KD):
                        ins = pe.transpose(p_xe[:, k * P:(k + 1) * P], x_g[par][:, k * P:(k + 1) * P], ident[:])
                    ins.then_inc(xe_t, 1)

                transpose_x(0, 1)

                def expert(e, par, i):
                    last = i is None and e == E_ALL - 1
                    pe.wait_ge(xlo_ready, e + 1)
                    for c in range(8):
                        multiply(pe, c, e * NCH + c + 1)
                    if not last:
                        transpose_x(1 - par, (turn(e, par, i) + (0 if par == 0 else 1)))
                    pe.wait_ge(hid_ready, e + 1)
                    for c in range(KF):
                        ins = pe.transpose(p_ht[:, c * P:(c + 1) * P], hid[:, c * P:(c + 1) * P], ident[:])
                    ins.then_inc(ht_done, 1)
                    pe.wait_ge(hlo_ready, e + 1)
                    if not (i is None and e == 0):
                        pe.wait_ge(y_a, e)
                        pe.wait_ge(y_v, e)
                    for c in range(8, NCH):
                        multiply(pe, c, e * NCH + c + 1)

                experts(pe, expert)

            def free_y(eng, e, par, i):
                if not (i is None and e < 2):
                    eng.wait_ge(s_ys[par], (turn(e, par, i) - 1) * 16)

            @block.scalar
            def _(act):
                def copy_x(e):
                    act.wait_ge(xe_t, e + 1)
                    act.activation(x_hi[:].rearrange("p k n -> p (k n)"), p_xe[:], ACT.Copy).then_inc(xhi_ready, 1)

                def copy_y(e, par, i):
                    act.wait_ge(chunk_used, e * NCH + NCH + RING)
                    free_y(act, e, par, i)
                    act.activation(y_sb[par][:, 0:CHUNK], p_y[:, 0:CHUNK], ACT.Copy).then_inc(y_a, 1)

                copy_x(0)

                def expert(e, par, i):
                    first, last = (i is None and e == 0), (i is None and e == E_ALL - 1)
                    loaded = turn(e, par, i) * 16
                    for c in range(8):
                        split_hi(act, c, par, loaded, e * NCH + c + 1)
                        if c == 3 and not first:
                            copy_y(e - 1, 1 - par, i_of_previous(e, par, i))
                    if not first:
                        act.wait_ge(hid_ready, e)
                    act.activation(act_g[:], p_g[:], ACT.Silu, scale=x_g[par][:, D:D + 1]).then_inc(silu_ready, 1)
                    for c in range(8, NCH):
                        split_hi(act, c, par, loaded, e * NCH + c + 1)
                    act.wait_ge(ht_done, e + 1)
                    act.activation(h_hi[:].rearrange("p k n -> p (k n)"), p_ht[:], ACT.Copy).then_inc(hhi_ready, 1)
                    if not last:
                        copy_x(e + 1)
                    else:
                        copy_y(e, par, None)

                experts(act, expert)

            @block.vector
            def _(dve):
                def copy_x(e):
                    dve.wait_ge(xhi_ready, e + 1)
                    dve.tensor_tensor(out=x_lo[:].rearrange("p k n -> p (k n)"), in0=p_xe[:], in1=x_hi[:].rearrange("p k n -> p (k n)"),
                                      op=ALU.subtract).then_inc(xlo_ready, 1)

                def copy_y(e, par, i):
                    dve.wait_ge(chunk_used, e * NCH + NCH + RING)
                    free_y(dve, e, par, i)
                    dve.tensor_copy(y_sb[par][:, CHUNK:2 * CHUNK], p_y[:, CHUNK:2 * CHUNK]).then_inc(y_v, 1)

                copy_x(0)

                def expert(e, par, i):
                    first, last = (i is None and e == 0), (i is None and e == E_ALL - 1)
                    for c in range(NCH - 1):
                        split_lo(dve, c, par, e * NCH + c + 1)
                        if c == 3 and not first:
                            copy_y(e - 1, 1 - par, i_of_previous(e, par, i))
                    dve.wait_ge(silu_ready, e + 1)
                    dve.wait_ge(chunk_used, e * NCH + 8 + RING)
                    if not first:
                        dve.wait_ge(ht_done, e)
                    dve.scalar_tensor_tensor(out=hid[:], in0=p_u[:], scalar=x_g[par][:, D:D + 1], in1=act_g[:],
                                             op0=ALU.mult, op1=ALU.mult).then_inc(hid_ready, 1)
                    split_lo(dve, NCH - 1, par, e * NCH + NCH)
                    dve.wait_ge(hhi_ready, e + 1)
                    dve.tensor_tensor(out=h_lo[:].rearrange("p k n -> p (k n)"), in0=p_ht[:], in1=h_hi[:].rearrange("p k n -> p (k n)"),
                                      op=ALU.subtract).then_inc(hlo_ready, 1)
                    if not last:
                        copy_x(e + 1)
                    else:
                        copy_y(e, par, None)

                experts(dve, expert)

        v_w, v_x, v_y = sem("over_weights"), sem("over_gathered"), sem("over_scattered")
        v_i, v_free, v_xt, v_xh, v_xl = (sem("over_indices"), sem("over_turn_free"), sem("over_x_T"), sem("over_xT_hi"),
                                         sem("over_xT_lo"))
        v_wh, v_wl, v_used = sem("over_w_hi"), sem("over_w_lo"), sem("over_chunk_used")
        v_s, v_h, v_ht, v_hh, v_hl, v_yc = (sem("over_silu"), sem("over_hidden"), sem("over_hidden_T"),
                                            sem("over_hiddenT_hi"), sem("over_hiddenT_lo"), sem("over_y_copied"))

        def over_multiply(pe, c, nth_chunk):
            multiply(pe, c, nth_chunk, v_wh, v_wl, v_used)

        with nc.Block() as block:
            def turns(eng, body, extra=None):
                n = eng.value_load(over[0:1, 0:1], min_val=0, max_val=N_OVER)
                with eng.If(n > 0):
                    with eng.Fori(0, n) as v:
                        body(v)
                        if extra:
                            extra(v)

            @block.sync
            def _(sp):
                def body(v):
                    sp.wait_ge(v_free, v + 1)
                    e = sp.value_load(over[0:1, bass.ds(v + 1, 1)], min_val=0, max_val=E_ALL - 1)
                    sp.dma_start(w_g[0][:], gate_rows(bass.ds(e, 1))).then_inc(v_w, 16)
                    sp.dma_start(w_u[0][:], up_rows(bass.ds(e, 1))).then_inc(v_w, 16)
                    sp.dma_start(w_d[0][:], down_rows(bass.ds(e, 1))).then_inc(v_w, 16)
                turns(sp, body)

            @block.gpsimd
            def _(pool):
                pool.sem_inc(v_free, 1)
                pool.sem_inc(v_used, RING)

                def body(v):
                    pool.tensor_copy(idx_m[0][:], m_idx[:, bass.ds(v + E_ALL, 1)]).then_inc(v_i, 1)
                    pool.tensor_copy(idx_y[0][:], y_idx[:, bass.ds(v + E_ALL, 1)]).then_inc(v_i, 1)
                    pool.wait_ge(v_i, v * 2 + 2)
                    pool.sem_inc(pool_held, 1)
                    pool.indirect_dma_start(out=x_g[0][:], out_offset=None, in_=m_dram,
                                            in_offset=bass.IndirectOffsetOnAxis(ap=idx_m[0][:, 0:1], axis=0),
                                            bounds_check=ROWS - 1, oob_is_err=False).then_inc(v_x, 16)
                    pool.wait_ge(v_yc, v + 1)
                    pool.sem_inc(pool_held, 1)
                    pool.indirect_dma_start(out=y_dram, out_offset=bass.IndirectOffsetOnAxis(ap=idx_y[0][:, 0:1], axis=0),
                                            in_=y_sb[0][:], in_offset=None,
                                            bounds_check=2 * ROWS - 1, oob_is_err=False).then_inc(v_y, 16)
                    pool.wait_ge(v_y, v * 16 + 16)
                    pool.sem_inc(v_free, 1)
                turns(pool, body)

            @block.tensor
            def _(pe):
                def body(v):
                    pe.wait_ge(v_x, v * 16 + 16)
                    for k in range(KD):
                        ins = pe.transpose(p_xe[:, k * P:(k + 1) * P], x_g[0][:, k * P:(k + 1) * P], ident[:])
                    ins.then_inc(v_xt, 1)
                    pe.wait_ge(v_xl, v + 1)
                    for c in range(8):
                        over_multiply(pe, c, v * NCH + c + 1)
                    pe.wait_ge(v_h, v + 1)
                    for c in range(KF):
                        ins = pe.transpose(p_ht[:, c * P:(c + 1) * P], hid[:, c * P:(c + 1) * P], ident[:])
                    ins.then_inc(v_ht, 1)
                    pe.wait_ge(v_hl, v + 1)
                    for c in range(8, NCH):
                        over_multiply(pe, c, v * NCH + c + 1)
                turns(pe, body)

            @block.scalar
            def _(act):
                def body(v):
                    act.wait_ge(v_xt, v + 1)
                    act.activation(x_hi[:].rearrange("p k n -> p (k n)"), p_xe[:], ACT.Copy).then_inc(v_xh, 1)
                    act.wait_ge(v_w, v * 48 + 48)
                    for c in range(8):
                        act.wait_ge(v_used, v * NCH + c + 1)
                        act.activation(w_hi[c % RING][:], chunk_of(c, 0)[0], ACT.Copy).then_inc(v_wh, 1)
                    act.activation(act_g[:], p_g[:], ACT.Silu, scale=x_g[0][:, D:D + 1]).then_inc(v_s, 1)
                    for c in range(8, NCH):
                        act.wait_ge(v_used, v * NCH + c + 1)
                        act.activation(w_hi[c % RING][:], chunk_of(c, 0)[0], ACT.Copy).then_inc(v_wh, 1)
                    act.wait_ge(v_ht, v + 1)
                    act.activation(h_hi[:].rearrange("p k n -> p (k n)"), p_ht[:], ACT.Copy).then_inc(v_hh, 1)
                turns(act, body)

            @block.vector
            def _(dve):
                def body(v):
                    dve.wait_ge(v_xh, v + 1)
                    dve.tensor_tensor(out=x_lo[:].rearrange("p k n -> p (k n)"), in0=p_xe[:], in1=x_hi[:].rearrange("p k n -> p (k n)"),
                                      op=ALU.subtract).then_inc(v_xl, 1)
                    for c in range(NCH):
                        dve.wait_ge(v_wh, v * NCH + c + 1)
                        dve.tensor_tensor(out=w_lo[c % RING][:], in0=chunk_of(c, 0)[0], in1=w_hi[c % RING][:], op=ALU.subtract).then_inc(v_wl, 1)
                        if c == NCH - 1:
                            dve.wait_ge(v_s, v + 1)
                            dve.scalar_tensor_tensor(out=hid[:], in0=p_u[:], scalar=x_g[0][:, D:D + 1], in1=act_g[:],
                                                     op0=ALU.mult, op1=ALU.mult).then_inc(v_h, 1)
                    dve.wait_ge(v_hh, v + 1)
                    dve.tensor_tensor(out=h_lo[:].rearrange("p k n -> p (k n)"), in0=p_ht[:], in1=h_hi[:].rearrange("p k n -> p (k n)"),
                                      op=ALU.subtract).then_inc(v_hl, 1)
                    dve.wait_ge(v_used, v * NCH + NCH + RING)
                    dve.tensor_copy(y_sb[0][:], p_y[:]).then_inc(v_yc, 1)
                turns(dve, body)
        p4.close()
        moe.close()

        p5 = ExitStack()
        wg_hi, wg_lo = (sb(p5, f"w_ple_gate_{n}", [P, KD, D], F32R) for n in ("hi", "lo"))
        wp_hi, wp_lo = (sb(p5, f"w_ple_proj_{n}", [P, PLE // P, D], F32R) for n in ("hi", "lo"))
        h_l = [sb(p5, f"h_loaded{i}", [P, D]) for i in range(2)]
        y_l = [sb(p5, f"y_loaded{i}", [P, 2, D]) for i in range(2)]
        pl = [sb(p5, f"ple_in{i}", [P, PLE]) for i in range(2)]
        h2 = [sb(p5, f"h2_{i}", [P, D]) for i in range(2)]
        n_hi, n_lo = ([sb(p5, f"h2_T_{n}{i}", [P, KD, P], F32R) for i in range(2)] for n in ("hi", "lo"))
        pl_hi, pl_lo = ([sb(p5, f"ple_T_{n}{i}", [P, PLE // P, P], F32R) for i in range(2)] for n in ("hi", "lo"))
        sg = sb(p5, "sigmoid_gate", [P, D])
        o5 = [sb(p5, f"out{i}", [P, D]) for i in range(2)]
        junk5 = sb(p5, "squares_of_h2", [P, D], BF16)
        st5 = [sb(p5, f"stats5_{i}", [P, 4]) for i in range(2)]
        p_nt = pb(p5, "p_nt", 2 * CHUNK)
        p_plt = pb(p5, "p_plt")
        p_gt = pb(p5, "p_gt", 2 * CHUNK)
        p_pp = pb(p5, "p_pp", 2 * CHUNK)
        s_l = [sem("tile_loaded0"), sem("tile_loaded1")]
        y0_zero, h2a, h2_ready = sem("y_rows_zeroed"), sem("h_plus_first"), sem("h2_ready")
        nt_done, nhi_ready, nlo_ready = sem("h2_transposed"), sem("h2_T_hi"), sem("h2_T_lo")
        plhi_ready, pllo_ready = sem("ple_T_hi"), sem("ple_T_lo")
        whi_ready, wlo_ready = sem("ple_w_hi"), sem("ple_w_lo")
        gt_done, ss5, var5, std5, r5 = sem("ple_products_done"), sem("h2_squares"), sem("h2_var"), sem("h2_std"), sem("h2_rstd")
        sg_ready, gp_ready, o_ready = sem("sigmoid_ready"), sem("gated_ready"), sem("out_ready")
        s_o = [sem("out_stored0"), sem("out_stored1")]
        KB = KD + PLE // P

        def weight(n, k):
            cs = slice(n * CHUNK, (n + 1) * CHUNK)
            if k < KD:
                return w_pg[:, k, cs], wg_hi[:, k, cs], wg_lo[:, k, cs], g_ple_c[:, k:k + 1]
            return w_pp[:, k - KD, cs], wp_hi[:, k - KD, cs], wp_lo[:, k - KD, cs], None

        def loads(T, i, par):
            return T // 2 + 1 if i is None else (i + 1 if par else i + 2)

        with nc.Block() as block:
            @block.sync
            def _(sp):
                def load(T, par):
                    rows = bass.ts(T, P)
                    sp.dma_start(h_l[par][:], h_dram[rows, :]).then_inc(s_l[par], 16)
                    sp.dma_start(pl[par][:], A["p_all"][rows, :]).then_inc(s_l[par], 16)
                    sp.dma_start(y_l[par][:], y_dram.rearrange("(t c) n -> t c n", c=2)[rows, :, :]).then_inc(s_l[par], 16)

                sp.dma_start(h_l[0][:], h_dram[0:P, :]).then_inc(s_l[0], 16)
                sp.dma_start(pl[0][:], A["p_all"][0:P, :]).then_inc(s_l[0], 16)
                sp.wait_ge(y0_zero, 1)
                sp.dma_start(y_l[0][0:NS, :, :], y_dram.rearrange("(t c) n -> t c n", c=2)[0:NS, :, :]).then_inc(s_l[0], 16)
                load(1, 1)

                def tile(T, par, i=None):
                    if i is not None or T + 2 < T_ALL:
                        sp.wait_ge(nt_done, T + 1)
                        load(T + 2, par)
                    sp.wait_ge(o_ready, T * 2 + 2)
                    sp.dma_start(O["y_all"][bass.ts(T, P), :], o5[par][:]).then_inc(s_o[par], 16)

                tiles(sp, tile)
                sp.wait_ge(s_o[0], 16 * 6)
                sp.wait_ge(s_o[1], 16 * 5)

            @block.tensor
            def _(pe):
                def transposes(T, par):
                    pe.wait_ge(h2_ready, T + 1)
                    for k in range(KD):
                        pe.transpose(p_nt[:, k * P:(k + 1) * P], h2[par][:, k * P:(k + 1) * P], ident[:])
                    for k in range(PLE // P):
                        ins = pe.transpose(p_plt[:, k * P:(k + 1) * P], pl[par][:, k * P:(k + 1) * P], ident[:])
                    ins.then_inc(nt_done, 1)

                transposes(0, 0)

                def tile(T, par, i=None):
                    first = isinstance(T, int) and T == 0
                    pe.wait_ge(plhi_ready, T + 1)
                    pe.wait_ge(pllo_ready, T + 1)
                    pe.wait_ge(nhi_ready, T + 1)
                    pe.wait_ge(nlo_ready, T + 1)
                    for n in range(2):
                        cs = slice(n * CHUNK, (n + 1) * CHUNK)
                        if not first:
                            pe.wait_ge(gp_ready, T * 2 - 1 + n)
                        for k in range(KB):
                            _, w_h, w_l, _ = weight(n, k)
                            gate = k < KD
                            out = (p_gt if gate else p_pp)[:, cs]
                            x_h, x_l = (n_hi[par][:, k, :], n_lo[par][:, k, :]) if gate else (pl_hi[par][:, k - KD, :], pl_lo[par][:, k - KD, :])
                            if first:
                                pe.wait_ge(wlo_ready, n * KB + k + 1)
                            pe.matmul(out, x_h, w_h, start=k in (0, KD), stop=False)
                            pe.matmul(out, x_h, w_l, start=False, stop=False)
                            ins = pe.matmul(out, x_l, w_h, start=False, stop=k in (KD - 1, KB - 1))
                        ins.then_inc(gt_done, 1)
                        if n == 0 and (i is not None or T + 1 < T_ALL):
                            transposes(T + 1, 1 - par)

                tiles(pe, tile)

            @block.scalar
            def _(act):
                act.wait_ge(s_ple, 32)

                def split_hi(n):
                    for k in range(KB):
                        raw, w_h, _, g = weight(n, k)
                        act.activation(w_h, raw, ACT.Copy, scale=1.0 if g is None else g).then_inc(whi_ready, 1)

                def stats(T, par):
                    act.wait_ge(h2_ready, T + 1)
                    if not (isinstance(T, int) and T == 0):
                        act.wait_ge(ss5, T)
                    act.activation(junk5[:], h2[par][:], ACT.Square, accum_out=st5[par][:, 0:1]).then_inc(ss5, 1)
                    act.wait_ge(nt_done, T + 1)
                    act.activation(n_hi[par][:].rearrange("p k n -> p (k n)"), p_nt[:], ACT.Copy).then_inc(nhi_ready, 1)
                    act.activation(pl_hi[par][:].rearrange("p k n -> p (k n)"), p_plt[:, 0:PLE], ACT.Copy).then_inc(plhi_ready, 1)
                    act.wait_ge(var5, T + 1)
                    act.activation(st5[par][:, 2:3], st5[par][:, 1:2], ACT.Sqrt).then_inc(std5, 1)

                split_hi(0)
                stats(0, 0)
                split_hi(1)

                def tile(T, par, i=None):
                    if i is not None or T + 1 < T_ALL:
                        stats(T + 1, 1 - par)
                    act.wait_ge(r5, T + 1)
                    for n in range(2):
                        cs = slice(n * CHUNK, (n + 1) * CHUNK)
                        act.wait_ge(gt_done, T * 2 + n + 1)
                        if not (isinstance(T, int) and T == 0):
                            act.wait_ge(gp_ready, T * 2 - 1 + n)
                        act.activation(sg[:, cs], p_gt[:, cs], ACT.Sigmoid, scale=st5[par][:, 3:4]).then_inc(sg_ready, 1)

                tiles(act, tile)

            @block.vector
            def _(dve):
                dve.memset(y_l[0][:], 0.0).then_inc(y0_zero, 1)
                for par in range(2):
                    dve.sem_inc(s_o[par], 16)

                def split_lo(n):
                    for k in range(KB):
                        raw, w_h, w_l, g = weight(n, k)
                        dve.wait_ge(whi_ready, n * KB + k + 1)
                        if g is None:
                            dve.tensor_tensor(out=w_l, in0=raw, in1=w_h, op=ALU.subtract).then_inc(wlo_ready, 1)
                        else:
                            dve.scalar_tensor_tensor(out=w_l, in0=raw, scalar=g, in1=w_h, op0=ALU.mult, op1=ALU.subtract).then_inc(wlo_ready, 1)

                def combine(T, par, nth):
                    dve.wait_ge(s_l[par], 48 * nth)
                    if not (isinstance(T, int) and T < 2):
                        dve.wait_ge(o_ready, T * 2 - 2)
                    dve.scalar_tensor_tensor(out=h2[par][:], in0=y_l[par][:, 0, :], scalar=gate_w[:, 0, bass.ds(T, 1)], in1=h_l[par][:],
                                             op0=ALU.mult, op1=ALU.add).then_inc(h2a, 1)
                    dve.wait_ge(h2a, T + 1)
                    dve.scalar_tensor_tensor(out=h2[par][:], in0=y_l[par][:, 1, :], scalar=gate_w[:, 1, bass.ds(T, 1)], in1=h2[par][:],
                                             op0=ALU.mult, op1=ALU.add).then_inc(h2_ready, 1)

                def norm(T, par):
                    dve.wait_ge(ss5, T + 1)
                    dve.tensor_scalar(st5[par][:, 1:2], st5[par][:, 0:1], 1.0 / D, EPS, ALU.mult, ALU.add).then_inc(var5, 1)
                    dve.wait_ge(nhi_ready, T + 1)
                    dve.tensor_tensor(out=n_lo[par][:].rearrange("p k n -> p (k n)"), in0=p_nt[:], in1=n_hi[par][:].rearrange("p k n -> p (k n)"),
                                      op=ALU.subtract).then_inc(nlo_ready, 1)
                    dve.wait_ge(plhi_ready, T + 1)
                    dve.tensor_tensor(out=pl_lo[par][:].rearrange("p k n -> p (k n)"), in0=p_plt[:, 0:PLE],
                                      in1=pl_hi[par][:].rearrange("p k n -> p (k n)"), op=ALU.subtract).then_inc(pllo_ready, 1)
                    dve.wait_ge(std5, T + 1)
                    dve.reciprocal(st5[par][:, 3:4], st5[par][:, 2:3]).then_inc(r5, 1)

                split_lo(0)
                combine(0, 0, 1)
                norm(0, 0)
                split_lo(1)

                def tile(T, par, i=None):
                    if i is not None or T + 1 < T_ALL:
                        combine(T + 1, 1 - par, (T + 1) // 2 + 1 if i is None else i + 2)
                        norm(T + 1, 1 - par)
                    dve.wait_ge(s_o[par], loads(T, i, par) * 16)
                    for n in range(2):
                        cs = slice(n * CHUNK, (n + 1) * CHUNK)
                        dve.wait_ge(sg_ready, T * 2 + n + 1)
                        dve.tensor_tensor(out=o5[par][:, cs], in0=sg[:, cs], in1=p_pp[:, cs], op=ALU.mult).then_inc(gp_ready, 1)
                        dve.wait_ge(gp_ready, T * 2 + n + 1)
                        dve.tensor_tensor(out=o5[par][:, cs], in0=o5[par][:, cs], in1=h2[par][:, cs], op=ALU.add).then_inc(o_ready, 1)

                tiles(dve, tile)
        p5.close()
        late.close()


def constants():
    t = np.arange(P)
    band = np.zeros((P, NG, 5, P), np.float32)
    for g, w in enumerate(WINDOWS):
        s_, t_ = t[:, None], t[None, :]
        inside = (s_ <= t_) & (t_ - s_ < w)
        same = (s_ == t_).astype(np.float32)
        band[:, g, V_PREV] = (t_ + P - s_ < w) / w
        band[:, g, V_FIRST] = inside / np.minimum(t_ + 1, w) - same
        band[:, g, V_CUR] = inside / w - same
        for b in range(NS):
            for r in range(STATE):
                band[b * STATE + r, g, V_STATE, b] = (r >= STATE - (w - 1)) / w
            band[b, g, V_NEW, b] = 1.0 / w - 1.0
    r, c = np.arange(P)[:, None], np.arange(AW)[None, :]
    head_mask = (c // HD == r % H).astype(np.float32)
    sel = (r // H % NS == np.arange(NS)[None, :]).astype(np.float32)
    route = np.zeros((P, 272), np.float32)
    route[:, 0:128] = t
    route[:, 128:160] = np.arange(E_ALL)
    route[:, 160:160 + N_BLK] = np.arange(N_BLK)
    route[:, 208:216] = P * np.arange(1, 9)
    for T in range(T_ALL):
        route[:, 216 + T] = 1.0 if T else (t < NS)
        for c in range(2):
            route[:, 225 + c * 9 + T] = 2 * (T * P + t) + c + 1
        route[:, 243 + T] = T * P + t + 1
    route[:, 252:252 + N_OVER] = np.arange(N_OVER)
    return {
        "c_ident": np.eye(P, dtype=np.float32), "c_head_mask": head_mask, "c_sel": sel,
        "c_band": band, "c_route": route,
        "c_mask": np.where(t[None, :] >= t[:, None], np.float32(-240000.0), np.float32(0.0)),
        "c_tri": (t[:, None] < t[None, :]).astype(np.float32),
    }


def kernel(**inputs):
    import concourse.bacc as bacc
    from concourse.bass_utils import run_bass_kernel_spmd

    x = {k: np.asarray(v) for k, v in inputs.items()}

    def tiled(prompt, sample):
        out = np.zeros((ROWS, prompt.shape[-1]), prompt.dtype)
        out[0:NS] = sample.reshape(NS, -1)
        out[P:] = prompt.reshape(SEQ, -1)
        return out

    cols = np.zeros((P, 64), np.float32)
    for at, name in ((0, "g_mix"), (8, "g_ffn"), (16, "g_ple")):
        cols[:, at:at + 8] = x[name][0].reshape(KD, P).T
    cols[:, 24:28] = x["s_pool"][0].reshape(NG, PW).T
    bias = x["b_sb"][0]
    cols[:, 36:44] = bias
    cols[0:NS * H, 45] = np.tile(bias, NS)
    state = np.zeros((P, AW), np.float32)
    state[0:NS * STATE] = x["state_pool"][0].reshape(NS * STATE, AW)
    arrays = {
        "x_all": tiled(x["x_prompt"], x["x_sample"]),
        "p_all": tiled(x["p_prompt"][0], x["p_sample"][0]),
        "cache_k": x["cache_k"][0].reshape(-1, P, AW), "cache_v": x["cache_v"][0].reshape(-1, P, AW),
        "state_pool": x["state_pool"][0], "state_rows": state,
        "page_table": x["page_table"].reshape(1, -1),
        "w_in": x["w_in"][0], "w_out": x["w_out"][0],
        "w_pool": x["w_pool"][0].transpose(1, 0, 2),
        "g_qk": np.stack([np.broadcast_to(x["g_q"][0], (P, HD)), np.broadcast_to(x["g_k"][0], (P, HD))], axis=1),
        "c_cols": cols,
        "g_ffn_bc": np.broadcast_to(x["g_ffn"][0], (P, D)),
        "w_router": np.concatenate([x["w_router_group"][0], x["w_router_expert"][0]], axis=1).reshape(KD, P, NR).transpose(1, 0, 2),
        "b_router": np.broadcast_to(np.concatenate([x["b_router_group"][0], x["b_router_expert"][0]]), (P, NR)),
        "w_gate": x["w_gate"][0], "w_up": x["w_up"][0], "w_down": x["w_down"][0],
        "w_ple_gate": x["w_ple_gate"][0], "w_ple_proj": x["w_ple_proj"][0],
    }
    arrays.update(constants())
    arrays = {f"in_{k}": np.ascontiguousarray(v) for k, v in arrays.items()}
    nc = bacc.Bacc("TRN2", target_bir_lowering=False, num_devices=1)
    A = {k[3:]: nc.dram_tensor(k, v.shape, mybir.dt.from_np(v.dtype), kind="ExternalInput").ap() for k, v in arrays.items()}
    outs = {"y_all": (ROWS, D), "k_all": (ROWS, AW), "v_all": (ROWS, AW),
            "pool_prompt": (STATE, AW), "pool_sample": (NS, STATE, AW)}
    O = {k: nc.dram_tensor("out_" + k, s, F32, kind="ExternalOutput").ap() for k, s in outs.items()}
    build(nc, A, O)
    r = run_bass_kernel_spmd(nc, [arrays], core_ids=[0]).results[0]
    y, k, v = r["out_y_all"], r["out_k_all"], r["out_v_all"]
    return (y[P:].reshape(1, SEQ, D), y[0:NS].reshape(NS, 1, D),
            k[P:].reshape(1, 1, SEQ, H, HD), v[P:].reshape(1, 1, SEQ, H, HD), r["out_pool_prompt"].reshape(1, 1, STATE, AW),
            k[0:NS].reshape(1, NS, 1, H, HD), v[0:NS].reshape(1, NS, 1, H, HD), r["out_pool_sample"].reshape(1, NS, STATE, AW))
```

```python
import numpy as np
import concourse.bass as bass
from concourse import mybir
from contextlib import ExitStack

F32 = mybir.dt.float32
F32R = mybir.dt.float32r
BF16 = mybir.dt.bfloat16
I32 = mybir.dt.int32
ALU = mybir.AluOpType
ACT = mybir.ActivationFunctionType
AX = mybir.AxisListType

P = 128
D = 1024
KD = D // P
SEQ, NS = 1024, 8
T_ALL = 1 + SEQ // P
ROWS = T_ALL * P
AW = 512
H, HD = 8, 64
NG, PW = 4, 128
WINDOWS = (2, 4, 8, 16)
STATE = 15
PAGES = 8
E_ALL, EG, EPG = 32, 4, 8
F = 512
KF = F // P
NR = EG + E_ALL
PLE = 256
EPS = 1e-6
SCALE = HD ** -0.5
N_OVER = (2 * (SEQ + NS) - 1) // P
N_BLK = E_ALL + N_OVER
CHUNK = 512
Q_RING = 4
V_RING = 4
W_RING = 4
MW = D + 16
NONE = 100000.0
V_PREV, V_FIRST, V_CUR, V_STATE, V_NEW = range(5)


class Chain:

    def __init__(self, eng, sem):
        self.eng, self.sem, self.base, self.n = eng, sem, 0, 0

    def __call__(self, ins):
        self.n += 1
        ins.then_inc(self.sem, 1)
        self.eng.wait_ge(self.sem, self.base + self.n)

    def loop(self, i, per_turn):
        self.start, self.per_turn = self.n, per_turn
        self.base = i * per_turn

    def end(self, turns):
        assert self.n == self.start + self.per_turn, (self.n - self.start, self.per_turn)
        self.base, self.n = 0, self.start + self.per_turn * turns


def tiles(eng, body, chain=None, per_turn=0):
    body(0, 0)
    if chain:
        n = chain.n
    with eng.Fori(0, 3) as i:
        if chain:
            chain.loop(i, per_turn)
        body(i * 2 + 1, 1, i)
        body(i * 2 + 2, 0, i)
    if chain:
        chain.end(3)
    body(7, 1)
    body(8, 0)


def two_first(eng, body, chain=None, per_turn=0):
    body(0, 0)
    body(1, 1)
    if chain:
        n = chain.n
    with eng.Fori(0, 3) as i:
        if chain:
            chain.loop(i, per_turn)
        body(i * 2 + 2, 0, i)
        body(i * 2 + 3, 1, i)
    if chain:
        chain.end(3)
    body(8, 0)


def build(nc, A, O):
    ctx = ExitStack()

    def dram(name, shape, dt=F32):
        return nc.dram_tensor(name, shape, dt, kind="Internal").ap()

    def sb(stack, name, shape, dt=F32):
        return stack.enter_context(nc.sbuf_tensor(name, shape, dt))

    def pb(stack, name, cols=CHUNK):
        return stack.enter_context(nc.psum_tensor(name, [P, cols], F32))

    def sem(name):
        return ctx.enter_context(nc.semaphore(name))

    q_dram = dram("q_samples", [NS, AW])
    h_dram = dram("h_rows", [ROWS, D])
    m_dram = dram("expert_input_rows", [ROWS, MW])
    y_dram = dram("expert_rows", [2 * ROWS, D])

    with ctx:
        ident = sb(ctx, "ident", [P, P])
        w_rt = sb(ctx, "w_router_sb", [P, KD, NR])
        b_rt = sb(ctx, "b_router_sb", [P, NR])
        cols = sb(ctx, "per_partition", [P, 64])
        g_mix_c, g_ple_c = cols[:, 0:8], cols[:, 16:24]
        s_pool_c = cols[:, 24:28]
        nb_c, pb_c = cols[:, 28:36], cols[:, 36:44]
        nbs_c, pbs_c = cols[:, 44:45], cols[:, 45:46]
        logits = sb(ctx, "logits", [P, T_ALL, NR])
        gate_w = sb(ctx, "gate_weights", [P, 2, T_ALL])
        h_sq = sb(ctx, "h_squares_sum", [P, T_ALL])
        h_rs = sb(ctx, "h_rstd", [P, 3, T_ALL])

        dve_chain = sem("dve_chain")
        chains = {}
        s_const = sem("const_loaded")
        s_out = sem("outputs_stored")

        mid = ctx.enter_context(ExitStack())
        qT = sb(mid, "qT", [P, H // 2, SEQ])
        kT = sb(mid, "kT", [P, H // 2, SEQ])
        v_sb = sb(mid, "v_sb", [P, T_ALL, AW])
        mixp = sb(mid, "pool_mixed_T", [P, NG, ROWS])
        zd = sb(mid, "decode_scores", [P, PAGES, P])
        table = sb(mid, "page_table_sb", [1, NS * PAGES], I32)

        wk_hi, wk_lo = (sb(mid, f"decode_weights_T_{n}", [P, PAGES, NS * H], F32R) for n in ("hi", "lo"))
        rs1 = sb(mid, "x_rstd_of_tiles", [P, T_ALL])
        ident_b = sb(mid, "ident_bf16", [P, P], BF16)
        mask_b = sb(mid, "causal_mask", [P, P], BF16)

        p1 = ExitStack()
        w_hi, w_lo = (sb(p1, f"w_in_{n}", [P, KD, 2 * AW], F32R) for n in ("hi", "lo"))
        w_raw = [sb(p1, f"w_in_raw{i}", [P, AW]) for i in range(W_RING)]
        x_sb = [sb(p1, f"x{i}", [P, D]) for i in range(2)]
        x_hi, x_lo = ([sb(p1, f"xT_{n}{i}", [P, KD, P], F32R) for i in range(2)] for n in ("hi", "lo"))
        p_xt = pb(p1, "p_xt", 2 * CHUNK)
        p_z = [pb(p1, f"p_z{i}") for i in range(2)]
        s_x = [sem("x_loaded0"), sem("x_loaded1")]
        s_wr = [sem(f"w_in_raw_loaded{i}") for i in range(W_RING)]
        s_first = sem("ident_cols_loaded")
        N_W = 2 * KD

        def w_block(c):
            return c % KD, slice(c // KD * AW, (c // KD + 1) * AW)

        def load_w(sp, rnd, c):
            n, k = 2 * rnd + c // KD, c % KD
            sp.dma_start(w_raw[c % W_RING][:], A["w_in"][k * P:(k + 1) * P, n * AW:(n + 1) * AW]).then_inc(s_wr[c % W_RING], 16)

        class Round:

            def __init__(self, rnd):
                self.rnd = rnd
                self.xt_done, self.xhi, self.xlo = sem(f"x_transposed_r{rnd}"), sem(f"xT_hi_r{rnd}"), sem(f"xT_lo_r{rnd}")
                self.whi, self.wlo = sem(f"w_in_hi_r{rnd}"), sem(f"w_in_lo_r{rnd}")
                self.z_done = sem(f"z_done_r{rnd}")

            def x_loads(self, T, par, i):
                nth = T // 2 + 1 if i is None else i + 2
                return nth + (0 if self.rnd == 0 else (4 if par else 5))

            def transpose_x(self, pe, T, par, i):
                pe.wait_ge(s_x[par], self.x_loads(T, par, i) * 16)
                for k in range(KD):
                    ins = pe.transpose(p_xt[:, k * P:(k + 1) * P], x_sb[par][:, k * P:(k + 1) * P], ident[:])
                ins.then_inc(self.xt_done, 1)

            def products(self, pe, T, par, n):
                cs = slice(n * AW, (n + 1) * AW)
                for k in range(KD):
                    if isinstance(T, int) and T == 0:
                        pe.wait_ge(self.wlo, W_RING + n * KD + k + 1)
                    pe.matmul(p_z[n][:], x_hi[par][:, k, :], w_hi[:, k, cs], start=(k == 0), stop=False)
                    pe.matmul(p_z[n][:], x_hi[par][:, k, :], w_lo[:, k, cs], start=False, stop=False)
                    ins = pe.matmul(p_z[n][:], x_lo[par][:, k, :], w_hi[:, k, cs], start=False, stop=(k == KD - 1))
                ins.then_inc(self.z_done, 1)

            def split_x_hi(self, act, T, par):
                act.wait_ge(self.xt_done, T + 1)
                act.activation(x_hi[par][:].rearrange("p k n -> p (k n)"), p_xt[:], ACT.Copy).then_inc(self.xhi, 1)

            def split_x_lo(self, dve, T, par):
                dve.wait_ge(self.xhi, T + 1)
                dve.tensor_tensor(out=x_lo[par][:].rearrange("p k n -> p (k n)"), in0=p_xt[:], in1=x_hi[par][:].rearrange("p k n -> p (k n)"),
                                  op=ALU.subtract).then_inc(self.xlo, 1)

            def split_w_hi(self, act):
                for c in range(N_W):
                    k, cs = w_block(c)
                    act.wait_ge(s_wr[c % W_RING], (self.rnd * (N_W // W_RING) + c // W_RING + 1) * 16)
                    act.activation(w_hi[:, k, cs], w_raw[c % W_RING][:], ACT.Copy, scale=g_mix_c[:, k:k + 1]).then_inc(self.whi, 1)

            def split_w_lo(self, dve):
                for c in range(N_W):
                    k, cs = w_block(c)
                    dve.wait_ge(self.whi, c + 1)
                    dve.scalar_tensor_tensor(out=w_lo[:, k, cs], in0=w_raw[c % W_RING][:], scalar=g_mix_c[:, k:k + 1], in1=w_hi[:, k, cs],
                                             op0=ALU.mult, op1=ALU.subtract).then_inc(self.wlo, 1)

        p1a = ExitStack()
        g_qk = sb(p1a, "g_qk", [P, 2, HD])
        mask_f = sb(p1a, "causal_mask_f32", [P, P])
        z_qk = sb(p1a, "z_qk", [P, 2 * AW])
        sq = sb(p1a, "squares", [P, 2 * AW])
        qk_n = sb(p1a, "qk_norm", [P, 2 * AW])
        k_pg = w_raw
        q_bc = [sb(p1a, f"q_bc{i}", [P, AW]) for i in range(2)]
        prod = [sb(p1a, f"prod{i}", [P, AW]) for i in range(Q_RING)]
        st1 = [sb(p1a, f"stats1_{i}", [P, 4]) for i in range(2)]
        st16 = sb(p1a, "stats16", [P, 3, 16])
        p_qk = pb(p1a, "p_qk", 2 * CHUNK)
        p_sq = pb(p1a, "p_squares_of_x", 2 * CHUNK)
        A1 = Round(0)
        ssx_ready, var_ready, std_ready, rx_ready = sem("x_squares"), sem("x_var"), sem("x_std"), sem("x_rstd")
        zqk_ready = sem("z_qk_copied")
        var16, std16 = sem("qk_var"), sem("qk_std")
        qkn_ready = sem("qk_normalised")
        qkt_done, qkT_ready = sem("qk_transposed"), sem("qT_kT_copied")
        s_k = sem("k_stored")
        s_q = sem("q_samples_stored")
        s_qb = [sem("q_bc_then_tile_loaded0"), sem("q_bc_then_tile_loaded1")]
        s_kp = [sem(f"page_loaded{i}") for i in range(Q_RING)]
        page_used = sem("k_page_used")
        prod_ready, prod_used = sem("prod_ready"), sem("prod_used")
        qbc_used = sem("q_bc_used")
        with nc.Block() as block:
            @block.sync
            def _(sp):
                sp.dma_start(ident[:], A["c_ident"]).then_inc(s_first, 16)
                sp.dma_start(cols[:], A["c_cols"]).then_inc(s_first, 16)
                sp.dma_start(x_sb[0][:], A["x_all"][0:P, :]).then_inc(s_x[0], 16)
                consts = [(g_qk[:], A["g_qk"]), (table[:], A["page_table"]), (w_rt[:], A["w_router"]), (b_rt[:], A["b_router"]),
                          (mask_f[:], A["c_mask"])]
                for c in range(N_W):
                    sp.wait_ge(A1.wlo, c + 1)
                    load_w(sp, 0, c)
                    if c == 7:
                        sp.dma_start(x_sb[1][:], A["x_all"][P:2 * P, :]).then_inc(s_x[1], 16)
                for out, in_ in consts:
                    sp.dma_start(out, in_).then_inc(s_const, 16)
                sp.dma_start(O["pool_sample"][:, 0:STATE - 1, :], A["state_pool"][:, 1:STATE, :]).then_inc(s_out, 16)
                sp.wait_ge(s_const, 16 * len(consts))

                sp.wait_ge(A1.wlo, N_W + W_RING)

                def store_k(T):
                    sp.wait_ge(qkn_ready, T + 1)
                    sp.dma_start(O["k_all"][bass.ts(T, P), :], qk_n[:, AW:2 * AW]).then_inc(s_k, 16)

                def load_pages(b, js):
                    for j in js:
                        n = b * PAGES + j
                        page = sp.value_load(table[0:1, bass.ds(n, 1)], min_val=0, max_val=A["cache_k"].shape[0] - 1)
                        sp.wait_ge(page_used, n + 1)
                        sp.dma_start(k_pg[j % Q_RING][:], A["cache_k"][bass.ds(page, 1), :, :].rearrange("a p n -> (a p) n")).then_inc(s_kp[j % Q_RING], 16)

                def load_x(T, par):
                    sp.wait_ge(ssx_ready, T + 1)
                    sp.wait_ge(A1.xt_done, T + 1)
                    rows = slice(0, P) if isinstance(T, int) and T == T_ALL - 1 else bass.ts(T + 2, P)
                    sp.dma_start(x_sb[par][:], A["x_all"][rows, :]).then_inc(s_x[par], 16)

                def tile(T, par, i=None):
                    if isinstance(T, int) and T == 0:
                        load_x(T, par)
                        store_k(0)
                        sp.dma_start(q_dram, qk_n[0:NS, 0:AW]).then_inc(s_q, 16)
                        sp.wait_ge(s_q, 16)
                        return
                    sp.wait_ge(qbc_used, T)
                    sp.dma_start(q_bc[1 - par][:], q_dram[bass.ds(T - 1, 1), :].to_broadcast([P, AW])).then_inc(s_qb[1 - par], 16)
                    load_pages(T - 1, range(PAGES // 2))
                    if not (isinstance(T, int) and T == 1):
                        store_k(T - 1)
                    load_x(T, par)
                    load_pages(T - 1, range(PAGES // 2, PAGES))

                two_first(sp, tile)
                store_k(T_ALL - 1)
                sp.wait_ge(page_used, NS * PAGES + Q_RING)
                for c in range(W_RING):
                    load_w(sp, 1, c)
                sp.wait_ge(s_k, 16 * T_ALL)
                sp.wait_ge(s_out, 16)

            @block.tensor
            def _(pe):
                pe.wait_ge(s_first, 32)
                A1.transpose_x(pe, 0, 0, None)

                def transpose_qk(T):
                    pe.wait_ge(qkn_ready, T + 1)
                    if not (isinstance(T, int) and T == 1):
                        pe.wait_ge(qkT_ready, T * 2 - 2)
                    for c in range(2 * AW // P):
                        ins = pe.transpose(p_qk[:, c * P:(c + 1) * P], qk_n[:, c * P:(c + 1) * P], ident[:])
                    ins.then_inc(qkt_done, 1)

                def tile(T, par, i=None):
                    first = isinstance(T, int) and T == 0
                    pe.wait_ge(A1.xlo, T + 1)
                    pe.wait_ge(A1.xhi, T + 1)
                    for n in range(2):
                        if not first:
                            pe.wait_ge(zqk_ready, T * 2 - 1 + n)
                        A1.products(pe, T, par, n)
                        if n == 0:
                            if i is not None or T + 1 < T_ALL:
                                A1.transpose_x(pe, T + 1, 1 - par, None if i is None else (i if par == 0 else i + 1))
                            if not (isinstance(T, int) and T < 2):
                                transpose_qk(T - 1)

                two_first(pe, tile)
                transpose_qk(T_ALL - 1)

            @block.scalar
            def _(act):
                act.wait_ge(s_first, 32)

                def stats(T, par, i):
                    act.wait_ge(s_x[par], A1.x_loads(T, par, i) * 16)
                    if not (isinstance(T, int) and T < 2):
                        act.wait_ge(rx_ready, T - 1)
                    if not (isinstance(T, int) and T == 0):
                        act.wait_ge(ssx_ready, T)
                    act.activation(p_sq[:], x_sb[par][:], ACT.Square, accum_out=st1[par][:, 0:1]).then_inc(ssx_ready, 1)
                    A1.split_x_hi(act, T, par)
                    act.wait_ge(var_ready, T + 1)
                    act.activation(st1[par][:, 2:3], st1[par][:, 1:2], ACT.Sqrt).then_inc(std_ready, 1)

                def copy_z(T, par, n):
                    act.wait_ge(A1.z_done, T * 2 + n + 1)
                    cs = slice(n * AW, (n + 1) * AW)
                    act.activation(sq[:, cs], p_z[n][:], ACT.Square, scale=st1[par][:, 3:4])
                    act.activation(z_qk[:, cs], p_z[n][:], ACT.Copy, scale=st1[par][:, 3:4]).then_inc(zqk_ready, 1)

                def copy_qkT(T):
                    act.wait_ge(qkt_done, T)
                    for half, out in enumerate((qT, kT)):
                        act.activation(out[:, :, bass.ts(T - 1, P)], p_qk[:, half * AW:(half + 1) * AW].rearrange("p (c n) -> p c n", n=P),
                                       ACT.Copy).then_inc(qkT_ready, 1)

                stats(0, 0, None)
                A1.split_w_hi(act)

                def tile(T, par, i=None):
                    act.wait_ge(rx_ready, T + 1)
                    if not (isinstance(T, int) and T == 0):
                        act.wait_ge(qkn_ready, T)
                    copy_z(T, par, 0)
                    if i is not None or T + 1 < T_ALL:
                        stats(T + 1, 1 - par, None if i is None else (i if par == 0 else i + 1))
                    if not (isinstance(T, int) and T < 2):
                        copy_qkT(T - 1)
                    copy_z(T, par, 1)
                    act.wait_ge(var16, T + 1)
                    act.activation(st16[:, 1, :], st16[:, 0, :], ACT.Sqrt).then_inc(std16, 1)

                two_first(act, tile)
                copy_qkT(T_ALL - 1)

            @block.vector
            def _(dve):
                chain = chains["dve"] = Chain(dve, dve_chain)
                dve.sem_inc(prod_used, Q_RING)
                dve.sem_inc(A1.wlo, W_RING)
                chain(dve.memset(zd[:], 0.0))
                dve.wait_ge(s_first, 32)
                chain(dve.tensor_copy(ident_b[:], ident[:]))
                chain(dve.tensor_scalar(nb_c, pb_c, -1.0, None, ALU.mult))
                chain(dve.tensor_scalar(nbs_c, pbs_c, -1.0, None, ALU.mult))

                def stats(T, par):
                    dve.wait_ge(ssx_ready, T + 1)
                    dve.tensor_scalar(st1[par][:, 1:2], st1[par][:, 0:1], 1.0 / D, EPS, ALU.mult, ALU.add).then_inc(var_ready, 1)
                    A1.split_x_lo(dve, T, par)
                    dve.wait_ge(std_ready, T + 1)
                    if not (isinstance(T, int) and T < 2):
                        dve.wait_ge(zqk_ready, T * 2 - 2)
                    dve.reciprocal(st1[par][:, 3:4], st1[par][:, 2:3]).then_inc(rx_ready, 1)

                stats(0, 0)
                A1.split_w_lo(dve)

                def heads(t):
                    return t.rearrange("p (h d) -> p h d", d=HD)

                def key_scores(T, js):
                    if isinstance(T, int) and T == 0:
                        return
                    for j in js:
                        dve.wait_ge(prod_ready, (T - 1) * PAGES + j + 1)
                        dve.tensor_reduce(out=zd[:, j, bass.ds((T - 1) * H, H)], in_=heads(prod[j % Q_RING][:]),
                                          axis=AX.X, op=ALU.add).then_inc(prod_used, 1)

                def tile(T, par, i=None):
                    if i is not None or T + 1 < T_ALL:
                        stats(T + 1, 1 - par)
                    key_scores(T, range(PAGES // 2))
                    dve.wait_ge(zqk_ready, T * 2 + 2)
                    chain(dve.tensor_reduce(out=st16[:, 2, :], in_=heads(sq[:]), axis=AX.X, op=ALU.add))
                    if not (isinstance(T, int) and T == 0):
                        dve.wait_ge(std16, T)
                    dve.tensor_scalar(st16[:, 0, :], st16[:, 2, :], 1.0 / HD, EPS, ALU.mult, ALU.add).then_inc(var16, 1)
                    dve.wait_ge(rx_ready, T + 1)
                    chain(dve.tensor_copy(rs1[:, bass.ds(T, 1)], st1[par][:, 3:4]))
                    dve.wait_ge(std16, T + 1)
                    chain(dve.reciprocal(st16[:, 2, :], st16[:, 1, :]))
                    chain(dve.tensor_tensor(out=heads(sq[:]), in0=heads(z_qk[:]),
                                            in1=st16[:, 2, :].unsqueeze(2).to_broadcast([P, 16, HD]), op=ALU.mult))
                    if isinstance(T, int) and T == 0:
                        dve.wait_ge(s_const, 80)
                        chain(dve.tensor_copy(mask_b[:], mask_f[:]))
                    else:
                        dve.wait_ge(s_k, T * 16)
                        if isinstance(T, int) and T == 1:
                            dve.wait_ge(s_q, 16)
                        else:
                            dve.wait_ge(qkt_done, T - 1)
                    for s in range(2):
                        ins = dve.tensor_tensor(out=heads(qk_n[:, s * AW:(s + 1) * AW]), in0=heads(sq[:, s * AW:(s + 1) * AW]),
                                                in1=g_qk[:, s, :].unsqueeze(1).to_broadcast([P, H, HD]), op=ALU.mult)
                    ins.then_inc(qkn_ready, 1)
                    key_scores(T, range(PAGES // 2, PAGES))

                two_first(dve, tile, chain, 2 * 4)

            @block.gpsimd
            def _(pool):
                pool.sem_inc(page_used, Q_RING)
                pool.sem_inc(qbc_used, 2)

                def sample(b, par, nth):
                    pool.wait_ge(s_qb[par], nth * 16)
                    for j in range(PAGES):
                        n = b * PAGES + j
                        pool.wait_ge(s_kp[j % Q_RING], (b * 2 + j // Q_RING + 1) * 16)
                        pool.wait_ge(prod_used, n + 1)
                        ins = pool.tensor_tensor(out=prod[j % Q_RING][:], in0=k_pg[j % Q_RING][:], in1=q_bc[par][:], op=ALU.mult)
                        ins.then_inc(prod_ready, 1)
                        pool.wait_ge(prod_ready, n + 1)
                        pool.sem_inc(page_used, 1)
                    pool.sem_inc(qbc_used, 1)

                with pool.Fori(0, NS // 2) as i:
                    sample(i * 2, 0, i + 1)
                    sample(i * 2 + 1, 1, i + 1)
        p1a.close()

        p1b = ExitStack()
        band = sb(p1b, "band", [P, NG, 5, P])
        w_pl = sb(p1b, "w_pool_sb", [P, NG, PW])
        u_s = sb(p1b, "u_samples", [P, AW])
        u_sb = [sb(p1b, f"u{i}", [P, AW]) for i in range(2)]
        st_sb = sb(p1b, "state_sb", [P, AW])
        pooledT = sb(p1b, "pooledT", [P, NG, P])
        keep_d = sb(p1b, "decode_keep", [P, SEQ + 1])
        beta_d = sb(p1b, "decode_beta", [P, SEQ])
        p_pool = pb(p1b, "p_pool")
        p_py = pb(p1b, "p_py")
        p_d = pb(p1b, "p_decode", 2 * CHUNK)
        B1 = Round(1)
        v_ready, u_ready = sem("v_copied"), sem("u_copied")
        pool_done, pooledT_ready = sem("pooled_done"), sem("pooledT_copied")
        py_done, mixp_ready = sem("pool_map_done"), sem("pool_mixed_copied")
        s_pc = sem("pooling_constants")
        s_v = sem("v_stored")
        d_step = sem("decode_weights_step")
        with nc.Block() as block:
            @block.sync
            def _(sp):
                for c in range(W_RING, N_W):
                    sp.wait_ge(B1.wlo, c + 1)
                    load_w(sp, 1, c)
                for out, in_ in ((band[:], A["c_band"]), (w_pl[:], A["w_pool"]), (st_sb[:], A["state_rows"])):
                    sp.dma_start(out, in_).then_inc(s_pc, 16)

                def tile(T, par, i=None):
                    if not (isinstance(T, int) and T == T_ALL - 1):
                        sp.wait_ge(B1.xt_done, T + 1)
                        sp.dma_start(x_sb[par][:], A["x_all"][bass.ts(T + 2, P), :]).then_inc(s_x[par], 16)
                    sp.wait_ge(v_ready, T + 1)
                    sp.dma_start(O["v_all"][bass.ts(T, P), :], v_sb[:, bass.ds(T, 1), :].rearrange("p a n -> p (a n)")).then_inc(s_v, 16)
                    if isinstance(T, int) and T == 0:
                        sp.wait_ge(u_ready, 1)
                        sp.dma_start(O["pool_sample"][:, STATE - 1, :], u_s[0:NS, :]).then_inc(s_out, 16)

                two_first(sp, tile)
                sp.wait_ge(u_ready, T_ALL)
                sp.dma_start(O["pool_prompt"], u_sb[1][P - STATE:P, :]).then_inc(s_out, 16)
                sp.wait_ge(s_v, 16 * T_ALL)
                sp.wait_ge(s_out, 48)
                sp.wait_ge(s_x[1], 16 * (4 + 5))

            @block.tensor
            def _(pe):
                B1.transpose_x(pe, 0, 0, None)

                def pooling(T, mat):
                    pe.wait_ge(u_ready, T + 1)
                    first = isinstance(T, int) and T == 0
                    if first:
                        pe.wait_ge(s_pc, 48)
                    else:
                        pe.wait_ge(pooledT_ready, T)
                    for g in range(NG):
                        cs = slice(g * PW, (g + 1) * PW)
                        for s, (left, m) in enumerate(mat(g)):
                            ins = pe.matmul(p_pool[:, cs], left[:, cs], m, start=(s == 0), stop=(s == 1))
                    ins.then_inc(pool_done, 1)

                def pool_map(T):
                    pe.wait_ge(pooledT_ready, T + 1)
                    if not (isinstance(T, int) and T == 0):
                        pe.wait_ge(mixp_ready, T)
                    for g in range(NG):
                        ins = pe.matmul(p_py[:, g * P:(g + 1) * P], w_pl[:, g, :], pooledT[:, g, :], start=True, stop=True)
                    ins.then_inc(py_done, 1)

                def matrices(T, par, i):
                    def mat(g):
                        if isinstance(T, int) and T == 0:
                            return [(st_sb, band[:, g, V_STATE, :]), (u_s, band[:, g, V_NEW, :])]
                        if isinstance(T, int) or par == 0:
                            cur = band[:, g, V_CUR, :]
                        else:
                            cur = band[:, g, bass.ds(V_FIRST + (i > 0), 1), :].rearrange("p a n -> p (a n)")
                        return [(u_sb[par], band[:, g, V_PREV, :]), (u_sb[1 - par], cur)]
                    return mat

                def tile(T, par, i=None):
                    first = isinstance(T, int) and T == 0
                    pe.wait_ge(B1.xlo, T + 1)
                    pe.wait_ge(B1.xhi, T + 1)
                    for n in range(2):
                        if not first:
                            pe.wait_ge([v_ready, u_ready][n], T)
                        B1.products(pe, T, par, n)
                        if n == 0:
                            if i is not None or T + 1 < T_ALL:
                                B1.transpose_x(pe, T + 1, 1 - par, None if i is None else (i if par == 0 else i + 1))
                            if not first:
                                pooling(T - 1, matrices(T - 1, 1 - par, i))
                        elif not first:
                            pool_map(T - 1)
                    if first:
                        for j in range(PAGES):
                            ins = pe.transpose(p_d[:, j * P:(j + 1) * P], zd[:, j, :], ident[:])
                        ins.then_inc(d_step, 1)
                    if isinstance(T, int) and T == 1:
                        pe.wait_ge(d_step, 4)
                        for j in range(PAGES):
                            ins = pe.transpose(p_d[:, j * P:(j + 1) * P], beta_d[:, j * P:(j + 1) * P], ident[:])
                        ins.then_inc(d_step, 1)

                two_first(pe, tile)
                pooling(T_ALL - 1, matrices(T_ALL - 1, 0, None))
                pool_map(T_ALL - 1)

            @block.scalar
            def _(act):
                B1.split_x_hi(act, 0, 0)
                B1.split_w_hi(act)

                def copy_pooled(T):
                    act.wait_ge(pool_done, T + 1)
                    if not (isinstance(T, int) and T == 0):
                        act.wait_ge(py_done, T)
                    act.activation(pooledT[:].rearrange("p g n -> p (g n)"), p_pool[:], ACT.Copy).then_inc(pooledT_ready, 1)

                def copy_mixed(T):
                    act.wait_ge(py_done, T + 1)
                    for g in range(NG):
                        ins = act.activation(mixp[:, g, bass.ts(T, P)], p_py[:, g * P:(g + 1) * P], ACT.Copy, scale=s_pool_c[:, g:g + 1])
                    ins.then_inc(mixp_ready, 1)

                def tile(T, par, i=None):
                    first = isinstance(T, int) and T == 0
                    if i is not None or T + 1 < T_ALL:
                        B1.split_x_hi(act, T + 1, 1 - par)
                    if not first:
                        copy_pooled(T - 1)
                        copy_mixed(T - 1)
                    if first:
                        act.wait_ge(d_step, 1)
                        act.activation(keep_d[:, 0:SEQ], p_d[:], ACT.Sigmoid, bias=nbs_c, scale=-SCALE).then_inc(d_step, 1)
                        act.activation(beta_d[:], p_d[:], ACT.Sigmoid, bias=pbs_c, scale=SCALE).then_inc(d_step, 1)
                    if isinstance(T, int) and T == 1:
                        act.wait_ge(d_step, 5)
                        act.activation(wk_hi[:], p_d[:].rearrange("p (j n) -> p j n", n=P)[:, :, 0:NS * H], ACT.Copy).then_inc(d_step, 1)

                two_first(act, tile)
                copy_pooled(T_ALL - 1)
                copy_mixed(T_ALL - 1)

            @block.vector
            def _(dve):
                chain = chains["dve"]
                chain.eng = dve
                dve.sem_inc(B1.wlo, W_RING)
                chain(dve.memset(u_sb[1][:], 0.0))
                chain(dve.memset(keep_d[:, SEQ:SEQ + 1], 1.0))
                B1.split_x_lo(dve, 0, 0)
                B1.split_w_lo(dve)

                def tile(T, par, i=None):
                    first = isinstance(T, int) and T == 0
                    if i is not None or T + 1 < T_ALL:
                        B1.split_x_lo(dve, T + 1, 1 - par)
                    rs = rs1[:, bass.ds(T, 1)]
                    dve.wait_ge(B1.z_done, T * 2 + 1)
                    dve.tensor_scalar(v_sb[:, bass.ds(T, 1), :].rearrange("p a n -> p (a n)"), p_z[0][:], rs, None, ALU.mult).then_inc(v_ready, 1)
                    dve.wait_ge(B1.z_done, T * 2 + 2)
                    if not first:
                        dve.wait_ge(pool_done, T)
                    dve.tensor_scalar((u_s if first else u_sb[1 - par])[:], p_z[1][:], rs, None, ALU.mult).then_inc(u_ready, 1)
                    if first:
                        dve.wait_ge(d_step, 3)
                        chain(dve.tensor_tensor_scan(out=keep_d[:, 0:SEQ][:, ::-1], data0=keep_d[:, 0:SEQ][:, ::-1],
                                                     data1=keep_d[:, 0:SEQ][:, ::-1], initial=1.0, op0=ALU.mult, op1=ALU.bypass))
                        dve.tensor_tensor(out=beta_d[:], in0=beta_d[:], in1=keep_d[:, 1:SEQ + 1], op=ALU.mult).then_inc(d_step, 1)
                    if isinstance(T, int) and T == 1:
                        dve.wait_ge(d_step, 6)
                        dve.tensor_tensor(out=wk_lo[:], in0=p_d[:].rearrange("p (j n) -> p j n", n=P)[:, :, 0:NS * H], in1=wk_hi[:],
                                          op=ALU.subtract).then_inc(d_step, 1)

                two_first(dve, tile)
        p1b.close()
        p1.close()

        p2 = ExitStack()
        keep = [sb(p2, f"keep{i}", [P, SEQ + 1]) for i in range(2)]
        beta = [sb(p2, f"beta{i}", [P, SEQ]) for i in range(2)]
        w_out = sb(p2, "w_out_sb", [P, KD, D])
        p_sc = [pb(p2, f"p_sc{i}", 2 * CHUNK) for i in range(2)]
        p_at = [pb(p2, f"p_at{i}") for i in range(2)]
        p_o = pb(p2, "p_o")
        p_w = pb(p2, "p_w")
        s_wout = sem("w_out_loaded")

        GRP = 4
        aT = [sb(p2, f"aT{i}", [P, GRP, P]) for i in range(4)]
        attn = [sb(p2, f"attn{i}", [P, AW]) for i in range(2)]
        mixT = sb(p2, "attn_mixed_T", [P, AW // P, P])
        mixT_s = sb(p2, "attn_mixed_T_samples", [P, AW // P, P])
        v_pg = [sb(p2, f"v_page{i}", [P, AW]) for i in range(V_RING)]
        v_hi, v_lo = ([sb(p2, f"v_page_{n}{i}", [P, AW], F32R) for i in range(3)] for n in ("hi", "lo"))
        w_dec = [sb(p2, f"decode_columns{i}", [P, PAGES, 2 * NS * H], F32R) for i in range(2)]
        sel = sb(p2, "row_to_sample", [P, NS])
        p_dec, head_mask, dec_m = p_sc[1][:, CHUNK:2 * CHUNK], beta[1][:, 0:CHUNK], keep[1][:, 0:CHUNK]
        x_r = [sb(p2, f"x_res{i}", [P, D]) for i in range(2)]
        h_sb = [sb(p2, f"h{i}", [P, D]) for i in range(2)]
        m_sb = [sb(p2, f"h_times_g{i}", [P, D]) for i in range(2)]
        hT = sb(p2, "hT", [P, KD, P])
        g_ffn = sb(p2, "g_ffn_sb", [P, D])

        sc_done, sig_done, a_done = sem("scores_done"), sem("sigmoids_done"), sem("weights_done")
        at_done, at_copied, o_done, attn_copied = sem("aT_done"), sem("aT_copied"), sem("heads_done"), sem("attn_copied")
        w_done, w_copied = sem("p_w_filled"), sem("p_w_copied")
        s_vp, vp_base = s_kp, NS * PAGES // Q_RING
        vhi_ready, vlo_ready = sem("v_page_hi"), sem("v_page_lo")
        page_done, wdec_ready, decm_ready = sem("v_page_multiplied"), sem("decode_columns_ready"), sem("decode_masked")
        s_xr = [sem("x_res_loaded0"), sem("x_res_loaded1")]
        h_ss, m_ready, mixs_zero = sem("h_squares"), sem("h_times_g_ready"), sem("mixed_zeroed")
        s_hm = [sem("h_m_stored0"), sem("h_m_stored1")]
        s_c2 = sem("const2_loaded")

        jobs = [1, 2, 3, 4, 0, 5, 6, 7, 8]
        plan = [("scores", 0), ("scores", 1)]
        plan += [("split", p) for p in range(3)]
        pieces, next_page, next_split = [], 0, 3
        for t in range(1, T_ALL):
            if t >= 2:
                pieces += [(jobs.index(t - 1), k) for k in range(8)]
            if t == 5:
                pieces += [(jobs.index(0), k) for k in range(8)]
            for h in range(H):
                n = (t - 1) * H + h
                plan.append(("turn", n))
                if n + 2 < (T_ALL - 1) * H:
                    plan.append(("scores", n + 2))
                for _ in range(min(0 if n < 3 else 3 if n < 17 else 2, NS * PAGES - next_page)):
                    plan.append(("page", next_page))
                    next_page += 1
                while next_split < min(next_page + 3, NS * PAGES):
                    plan.append(("split", next_split))
                    next_split += 1
                if pieces:
                    plan.append(("piece", pieces.pop(0)))
                    if t >= 5 and plan[-1][1][1] in (1, 3):
                        plan.append(("piece", pieces.pop(0)))
                plan.append(("values", n))
                if n == 28:
                    assert next_page == NS * PAGES
                    plan.append(("mask", 0))
                if n == 29:
                    plan.append(("samples", 0))
            plan.append(("attn", t))
        assert not pieces
        plan += [("piece", (jobs.index(T_ALL - 1), k)) for k in range(8)]
        group_of, n_groups = {}, 0
        for what, arg in plan:
            if what == "turn":
                group_of[arg] = n_groups
                n_groups += (arg // H + 1 + GRP - 1) // GRP
            elif what == "samples":
                group_of["samples"] = n_groups
                n_groups += 1
        fills = {}
        for what, arg in plan:
            if what == "piece":
                j, k = arg
                name = {0: "mix", 2: "h0", 4: "h1", 5: "t0", 6: "t1", 7: "logits"}.get(k)
                if name and not (name == "mix" and jobs[j] == 0):
                    fills[j, name] = len(fills)

        def bank(j, name):
            if j == len(jobs) - 1 and name in ("h0", "h1", "t0", "t1"):
                i, half = {"h0": (0, 0), "h1": (0, 1), "t0": (1, 0), "t1": (1, 1)}[name]
                return p_sc[i][:, half * CHUNK:(half + 1) * CHUNK]
            return p_w[:]

        with nc.Block() as block:
            @block.sync
            def _(sp):
                w_out_rows = A["w_out"].rearrange("(k p) n -> p k n", p=P)

                def load_pages(b):
                    for j in range(PAGES):
                        n = b * PAGES + j
                        page = sp.value_load(table[0:1, bass.ds(n, 1)], min_val=0, max_val=A["cache_v"].shape[0] - 1)
                        sp.wait_ge(vlo_ready, n + 1)
                        sp.dma_start(v_pg[j % V_RING][:], A["cache_v"][bass.ds(page, 1), :, :].rearrange("a p n -> (a p) n")).then_inc(s_vp[j % V_RING], 16)
                        if isinstance(b, int) and (j >= 4 if b == 0 else j % 2 == 1):
                            k = j - 4 if b == 0 else 4 + j // 2
                            sp.dma_start(w_out[:, k, :], w_out_rows[:, k, :]).then_inc(s_wout, 16)

                load_pages(0)
                load_pages(1)
                for out, in_ in ((g_ffn[:], A["g_ffn_bc"]), (head_mask, A["c_head_mask"]), (sel[:], A["c_sel"])):
                    sp.dma_start(out, in_).then_inc(s_c2, 16)
                with sp.Fori(0, NS - 2) as i:
                    load_pages(i + 2)

            @block.gpsimd
            def _(pool):
                pool.memset(mixT_s[:], 0.0).then_inc(mixs_zero, 1)
                for j in range(2):
                    pool.dma_start(x_r[j][:], A["x_all"][bass.ts(jobs[j], P), :]).then_inc(s_xr[j], 16)
                for j, T in enumerate(jobs):
                    pool.wait_ge(m_ready, 2 * j + 2)
                    pool.wait_ge(h_ss, j + 1)
                    pool.dma_start(h_dram[T * P:(T + 1) * P, :], h_sb[j % 2][:]).then_inc(s_hm[j % 2], 16)
                    pool.dma_start(m_dram[T * P:(T + 1) * P, 0:D], m_sb[j % 2][:]).then_inc(s_hm[j % 2], 16)
                    if j + 2 < len(jobs):
                        pool.dma_start(x_r[j % 2][:], A["x_all"][bass.ts(jobs[j + 2], P), :]).then_inc(s_xr[j % 2], 16)
                pool.wait_ge(s_hm[0], 32 * 5)
                pool.wait_ge(s_hm[1], 32 * 4)

            @block.tensor
            def _(pe):
                for what, arg in plan:
                    if what == "scores":
                        t, h = arg // H + 1, arg % H
                        rows = slice(HD * (h % 2), HD * (h % 2) + HD)
                        if arg >= 2:
                            pe.wait_ge(sig_done, arg - 1)
                        N = t * P
                        for c in range(0, N, CHUNK):
                            w = min(CHUNK, N - c)
                            has_mask = c + w == N
                            ins = pe.matmul(p_sc[arg % 2][:, c:c + w], qT[rows, h // 2, (t - 1) * P:t * P],
                                            kT[rows, h // 2, c:c + w], start=True, stop=not has_mask)
                            if has_mask:
                                ins = pe.matmul(p_sc[arg % 2][:, N - P:N], ident_b[:], mask_b[:], start=False, stop=True)
                        ins.then_inc(sc_done, 1)
                    elif what == "turn":
                        t = arg // H + 1
                        pe.wait_ge(a_done, arg + 1)
                        g0 = group_of[arg]
                        for g in range((t + GRP - 1) // GRP):
                            if g0 + g >= 2:
                                pe.wait_ge(at_copied, g0 + g - 1)
                            for b in range(g * GRP, min(t, (g + 1) * GRP)):
                                ins = pe.transpose(p_at[(g0 + g) % 2][:, (b % GRP) * P:(b % GRP + 1) * P],
                                                   beta[arg % 2][:, SEQ - t * P + b * P:SEQ - t * P + (b + 1) * P], ident[:])
                            ins.then_inc(at_done, 1)
                    elif what == "values":
                        t, h = arg // H + 1, arg % H
                        g0 = group_of[arg]
                        if h == 0 and t >= 2:
                            pe.wait_ge(attn_copied, t - 1)
                        for g in range((t + GRP - 1) // GRP):
                            pe.wait_ge(at_copied, g0 + g + 1)
                            for b in range(g * GRP, min(t, (g + 1) * GRP)):
                                ins = pe.matmul(p_o[:, h * HD:(h + 1) * HD], aT[(g0 + g) % 4][:, b % GRP, :],
                                                v_sb[:, b + 1, h * HD:(h + 1) * HD], start=(b == 0), stop=(b == t - 1))
                        ins.then_inc(o_done, 1)
                    elif what == "page":
                        b, j = arg // PAGES, arg % PAGES
                        if j == 0:
                            pe.wait_ge(wdec_ready, b + 1)
                        pe.wait_ge(vlo_ready, V_RING + arg + 1)
                        pe.wait_ge(vhi_ready, arg + 1)
                        pe.matmul(p_dec, w_dec[b % 2][:, j, :], v_hi[arg % 3][:], start=(arg == 0), stop=False)
                        ins = pe.matmul(p_dec, w_dec[b % 2][:, j, :], v_lo[arg % 3][:], start=False, stop=(arg == NS * PAGES - 1))
                        ins.then_inc(page_done, 1)
                    elif what == "samples":
                        g = group_of["samples"]
                        pe.wait_ge(at_copied, g - 1)
                        pe.wait_ge(s_c2, 48)
                        pe.wait_ge(decm_ready, 1)
                        for c in range(AW // P):
                            ins = pe.matmul(p_at[g % 2][:, c * NS:(c + 1) * NS], dec_m[:, c * P:(c + 1) * P], sel[:], start=True, stop=True)
                        ins.then_inc(at_done, 1)
                    elif what == "piece":
                        j, k = arg
                        T = jobs[j]

                        def begin(name):
                            if fills[j, name] > 0 and not (j == len(jobs) - 1 and name in ("h1", "t0", "t1")):
                                pe.wait_ge(w_copied, fills[j, name])

                        if k == 0 and T > 0:
                            begin("mix")
                            pe.wait_ge(attn_copied, T)
                            for c in range(AW // P):
                                ins = pe.transpose(p_w[:, c * P:(c + 1) * P], attn[T % 2][:, c * P:(c + 1) * P], ident[:])
                            ins.then_inc(w_done, 1)
                        if k in (1, 2, 3, 4):
                            n = (k - 1) // 2
                            if k == 1:
                                begin("h0")
                                pe.wait_ge(s_wout, 16 * KD)
                                if T == 0:
                                    pe.wait_ge(at_copied, group_of["samples"] + 1)
                            if k == 3:
                                begin("h1")
                            for kk in range(4 * ((k - 1) % 2), 4 * ((k - 1) % 2) + 4):
                                if kk < 4:
                                    lhs = (mixT if T > 0 else mixT_s)[:, kk, :]
                                else:
                                    lhs = mixp[:, kk - 4, T * P:(T + 1) * P]
                                ins = pe.matmul(bank(j, f"h{n}"), lhs, w_out[:, kk, n * CHUNK:(n + 1) * CHUNK], start=(kk == 0), stop=(kk == 7))
                            if k in (2, 4):
                                ins.then_inc(w_done, 1)
                        if k in (5, 6):
                            begin(f"t{k - 5}")
                            pe.wait_ge(m_ready, 2 * j + k - 4)
                            for c in range(4):
                                kk = 4 * (k - 5) + c
                                ins = pe.transpose(bank(j, f"t{k - 5}")[:, c * P:(c + 1) * P], m_sb[j % 2][:, kk * P:(kk + 1) * P], ident[:])
                            ins.then_inc(w_done, 1)
                        if k == 7:
                            begin("logits")
                            for kk in range(KD):
                                ins = pe.matmul(p_w[:, 0:NR], hT[:, kk, :], w_rt[:, kk, :], start=(kk == 0), stop=(kk == KD - 1))
                            ins.then_inc(w_done, 1)

            @block.scalar
            def _(act):
                act.wait_ge(mixs_zero, 1)
                for what, arg in plan:
                    if what == "scores":
                        t, h = arg // H + 1, arg % H
                        N = t * P
                        act.wait_ge(sc_done, arg + 1)
                        if arg >= 2:
                            act.wait_ge(a_done, arg - 1)
                        act.activation(keep[arg % 2][:, SEQ - N:SEQ], p_sc[arg % 2][:, 0:N], ACT.Sigmoid, bias=nb_c[:, h:h + 1], scale=-SCALE)
                        act.activation(beta[arg % 2][:, SEQ - N:SEQ], p_sc[arg % 2][:, 0:N], ACT.Sigmoid, bias=pb_c[:, h:h + 1],
                                       scale=SCALE).then_inc(sig_done, 1)
                    elif what == "turn":
                        t = arg // H + 1
                        g0 = group_of[arg]
                        if arg >= 2:
                            act.wait_ge(o_done, arg - 1)
                        for g in range((t + GRP - 1) // GRP):
                            w = min(GRP, t - g * GRP)
                            act.wait_ge(at_done, g0 + g + 1)
                            act.activation(aT[(g0 + g) % 4][:, 0:w, :], p_at[(g0 + g) % 2][:, 0:w * P].rearrange("p (b n) -> p b n", n=P),
                                           ACT.Copy).then_inc(at_copied, 1)
                    elif what == "split":
                        act.wait_ge(s_vp[arg % V_RING], (vp_base + arg // V_RING + 1) * 16)
                        if arg >= 3:
                            act.wait_ge(page_done, arg - 2)
                        act.activation(v_hi[arg % 3][:], v_pg[arg % V_RING][:], ACT.Copy).then_inc(vhi_ready, 1)
                    elif what == "samples":
                        g = group_of["samples"]
                        act.wait_ge(at_done, g + 1)
                        act.activation(mixT_s[:, :, 0:NS], p_at[g % 2][:, 0:AW // P * NS].rearrange("p (c b) -> p c b", b=NS),
                                       ACT.Copy).then_inc(at_copied, 1)
                    elif what == "attn":
                        act.wait_ge(o_done, arg * H)
                        if arg >= 3:
                            act.wait_ge(w_done, fills[jobs.index(arg - 2), "mix"] + 1)
                        act.activation(attn[arg % 2][:], p_o[:], ACT.Copy).then_inc(attn_copied, 1)
                    elif what == "piece":
                        j, k = arg
                        T = jobs[j]
                        if k == 0 and T > 0:
                            act.wait_ge(w_done, fills[j, "mix"] + 1)
                            act.activation(mixT[:].rearrange("p c n -> p (c n)"), p_w[:], ACT.Copy).then_inc(w_copied, 1)
                        if k == 5:
                            act.wait_ge(w_copied, fills[j, "h1"] + 1)
                            if j >= 1:
                                act.wait_ge(h_ss, j)
                            act.activation(x_r[j % 2][:], h_sb[j % 2][:], ACT.Square, accum_out=h_sq[:, T:T + 1]).then_inc(h_ss, 1)
            @block.vector
            def _(dve):
                chain = chains["dve"]
                chain.eng = dve
                dve.sem_inc(vlo_ready, V_RING)
                for i in range(2):
                    chain(dve.memset(keep[i][:, SEQ:SEQ + 1], 1.0))
                dve.wait_ge(mixs_zero, 1)
                zero_cols = mixT_s[:, 0:1, 64:64 + H].to_broadcast([P, PAGES, H])
                for i in range(2):
                    for half in range(2):
                        chain(dve.tensor_copy(w_dec[i][:, 4 * half:4 * half + 4, :], mixT_s[:]))

                for what, arg in plan:
                    if what == "scores":
                        t = arg // H + 1
                        N = t * P
                        b = arg % 2
                        dve.wait_ge(sig_done, arg + 1)
                        chain(dve.tensor_tensor_scan(out=keep[b][:, SEQ - N:SEQ][:, ::-1], data0=keep[b][:, SEQ - N:SEQ][:, ::-1],
                                                     data1=keep[b][:, SEQ - N:SEQ][:, ::-1], initial=1.0, op0=ALU.mult, op1=ALU.bypass))
                        dve.tensor_tensor(out=beta[b][:, SEQ - N:SEQ], in0=beta[b][:, SEQ - N:SEQ], in1=keep[b][:, SEQ - N + 1:SEQ + 1],
                                          op=ALU.mult).then_inc(a_done, 1)
                    elif what == "split":
                        b, j = arg // PAGES, arg % PAGES
                        if j == 0:
                            if b >= 2:
                                dve.wait_ge(page_done, (b - 1) * PAGES)
                                for part in range(2):
                                    c0 = part * NS * H + (b - 2) * H
                                    chain(dve.tensor_copy(w_dec[b % 2][:, :, c0:c0 + H], zero_cols))
                            for part, w in enumerate((wk_hi, wk_lo)):
                                c0 = part * NS * H + b * H
                                chain(dve.tensor_copy(w_dec[b % 2][:, :, c0:c0 + H], w[:, :, b * H:(b + 1) * H]))
                            dve.sem_inc(wdec_ready, 1)
                        dve.wait_ge(vhi_ready, arg + 1)
                        dve.tensor_tensor(out=v_lo[arg % 3][:], in0=v_pg[arg % V_RING][:], in1=v_hi[arg % 3][:],
                                          op=ALU.subtract).then_inc(vlo_ready, 1)
                    elif what == "mask":
                        dve.wait_ge(page_done, NS * PAGES)
                        dve.wait_ge(s_c2, 48)
                        dve.tensor_tensor(out=dec_m, in0=p_dec, in1=head_mask, op=ALU.mult).then_inc(decm_ready, 1)
                    elif what == "piece":
                        j, k = arg
                        T = jobs[j]
                        if k in (2, 4):
                            n = (k - 2) // 2
                            cs = slice(n * CHUNK, (n + 1) * CHUNK)
                            dve.wait_ge(w_done, fills[j, f"h{n}"] + 1)
                            if n == 0:
                                dve.wait_ge(s_c2, 48)
                                dve.wait_ge(s_xr[j % 2], 16 * (j // 2 + 1))
                                if j >= 2:
                                    dve.wait_ge(s_hm[j % 2], 32 * (j // 2))
                            dve.tensor_tensor(out=h_sb[j % 2][:, cs], in0=bank(j, f"h{n}"), in1=x_r[j % 2][:, cs], op=ALU.add).then_inc(w_copied, 1)
                            dve.wait_ge(w_copied, fills[j, f"h{n}"] + 1)
                            dve.tensor_tensor(out=m_sb[j % 2][:, cs], in0=h_sb[j % 2][:, cs], in1=g_ffn[:, cs], op=ALU.mult).then_inc(m_ready, 1)
                        if k in (5, 6):
                            dve.wait_ge(w_done, fills[j, f"t{k - 5}"] + 1)
                            dve.tensor_copy(hT[:, 4 * (k - 5):4 * (k - 4), :].rearrange("p c n -> p (c n)"), bank(j, f"t{k - 5}")).then_inc(w_copied, 1)
                        if k == 7:
                            dve.wait_ge(w_done, fills[j, "logits"] + 1)
                            dve.tensor_copy(logits[:, T, :], p_w[:, 0:NR]).then_inc(w_copied, 1)
                dve.wait_ge(w_copied, len(fills))
        p2.close()
        mid.close()

        late = ctx.enter_context(ExitStack())
        w_pg = sb(late, "w_ple_gate_sb", [P, KD, D])
        w_pp = sb(late, "w_ple_proj_sb", [P, PLE // P, D])
        moe = ExitStack()
        m_idx = sb(moe, "m_row_of_slot", [P, N_BLK], I32)
        y_idx = sb(moe, "y_row_of_slot", [P, N_BLK], I32)
        over = sb(moe, "overflow_blocks", [P, 1 + N_OVER], I32)
        w_g = [sb(moe, f"w_gate{i}", [P, KD, F]) for i in range(2)]
        w_u = [sb(moe, f"w_up{i}", [P, KD, F]) for i in range(2)]
        w_d = [sb(moe, f"w_down{i}", [P, KF, D]) for i in range(2)]
        x_g = [sb(moe, f"x_gathered{i}", [P, MW]) for i in range(2)]
        s_wg = [sem("w_gate_loaded0"), sem("w_gate_loaded1")]
        s_wu = [sem("w_up_loaded0"), sem("w_up_loaded1")]
        s_wd = [sem("w_down_loaded0"), sem("w_down_loaded1")]
        xg_zero = sem("x_gathered_zeroed")

        def gate_rows(e):
            return A["w_gate"][e, :, :].rearrange("a (k p) n -> p (a k) n", p=P)

        def up_rows(e):
            return A["w_up"][e, :, :].rearrange("a (k p) n -> p (a k) n", p=P)

        def down_rows(e):
            return A["w_down"][e, :, :].rearrange("a (k p) n -> p (a k) n", p=P)

        p3 = ExitStack()
        T9 = T_ALL
        c3 = sb(p3, "routing_constants", [P, A["c_route"].shape[1]])
        iota128, iota_e, iota_b = c3[:, 0:128], c3[:, 128:160], c3[:, 160:160 + N_BLK]
        mult8 = c3[:, 208:216]
        valid = c3[:, 216:225]
        y_val, m_val = c3[:, 225:243].rearrange("p (a b) -> p a b", a=2), c3[:, 243:252]
        iota_o = c3[:, 252:252 + N_OVER]
        tri_f = sb(p3, "tri_f32", [P, P])
        tri = sb(p3, "tri", [P, P], BF16)
        ones_b = sb(p3, "ones_bf16", [P, P], BF16)
        a_b = sb(p3, "assigned_bf16", [P, T9, E_ALL], BF16)
        r4 = [sb(p3, f"r4_{i}", [P, T9, EG]) for i in range(4)]
        r8 = [sb(p3, f"r8_{i}", [P, T9, EPG]) for i in range(4)]
        r32 = sb(p3, "group_experts", [P, T9, E_ALL])
        oh = sb(p3, "expert_onehots", [P, 2, T9, E_ALL])
        r64 = sb(p3, "onehot_products", [P, 2, T9, E_ALL])
        pairs = sb(p3, "slots_of_choices", [P, 6, 2, T9])
        s9 = sb(p3, "scalars9", [P, 24, T9])
        pre = sb(p3, "rank_before", [P, T9, E_ALL])
        tot = sb(p3, "totals", [P, 6, E_ALL])
        cmp8 = sb(p3, "compares8", [P, E_ALL, 8])
        cmp9 = sb(p3, "compares9", [P, 2, T9, 8])
        cmp_o = sb(p3, "compares_o", [P, N_OVER, E_ALL])
        over_f = sb(p3, "overflow_f", [P, 1 + N_OVER])
        h_rs_rows = sb(p3, "h_rstd_columns", [P, T_ALL, MW - D])
        R = [sb(p3, f"row_onehot{i}", [P, P]) for i in range(4)]
        B = [sb(p3, f"block_onehot{i}", [P, 2, N_BLK]) for i in range(4)]
        tab = sb(p3, "slot_tables", [P, 2, 2, N_BLK])
        p_rank, p_tab = pb(p3, "p_rank"), pb(p3, "p_tab")
        s_c3, exp_in, exp_out, a_ready, rank_done = sem("const3_loaded"), sem("exp_wanted"), sem("exp_done"), sem("assigned"), sem("ranks_done")
        rs_in, rs_out, rs_ready, s_rs = sem("rstd_wanted"), sem("h_std"), sem("h_rstd_ready"), sem("h_rstd_stored")
        slots_ready, row_ready = sem("slots_ready"), sem("row_onehots_ready")
        oh_ready, oh_used = sem("block_onehots_ready"), sem("onehots_used")

        with nc.Block() as block:
            @block.sync
            def _(sp):
                sp.dma_start(c3[:], A["c_route"]).then_inc(s_c3, 16)
                sp.dma_start(tri_f[:], A["c_tri"]).then_inc(s_c3, 16)
                for e in range(2):
                    sp.dma_start(w_g[e][:], gate_rows(slice(e, e + 1))).then_inc(s_wg[e], 16)
                    sp.dma_start(w_u[e][:], up_rows(slice(e, e + 1))).then_inc(s_wu[e], 16)
                    sp.dma_start(w_d[e][:], down_rows(slice(e, e + 1))).then_inc(s_wd[e], 16)
                    if e == 0:
                        sp.wait_ge(rs_ready, 2)
                        with nc.allow_non_contiguous_dma(reason="the last 16 columns of each row"):
                            sp.dma_start(m_dram.rearrange("(t p) n -> p t n", p=P)[:, :, D:MW], h_rs_rows[:]).then_inc(s_rs, 16)
                sp.wait_ge(s_c3, 32)
                sp.wait_ge(s_rs, 16)

            @block.gpsimd
            def _(pool):
                pool.memset(x_g[0][:], 0.0).then_inc(xg_zero, 1)
                pool.memset(x_g[1][:], 0.0).then_inc(xg_zero, 1)
                pool.wait_ge(s_c3, 32)
                pool.wait_ge(slots_ready, 1)
                for t in range(T9):
                    for c in range(2):
                        n = 2 * t + c
                        if n >= 4:
                            pool.wait_ge(oh_used, n - 3)
                        pool.tensor_scalar(R[n % 4][:], iota128, pairs[:, 3, c, t:t + 1], None, ALU.is_equal).then_inc(row_ready, 1)

            @block.scalar
            def _(act):
                act.wait_ge(rs_in, 1)
                act.activation(h_rs[:, 1, :], h_rs[:, 0, :], ACT.Sqrt).then_inc(rs_out, 1)
                act.wait_ge(exp_in, 1)
                act.activation(r4[1][:], r4[0][:], ACT.Exp).then_inc(exp_out, 1)
                act.wait_ge(exp_in, 2)
                act.activation(s9[:, 5, :], s9[:, 4, :], ACT.Exp).then_inc(exp_out, 1)

            @block.tensor
            def _(pe):
                pe.wait_ge(a_ready, 1)
                for i in range(T9):
                    for j in range(i + 1):
                        pe.matmul(p_rank[:, i * E_ALL:(i + 1) * E_ALL], (tri if j == i else ones_b)[:], a_b[:, j, :],
                                  start=(j == 0), stop=(j == i))
                for j in range(T9):
                    ins = pe.matmul(p_rank[:, T9 * E_ALL:(T9 + 1) * E_ALL], ones_b[:], a_b[:, j, :], start=(j == 0), stop=(j == T9 - 1))
                ins.then_inc(rank_done, 1)
                for n in range(2 * T9):
                    pe.wait_ge(oh_ready, 2 * n + 2)
                    pe.wait_ge(row_ready, n + 1)
                    ins = pe.matmul(p_tab[:, 0:2 * N_BLK], R[n % 4][:], B[n % 4][:].rearrange("p a b -> p (a b)"),
                                    start=(n == 0), stop=(n == 2 * T9 - 1))
                    ins.then_inc(oh_used, 1)

            @block.vector
            def _(dve):
                chain = chains["dve"]
                chain.eng = dve
                dve.wait_ge(s_c3, 32)
                chain(dve.tensor_copy(tri[:], tri_f[:]))
                chain(dve.memset(ones_b[:], 1.0))
                V = dve

                def bc(ap, n):
                    return ap.unsqueeze(2).to_broadcast([P, T9, n])

                def tt(out, a, b, op):
                    chain(V.tensor_tensor(out=out, in0=a, in1=b, op=op))

                def ts(out, a, s1, s2, o1, o2=None):
                    if o2 is None:
                        chain(V.tensor_scalar(out, a, s1, None, o1))
                    else:
                        chain(V.tensor_scalar(out, a, s1, s2, o1, o2))

                def red(out, a, op):
                    chain(V.tensor_reduce(out=out, in_=a, axis=AX.X, op=op))

                def first_max(vals, n, top, idx, hot, tmp):
                    red(top, vals, ALU.max)
                    tt(tmp, vals, bc(top, n), ALU.is_equal)
                    ts(tmp, tmp, -64.0, 64.0, ALU.mult, ALU.add)
                    it = c3[:, 0:n].unsqueeze(1).to_broadcast([P, T9, n])
                    tt(tmp, tmp, it, ALU.add)
                    red(idx, tmp, ALU.min)
                    tt(hot, it, bc(idx, n), ALU.is_equal)

                V.tensor_scalar(h_rs[:, 0, :], h_sq[:], 1.0 / D, EPS, ALU.mult, ALU.add).then_inc(rs_in, 1)
                V.wait_ge(rs_out, 1)
                V.reciprocal(h_rs[:, 2, :], h_rs[:, 1, :]).then_inc(rs_ready, 1)
                V.wait_ge(rs_ready, 1)
                V.tensor_copy(h_rs_rows[:], bc(h_rs[:, 2, :], MW - D)).then_inc(rs_ready, 1)
                tt(logits[:], logits[:], bc(h_rs[:, 2, :], NR), ALU.mult)
                tt(logits[:], logits[:], b_rt[:].unsqueeze(1).to_broadcast([P, T9, NR]), ALU.add)
                Lg, Le = logits[:, :, 0:EG], logits[:, :, EG:NR]
                first_max(Lg, EG, s9[:, 0, :], s9[:, 1, :], r4[2][:], r4[3][:])
                V.tensor_tensor(out=r4[0][:], in0=Lg, in1=bc(s9[:, 0, :], EG), op=ALU.subtract).then_inc(exp_in, 1)
                tt(r32[:].rearrange("p t (g e) -> p t g e", g=EG), Le.rearrange("p t (g e) -> p t g e", g=EG),
                   r4[2][:].unsqueeze(3).to_broadcast([P, T9, EG, EPG]), ALU.mult)
                red(r8[0][:], r32[:].rearrange("p t (g e) -> p t e g", g=EG), ALU.add)
                first_max(r8[0][:], EPG, s9[:, 2, :], s9[:, 6, :], r8[1][:], r8[3][:])
                ts(r8[3][:], r8[1][:], -3.0e38, None, ALU.mult)
                tt(r8[2][:], r8[0][:], r8[3][:], ALU.add)
                first_max(r8[2][:], EPG, s9[:, 3, :], s9[:, 7, :], r8[1][:], r8[3][:])
                V.tensor_tensor(out=s9[:, 4, :], in0=s9[:, 3, :], in1=s9[:, 2, :], op=ALU.subtract).then_inc(exp_in, 1)
                iv = iota_e.unsqueeze(1).to_broadcast([P, T9, E_ALL])
                for c in range(2):
                    ts(s9[:, 8 + c, :], s9[:, 1, :], float(EPG), None, ALU.mult)
                    tt(s9[:, 8 + c, :], s9[:, 8 + c, :], s9[:, 6 + c, :], ALU.add)
                    tt(oh[:, c, :, :], iv, bc(s9[:, 8 + c, :], E_ALL), ALU.is_equal)
                    tt(oh[:, c, :, :], oh[:, c, :, :], bc(valid, E_ALL), ALU.mult)
                V.tensor_tensor(out=a_b[:], in0=oh[:, 0, :, :], in1=oh[:, 1, :, :], op=ALU.add).then_inc(a_ready, 1)
                V.wait_ge(rank_done, 1)
                chain(V.tensor_copy(pre[:].rearrange("p t e -> p (t e)"), p_rank[:, 0:T9 * E_ALL]))
                chain(V.tensor_copy(tot[:, 0, :], p_rank[:, T9 * E_ALL:(T9 + 1) * E_ALL]))
                tt(cmp8[:], tot[:, 0, :].unsqueeze(2).to_broadcast([P, E_ALL, 8]), mult8.unsqueeze(1).to_broadcast([P, E_ALL, 8]), ALU.is_gt)
                red(tot[:, 1, :], cmp8[:], ALU.add)
                chain(V.tensor_tensor_scan(out=tot[:, 2, :], data0=tot[:, 1, :], data1=tot[:, 1, :], initial=0.0, op0=ALU.add, op1=ALU.bypass))
                tt(tot[:, 3, :], tot[:, 2, :], tot[:, 1, :], ALU.subtract)
                tt(cmp_o[:], tot[:, 2, :].unsqueeze(1).to_broadcast([P, N_OVER, E_ALL]), iota_o.unsqueeze(2).to_broadcast([P, N_OVER, E_ALL]), ALU.is_le)
                chain(V.tensor_copy(over_f[:, 0:1], tot[:, 2, E_ALL - 1:E_ALL]))
                red(over_f[:, 1:], cmp_o[:], ALU.add)
                ts(over_f[:, 1:], over_f[:, 1:], float(E_ALL - 1), None, ALU.min)
                chain(V.tensor_copy(over[:], over_f[:]))
                expert = s9[:, 8:10, :]
                rank, base, rb, r, blk, isov = (pairs[:, q, :, :] for q in range(6))

                def both(ap, shape):
                    return ap.to_broadcast([P, 2] + shape)

                def stt(out, a, scalar, b, o1, o2):
                    chain(V.scalar_tensor_tensor(out=out, in0=a, scalar=scalar, in1=b, op0=o1, op1=o2))

                tt(r64[:], oh[:], both(pre[:].unsqueeze(1), [T9, E_ALL]), ALU.mult)
                red(rank, r64[:], ALU.add)
                tt(r64[:], oh[:], both(tot[:, 3, :].unsqueeze(1).unsqueeze(1), [T9, E_ALL]), ALU.mult)
                red(base, r64[:], ALU.add)
                tt(cmp9[:], rank.unsqueeze(3).to_broadcast([P, 2, T9, 8]), both(mult8.unsqueeze(1).unsqueeze(1), [T9, 8]), ALU.is_ge)
                red(rb, cmp9[:], ALU.add)
                stt(r, rb, -float(P), rank, ALU.mult, ALU.add)
                ts(isov, rb, 1.0, None, ALU.min)
                tt(blk, base, rb, ALU.add)
                stt(blk, blk, float(E_ALL - 1), expert, ALU.add, ALU.subtract)
                tt(blk, blk, isov, ALU.mult)
                tt(blk, blk, expert, ALU.add)
                ts(isov[:, 0, :], valid, -999.0, 999.0, ALU.mult, ALU.add)
                V.tensor_tensor(out=blk, in0=blk, in1=both(isov[:, 0:1, :], [T9]), op=ALU.add).then_inc(slots_ready, 1)
                V.wait_ge(slots_ready, 1)
                for t in range(T9):
                    for c in range(2):
                        n = 2 * t + c
                        col = blk[:, c, t:t + 1]
                        if n >= 4:
                            V.wait_ge(oh_used, n - 3)
                        V.tensor_scalar(B[n % 4][:, 0, :], iota_b, col, y_val[:, c, t:t + 1], ALU.is_equal, ALU.mult).then_inc(oh_ready, 1)
                        V.tensor_scalar(B[n % 4][:, 1, :], iota_b, col, m_val[:, t:t + 1], ALU.is_equal, ALU.mult).then_inc(oh_ready, 1)
                V.wait_ge(exp_out, 2)
                red(s9[:, 10, :], r4[1][:], ALU.add)
                ts(s9[:, 11, :], s9[:, 5, :], 1.0, None, ALU.add)
                tt(s9[:, 10, :], s9[:, 10, :], s9[:, 11, :], ALU.mult)
                chain(V.reciprocal(gate_w[:, 0, :], s9[:, 10, :]))
                tt(gate_w[:, 1, :], gate_w[:, 0, :], s9[:, 5, :], ALU.mult)
                V.wait_ge(oh_used, 2 * T9)
                chain(V.tensor_copy(tab[:, 0, :, :].rearrange("p a b -> p (a b)"), p_tab[:, 0:2 * N_BLK]))
                ts(tab[:, 1, :, :], tab[:, 0, :, :], 0.0, NONE, ALU.is_equal, ALU.mult)
                tt(tab[:, 1, :, :], tab[:, 1, :, :], tab[:, 0, :, :], ALU.add)
                ts(tab[:, 1, :, :], tab[:, 1, :, :], -1.0, None, ALU.add)
                chain(V.tensor_copy(y_idx[:], tab[:, 1, 0, :]))
                chain(V.tensor_copy(m_idx[:], tab[:, 1, 1, :]))
        p3.close()

        s_ple = sem("ple_weights_loaded")
        p4 = ExitStack()
        NCH, RING = 12, 4
        idx_m = [sb(p4, f"idx_m{i}", [P, 1], I32) for i in range(2)]
        idx_y = [sb(p4, f"idx_y{i}", [P, 1], I32) for i in range(2)]
        w_hi = [sb(p4, f"w_hi{i}", [P, 2, CHUNK], F32R) for i in range(RING)]
        w_lo = [sb(p4, f"w_lo{i}", [P, 2, CHUNK], F32R) for i in range(RING)]
        x_hi = sb(p4, "xeT_hi", [P, KD, P], F32R)
        x_lo = sb(p4, "xeT_lo", [P, KD, P], F32R)
        act_g = sb(p4, "silu_gate", [P, F])
        hid = sb(p4, "hidden", [P, F])
        h_hi = sb(p4, "hiddenT_hi", [P, KF, P], F32R)
        h_lo = sb(p4, "hiddenT_lo", [P, KF, P], F32R)
        y_sb = [sb(p4, f"y{i}", [P, D]) for i in range(2)]
        p_xe = pb(p4, "p_xe", 2 * CHUNK)
        p_g, p_u, p_ht = pb(p4, "p_g"), pb(p4, "p_u"), pb(p4, "p_ht")
        p_y = pb(p4, "p_y", 2 * CHUNK)
        s_xg = [sem("x_gathered0"), sem("x_gathered1")]
        s_ys = [sem("y_scattered0"), sem("y_scattered1")]
        idx_ready, pool_held = sem("indices_copied"), sem("pool_waits_held")
        xe_t, xhi_ready, xlo_ready = sem("xe_transposed"), sem("xeT_hi_ready"), sem("xeT_lo_ready")
        hi_ready, lo_ready, chunk_used = sem("w_hi_ready"), sem("w_lo_ready"), sem("w_chunk_used")
        silu_ready, hid_ready = sem("silu_ready"), sem("hidden_ready")
        ht_done, hhi_ready, hlo_ready = sem("hidden_transposed"), sem("hiddenT_hi_ready"), sem("hiddenT_lo_ready")
        y_a, y_v = sem("y_copied_act"), sem("y_copied_dve")

        def chunk_of(c, par):
            if c < 8:
                w, s_w = (w_g, s_wg) if c < 4 else (w_u, s_wu)
                k = 2 * (c % 4)
                return w[par][:, k:k + 2, :], s_w[par]
            n, k = (c - 8) // 2, 2 * (c % 2)
            return w_d[par][:, k:k + 2, n * CHUNK:(n + 1) * CHUNK], s_wd[par]

        def split_hi(act, c, par, loaded, nth_chunk):
            raw, s_w = chunk_of(c, par)
            act.wait_ge(s_w, loaded)
            act.wait_ge(chunk_used, nth_chunk)
            act.activation(w_hi[c % RING][:], raw, ACT.Copy).then_inc(hi_ready, 1)

        def split_lo(dve, c, par, nth_chunk):
            raw, _ = chunk_of(c, par)
            dve.wait_ge(hi_ready, nth_chunk)
            dve.tensor_tensor(out=w_lo[c % RING][:], in0=raw, in1=w_hi[c % RING][:], op=ALU.subtract).then_inc(lo_ready, 1)

        def multiply(pe, c, nth_chunk, hi_ready=hi_ready, lo_ready=lo_ready, chunk_used=chunk_used):
            if c < 8:
                out, a_hi, a_lo, k0 = (p_g if c < 4 else p_u)[:], x_hi, x_lo, 2 * (c % 4)
                first, last = c % 4 == 0, c % 4 == 3
            else:
                n = (c - 8) // 2
                out, a_hi, a_lo, k0 = p_y[:, n * CHUNK:(n + 1) * CHUNK], h_hi, h_lo, 2 * (c % 2)
                first, last = c % 2 == 0, c % 2 == 1
            pe.wait_ge(hi_ready, nth_chunk)
            for k in range(2):
                pe.matmul(out, a_hi[:, k0 + k, :], w_hi[c % RING][:, k, :], start=(first and k == 0), stop=False)
                pe.matmul(out, a_lo[:, k0 + k, :], w_hi[c % RING][:, k, :], start=False, stop=False)
            pe.wait_ge(lo_ready, nth_chunk)
            for k in range(2):
                ins = pe.matmul(out, a_hi[:, k0 + k, :], w_lo[c % RING][:, k, :], start=False, stop=(last and k == 1))
            ins.then_inc(chunk_used, 1)

        def experts(eng, body):
            for e in range(3):
                body(e, e % 2, None)
            with eng.Fori(0, (E_ALL - 6) // 2) as i:
                body(i * 2 + 3, 1, i)
                body(i * 2 + 4, 0, i)
            for e in range(E_ALL - 3, E_ALL):
                body(e, e % 2, None)

        def turn(e, par, i):
            return e // 2 + 1 if i is None else (i + 2 if par else i + 3)

        def i_of_previous(e, par, i):
            return None if i is None else (i - 1 if par else i)

        with nc.Block() as block:
            @block.sync
            def _(sp):
                def expert(e, par, i):
                    if i is None and e + 2 >= E_ALL:
                        return
                    sl = slice(e + 2, e + 3) if i is None else bass.ds(e + 2, 1)
                    sp.wait_ge(lo_ready, e * NCH + 4)
                    sp.dma_start(w_g[par][:], gate_rows(sl)).then_inc(s_wg[par], 16)
                    sp.wait_ge(lo_ready, e * NCH + 8)
                    sp.dma_start(w_u[par][:], up_rows(sl)).then_inc(s_wu[par], 16)
                    sp.wait_ge(lo_ready, e * NCH + 12)
                    sp.dma_start(w_d[par][:], down_rows(sl)).then_inc(s_wd[par], 16)

                experts(sp, expert)
                sp.dma_start(w_pg[:], A["w_ple_gate"].rearrange("(k p) n -> p k n", p=P)).then_inc(s_ple, 16)
                sp.dma_start(w_pp[:], A["w_ple_proj"].rearrange("(k p) n -> p k n", p=P)).then_inc(s_ple, 16)

            @block.gpsimd
            def _(pool):
                def gather(e, par, nth_index):
                    pool.tensor_copy(idx_m[par][:], m_idx[:, bass.ds(e, 1)]).then_inc(idx_ready, 1)
                    pool.wait_ge(idx_ready, nth_index)
                    pool.sem_inc(pool_held, 1)
                    pool.indirect_dma_start(out=x_g[par][:], out_offset=None, in_=m_dram,
                                            in_offset=bass.IndirectOffsetOnAxis(ap=idx_m[par][:, 0:1], axis=0),
                                            bounds_check=ROWS - 1, oob_is_err=False).then_inc(s_xg[par], 16)

                pool.wait_ge(xg_zero, 2)
                gather(0, 0, 1)
                gather(1, 1, 2)

                def expert(e, par, i):
                    if i is not None or e + 2 < E_ALL:
                        pool.wait_ge(hid_ready, e + 1)
                        pool.sem_inc(pool_held, 1)
                        gather(e + 2, par, e * 2 + 3)
                    pool.wait_ge(y_a, e + 1)
                    pool.wait_ge(y_v, e + 1)
                    pool.sem_inc(pool_held, 1)
                    pool.tensor_copy(idx_y[par][:], y_idx[:, bass.ds(e, 1)]).then_inc(idx_ready, 1)
                    pool.wait_ge(idx_ready, e * 2 + 4 if i is not None or e < E_ALL - 2 else E_ALL + e + 1)
                    pool.sem_inc(pool_held, 1)
                    pool.indirect_dma_start(out=y_dram, out_offset=bass.IndirectOffsetOnAxis(ap=idx_y[par][:, 0:1], axis=0),
                                            in_=y_sb[par][:], in_offset=None,
                                            bounds_check=2 * ROWS - 1, oob_is_err=False).then_inc(s_ys[par], 16)

                experts(pool, expert)
                pool.wait_ge(s_ys[0], 16 * (E_ALL // 2))
                pool.wait_ge(s_ys[1], 16 * (E_ALL // 2))

            @block.tensor
            def _(pe):
                pe.sem_inc(chunk_used, RING)

                def transpose_x(par, nth):
                    pe.wait_ge(s_xg[par], nth * 16)
                    for k in range(KD):
                        ins = pe.transpose(p_xe[:, k * P:(k + 1) * P], x_g[par][:, k * P:(k + 1) * P], ident[:])
                    ins.then_inc(xe_t, 1)

                transpose_x(0, 1)

                def expert(e, par, i):
                    last = i is None and e == E_ALL - 1
                    pe.wait_ge(xlo_ready, e + 1)
                    for c in range(8):
                        multiply(pe, c, e * NCH + c + 1)
                    if not last:
                        transpose_x(1 - par, (turn(e, par, i) + (0 if par == 0 else 1)))
                    pe.wait_ge(hid_ready, e + 1)
                    for c in range(KF):
                        ins = pe.transpose(p_ht[:, c * P:(c + 1) * P], hid[:, c * P:(c + 1) * P], ident[:])
                    ins.then_inc(ht_done, 1)
                    pe.wait_ge(hlo_ready, e + 1)
                    if not (i is None and e == 0):
                        pe.wait_ge(y_a, e)
                        pe.wait_ge(y_v, e)
                    for c in range(8, NCH):
                        multiply(pe, c, e * NCH + c + 1)

                experts(pe, expert)

            def free_y(eng, e, par, i):
                if not (i is None and e < 2):
                    eng.wait_ge(s_ys[par], (turn(e, par, i) - 1) * 16)

            @block.scalar
            def _(act):
                def copy_x(e):
                    act.wait_ge(xe_t, e + 1)
                    act.activation(x_hi[:].rearrange("p k n -> p (k n)"), p_xe[:], ACT.Copy).then_inc(xhi_ready, 1)

                def copy_y(e, par, i):
                    act.wait_ge(chunk_used, e * NCH + NCH + RING)
                    free_y(act, e, par, i)
                    act.activation(y_sb[par][:, 0:CHUNK], p_y[:, 0:CHUNK], ACT.Copy).then_inc(y_a, 1)

                for c in range(RING):
                    split_hi(act, c, 0, 16, c + 1)
                copy_x(0)

                def expert(e, par, i):
                    first, last = (i is None and e == 0), (i is None and e == E_ALL - 1)
                    loaded = turn(e, par, i) * 16
                    for c in range(RING if first else 0, 8):
                        split_hi(act, c, par, loaded, e * NCH + c + 1)
                        if c == 3 and not first:
                            copy_y(e - 1, 1 - par, i_of_previous(e, par, i))
                    if not first:
                        act.wait_ge(hid_ready, e)
                    act.activation(act_g[:], p_g[:], ACT.Silu, scale=x_g[par][:, D:D + 1]).then_inc(silu_ready, 1)
                    for c in range(8, NCH):
                        split_hi(act, c, par, loaded, e * NCH + c + 1)
                    act.wait_ge(ht_done, e + 1)
                    act.activation(h_hi[:].rearrange("p k n -> p (k n)"), p_ht[:], ACT.Copy).then_inc(hhi_ready, 1)
                    if not last:
                        copy_x(e + 1)
                    else:
                        copy_y(e, par, None)

                experts(act, expert)

            @block.vector
            def _(dve):
                def copy_x(e):
                    dve.wait_ge(xhi_ready, e + 1)
                    dve.tensor_tensor(out=x_lo[:].rearrange("p k n -> p (k n)"), in0=p_xe[:], in1=x_hi[:].rearrange("p k n -> p (k n)"),
                                      op=ALU.subtract).then_inc(xlo_ready, 1)

                def copy_y(e, par, i):
                    dve.wait_ge(chunk_used, e * NCH + NCH + RING)
                    free_y(dve, e, par, i)
                    dve.tensor_copy(y_sb[par][:, CHUNK:2 * CHUNK], p_y[:, CHUNK:2 * CHUNK]).then_inc(y_v, 1)

                for c in range(RING):
                    split_lo(dve, c, 0, c + 1)
                copy_x(0)

                def expert(e, par, i):
                    first, last = (i is None and e == 0), (i is None and e == E_ALL - 1)
                    for c in range(RING if first else 0, NCH - 1):
                        split_lo(dve, c, par, e * NCH + c + 1)
                        if c == 3 and not first:
                            copy_y(e - 1, 1 - par, i_of_previous(e, par, i))
                    dve.wait_ge(silu_ready, e + 1)
                    dve.wait_ge(chunk_used, e * NCH + 8 + RING)
                    if not first:
                        dve.wait_ge(ht_done, e)
                    dve.scalar_tensor_tensor(out=hid[:], in0=p_u[:], scalar=x_g[par][:, D:D + 1], in1=act_g[:],
                                             op0=ALU.mult, op1=ALU.mult).then_inc(hid_ready, 1)
                    split_lo(dve, NCH - 1, par, e * NCH + NCH)
                    dve.wait_ge(hhi_ready, e + 1)
                    dve.tensor_tensor(out=h_lo[:].rearrange("p k n -> p (k n)"), in0=p_ht[:], in1=h_hi[:].rearrange("p k n -> p (k n)"),
                                      op=ALU.subtract).then_inc(hlo_ready, 1)
                    if not last:
                        copy_x(e + 1)
                    else:
                        copy_y(e, par, None)

                experts(dve, expert)

        v_w, v_x, v_y = sem("over_weights"), sem("over_gathered"), sem("over_scattered")
        v_i, v_free, v_xt, v_xh, v_xl = (sem("over_indices"), sem("over_turn_free"), sem("over_x_T"), sem("over_xT_hi"),
                                         sem("over_xT_lo"))
        v_wh, v_wl, v_used = sem("over_w_hi"), sem("over_w_lo"), sem("over_chunk_used")
        v_s, v_h, v_ht, v_hh, v_hl, v_yc = (sem("over_silu"), sem("over_hidden"), sem("over_hidden_T"),
                                            sem("over_hiddenT_hi"), sem("over_hiddenT_lo"), sem("over_y_copied"))

        def over_multiply(pe, c, nth_chunk):
            multiply(pe, c, nth_chunk, v_wh, v_wl, v_used)

        with nc.Block() as block:
            def turns(eng, body, extra=None):
                n = eng.value_load(over[0:1, 0:1], min_val=0, max_val=N_OVER)
                with eng.If(n > 0):
                    with eng.Fori(0, n) as v:
                        body(v)
                        if extra:
                            extra(v)

            @block.sync
            def _(sp):
                def body(v):
                    sp.wait_ge(v_free, v + 1)
                    e = sp.value_load(over[0:1, bass.ds(v + 1, 1)], min_val=0, max_val=E_ALL - 1)
                    sp.dma_start(w_g[0][:], gate_rows(bass.ds(e, 1))).then_inc(v_w, 16)
                    sp.dma_start(w_u[0][:], up_rows(bass.ds(e, 1))).then_inc(v_w, 16)
                    sp.dma_start(w_d[0][:], down_rows(bass.ds(e, 1))).then_inc(v_w, 16)
                turns(sp, body)

            @block.gpsimd
            def _(pool):
                pool.sem_inc(v_free, 1)
                pool.sem_inc(v_used, RING)

                def body(v):
                    pool.tensor_copy(idx_m[0][:], m_idx[:, bass.ds(v + E_ALL, 1)]).then_inc(v_i, 1)
                    pool.tensor_copy(idx_y[0][:], y_idx[:, bass.ds(v + E_ALL, 1)]).then_inc(v_i, 1)
                    pool.wait_ge(v_i, v * 2 + 2)
                    pool.sem_inc(pool_held, 1)
                    pool.indirect_dma_start(out=x_g[0][:], out_offset=None, in_=m_dram,
                                            in_offset=bass.IndirectOffsetOnAxis(ap=idx_m[0][:, 0:1], axis=0),
                                            bounds_check=ROWS - 1, oob_is_err=False).then_inc(v_x, 16)
                    pool.wait_ge(v_yc, v + 1)
                    pool.sem_inc(pool_held, 1)
                    pool.indirect_dma_start(out=y_dram, out_offset=bass.IndirectOffsetOnAxis(ap=idx_y[0][:, 0:1], axis=0),
                                            in_=y_sb[0][:], in_offset=None,
                                            bounds_check=2 * ROWS - 1, oob_is_err=False).then_inc(v_y, 16)
                    pool.wait_ge(v_y, v * 16 + 16)
                    pool.sem_inc(v_free, 1)
                turns(pool, body)

            @block.tensor
            def _(pe):
                def body(v):
                    pe.wait_ge(v_x, v * 16 + 16)
                    for k in range(KD):
                        ins = pe.transpose(p_xe[:, k * P:(k + 1) * P], x_g[0][:, k * P:(k + 1) * P], ident[:])
                    ins.then_inc(v_xt, 1)
                    pe.wait_ge(v_xl, v + 1)
                    for c in range(8):
                        over_multiply(pe, c, v * NCH + c + 1)
                    pe.wait_ge(v_h, v + 1)
                    for c in range(KF):
                        ins = pe.transpose(p_ht[:, c * P:(c + 1) * P], hid[:, c * P:(c + 1) * P], ident[:])
                    ins.then_inc(v_ht, 1)
                    pe.wait_ge(v_hl, v + 1)
                    for c in range(8, NCH):
                        over_multiply(pe, c, v * NCH + c + 1)
                turns(pe, body)

            @block.scalar
            def _(act):
                def body(v):
                    act.wait_ge(v_xt, v + 1)
                    act.activation(x_hi[:].rearrange("p k n -> p (k n)"), p_xe[:], ACT.Copy).then_inc(v_xh, 1)
                    act.wait_ge(v_w, v * 48 + 48)
                    for c in range(8):
                        act.wait_ge(v_used, v * NCH + c + 1)
                        act.activation(w_hi[c % RING][:], chunk_of(c, 0)[0], ACT.Copy).then_inc(v_wh, 1)
                    act.activation(act_g[:], p_g[:], ACT.Silu, scale=x_g[0][:, D:D + 1]).then_inc(v_s, 1)
                    for c in range(8, NCH):
                        act.wait_ge(v_used, v * NCH + c + 1)
                        act.activation(w_hi[c % RING][:], chunk_of(c, 0)[0], ACT.Copy).then_inc(v_wh, 1)
                    act.wait_ge(v_ht, v + 1)
                    act.activation(h_hi[:].rearrange("p k n -> p (k n)"), p_ht[:], ACT.Copy).then_inc(v_hh, 1)
                turns(act, body)

            @block.vector
            def _(dve):
                def body(v):
                    dve.wait_ge(v_xh, v + 1)
                    dve.tensor_tensor(out=x_lo[:].rearrange("p k n -> p (k n)"), in0=p_xe[:], in1=x_hi[:].rearrange("p k n -> p (k n)"),
                                      op=ALU.subtract).then_inc(v_xl, 1)
                    for c in range(NCH):
                        dve.wait_ge(v_wh, v * NCH + c + 1)
                        dve.tensor_tensor(out=w_lo[c % RING][:], in0=chunk_of(c, 0)[0], in1=w_hi[c % RING][:], op=ALU.subtract).then_inc(v_wl, 1)
                        if c == NCH - 1:
                            dve.wait_ge(v_s, v + 1)
                            dve.scalar_tensor_tensor(out=hid[:], in0=p_u[:], scalar=x_g[0][:, D:D + 1], in1=act_g[:],
                                                     op0=ALU.mult, op1=ALU.mult).then_inc(v_h, 1)
                    dve.wait_ge(v_hh, v + 1)
                    dve.tensor_tensor(out=h_lo[:].rearrange("p k n -> p (k n)"), in0=p_ht[:], in1=h_hi[:].rearrange("p k n -> p (k n)"),
                                      op=ALU.subtract).then_inc(v_hl, 1)
                    dve.wait_ge(v_used, v * NCH + NCH + RING)
                    dve.tensor_copy(y_sb[0][:], p_y[:]).then_inc(v_yc, 1)
                turns(dve, body)
        p4.close()
        moe.close()

        p5 = ExitStack()
        wg_hi, wg_lo = (sb(p5, f"w_ple_gate_{n}", [P, KD, D], F32R) for n in ("hi", "lo"))
        wp_hi, wp_lo = (sb(p5, f"w_ple_proj_{n}", [P, PLE // P, D], F32R) for n in ("hi", "lo"))
        h_l = [sb(p5, f"h_loaded{i}", [P, D]) for i in range(2)]
        y_l = [sb(p5, f"y_loaded{i}", [P, 2, D]) for i in range(2)]
        pl = [sb(p5, f"ple_in{i}", [P, PLE]) for i in range(2)]
        h2 = [sb(p5, f"h2_{i}", [P, D]) for i in range(2)]
        n_hi, n_lo = ([sb(p5, f"h2_T_{n}{i}", [P, KD, P], F32R) for i in range(2)] for n in ("hi", "lo"))
        pl_hi, pl_lo = ([sb(p5, f"ple_T_{n}{i}", [P, PLE // P, P], F32R) for i in range(2)] for n in ("hi", "lo"))
        sg = sb(p5, "sigmoid_gate", [P, D])
        o5 = [sb(p5, f"out{i}", [P, D]) for i in range(2)]
        junk5 = sb(p5, "squares_of_h2", [P, D], BF16)
        st5 = [sb(p5, f"stats5_{i}", [P, 4]) for i in range(2)]
        p_nt = pb(p5, "p_nt", 2 * CHUNK)
        p_plt = pb(p5, "p_plt")
        p_gt = pb(p5, "p_gt", 2 * CHUNK)
        p_pp = pb(p5, "p_pp", 2 * CHUNK)
        s_l, l_base = s_qb, NS // 2
        y0_zero, h2a, h2_ready = sem("y_rows_zeroed"), sem("h_plus_first"), sem("h2_ready")
        nt_done, nhi_ready, nlo_ready = sem("h2_transposed"), sem("h2_T_hi"), sem("h2_T_lo")
        plhi_ready, pllo_ready = sem("ple_T_hi"), sem("ple_T_lo")
        whi_ready, wlo_ready = sem("ple_w_hi"), sem("ple_w_lo")
        gt_done, ss5, var5, std5, r5 = sem("ple_products_done"), sem("h2_squares"), sem("h2_var"), sem("h2_std"), sem("h2_rstd")
        sg_ready, gp_ready, o_ready = sem("sigmoid_ready"), sem("gated_ready"), sem("out_ready")
        s_o = [sem("out_stored0"), sem("out_stored1")]
        KB = KD + PLE // P

        def weight(n, k):
            cs = slice(n * CHUNK, (n + 1) * CHUNK)
            if k < KD:
                return w_pg[:, k, cs], wg_hi[:, k, cs], wg_lo[:, k, cs], g_ple_c[:, k:k + 1]
            return w_pp[:, k - KD, cs], wp_hi[:, k - KD, cs], wp_lo[:, k - KD, cs], None

        def loads(T, i, par):
            return T // 2 + 1 if i is None else (i + 1 if par else i + 2)

        with nc.Block() as block:
            @block.sync
            def _(sp):
                def load(T, par):
                    rows = bass.ts(T, P)
                    sp.dma_start(h_l[par][:], h_dram[rows, :]).then_inc(s_l[par], 16)
                    sp.dma_start(pl[par][:], A["p_all"][rows, :]).then_inc(s_l[par], 16)
                    sp.dma_start(y_l[par][:], y_dram.rearrange("(t c) n -> t c n", c=2)[rows, :, :]).then_inc(s_l[par], 16)

                sp.dma_start(h_l[0][:], h_dram[0:P, :]).then_inc(s_l[0], 16)
                sp.dma_start(pl[0][:], A["p_all"][0:P, :]).then_inc(s_l[0], 16)
                sp.wait_ge(y0_zero, 1)
                sp.dma_start(y_l[0][0:NS, :, :], y_dram.rearrange("(t c) n -> t c n", c=2)[0:NS, :, :]).then_inc(s_l[0], 16)
                load(1, 1)

                def tile(T, par, i=None):
                    if i is not None or T + 2 < T_ALL:
                        sp.wait_ge(nt_done, T + 1)
                        load(T + 2, par)
                    sp.wait_ge(o_ready, T * 2 + 2)
                    sp.dma_start(O["y_all"][bass.ts(T, P), :], o5[par][:]).then_inc(s_o[par], 16)

                tiles(sp, tile)
                sp.wait_ge(s_o[0], 16 * 6)
                sp.wait_ge(s_o[1], 16 * 5)

            @block.tensor
            def _(pe):
                def transposes(T, par):
                    pe.wait_ge(h2_ready, T + 1)
                    for k in range(KD):
                        pe.transpose(p_nt[:, k * P:(k + 1) * P], h2[par][:, k * P:(k + 1) * P], ident[:])
                    for k in range(PLE // P):
                        ins = pe.transpose(p_plt[:, k * P:(k + 1) * P], pl[par][:, k * P:(k + 1) * P], ident[:])
                    ins.then_inc(nt_done, 1)

                transposes(0, 0)

                def tile(T, par, i=None):
                    first = isinstance(T, int) and T == 0
                    pe.wait_ge(plhi_ready, T + 1)
                    pe.wait_ge(pllo_ready, T + 1)
                    pe.wait_ge(nhi_ready, T + 1)
                    pe.wait_ge(nlo_ready, T + 1)
                    for n in range(2):
                        cs = slice(n * CHUNK, (n + 1) * CHUNK)
                        if not first:
                            pe.wait_ge(gp_ready, T * 2 - 1 + n)
                        for k in range(KB):
                            _, w_h, w_l, _ = weight(n, k)
                            gate = k < KD
                            out = (p_gt if gate else p_pp)[:, cs]
                            x_h, x_l = (n_hi[par][:, k, :], n_lo[par][:, k, :]) if gate else (pl_hi[par][:, k - KD, :], pl_lo[par][:, k - KD, :])
                            if first:
                                pe.wait_ge(wlo_ready, n * KB + k + 1)
                            pe.matmul(out, x_h, w_h, start=k in (0, KD), stop=False)
                            pe.matmul(out, x_h, w_l, start=False, stop=False)
                            ins = pe.matmul(out, x_l, w_h, start=False, stop=k in (KD - 1, KB - 1))
                        ins.then_inc(gt_done, 1)
                        if n == 0 and (i is not None or T + 1 < T_ALL):
                            transposes(T + 1, 1 - par)

                tiles(pe, tile)

            @block.scalar
            def _(act):
                act.wait_ge(s_ple, 32)

                def split_hi(n, ks):
                    for k in ks:
                        raw, w_h, _, g = weight(n, k)
                        act.activation(w_h, raw, ACT.Copy, scale=1.0 if g is None else g).then_inc(whi_ready, 1)

                def stats(T, par):
                    act.wait_ge(h2_ready, T + 1)
                    if not (isinstance(T, int) and T == 0):
                        act.wait_ge(ss5, T)
                    act.activation(junk5[:], h2[par][:], ACT.Square, accum_out=st5[par][:, 0:1]).then_inc(ss5, 1)
                    act.wait_ge(nt_done, T + 1)
                    act.activation(n_hi[par][:].rearrange("p k n -> p (k n)"), p_nt[:], ACT.Copy).then_inc(nhi_ready, 1)
                    act.activation(pl_hi[par][:].rearrange("p k n -> p (k n)"), p_plt[:, 0:PLE], ACT.Copy).then_inc(plhi_ready, 1)
                    act.wait_ge(var5, T + 1)
                    act.activation(st5[par][:, 2:3], st5[par][:, 1:2], ACT.Sqrt).then_inc(std5, 1)

                split_hi(0, range(6))
                stats(0, 0)
                split_hi(0, range(6, KB))
                split_hi(1, range(KB))

                def tile(T, par, i=None):
                    if i is not None or T + 1 < T_ALL:
                        stats(T + 1, 1 - par)
                    act.wait_ge(r5, T + 1)
                    for n in range(2):
                        cs = slice(n * CHUNK, (n + 1) * CHUNK)
                        act.wait_ge(gt_done, T * 2 + n + 1)
                        if not (isinstance(T, int) and T == 0):
                            act.wait_ge(gp_ready, T * 2 - 1 + n)
                        act.activation(sg[:, cs], p_gt[:, cs], ACT.Sigmoid, scale=st5[par][:, 3:4]).then_inc(sg_ready, 1)

                tiles(act, tile)

            @block.vector
            def _(dve):
                dve.memset(y_l[0][:], 0.0).then_inc(y0_zero, 1)
                for par in range(2):
                    dve.sem_inc(s_o[par], 16)

                def split_lo(n, ks):
                    for k in ks:
                        raw, w_h, w_l, g = weight(n, k)
                        dve.wait_ge(whi_ready, n * KB + k + 1)
                        if g is None:
                            dve.tensor_tensor(out=w_l, in0=raw, in1=w_h, op=ALU.subtract).then_inc(wlo_ready, 1)
                        else:
                            dve.scalar_tensor_tensor(out=w_l, in0=raw, scalar=g, in1=w_h, op0=ALU.mult, op1=ALU.subtract).then_inc(wlo_ready, 1)

                def combine(T, par, nth):
                    dve.wait_ge(s_l[par], 48 * nth + 16 * l_base)
                    if not (isinstance(T, int) and T < 2):
                        dve.wait_ge(o_ready, T * 2 - 2)
                    dve.scalar_tensor_tensor(out=h2[par][:], in0=y_l[par][:, 0, :], scalar=gate_w[:, 0, bass.ds(T, 1)], in1=h_l[par][:],
                                             op0=ALU.mult, op1=ALU.add).then_inc(h2a, 1)
                    dve.wait_ge(h2a, T + 1)
                    dve.scalar_tensor_tensor(out=h2[par][:], in0=y_l[par][:, 1, :], scalar=gate_w[:, 1, bass.ds(T, 1)], in1=h2[par][:],
                                             op0=ALU.mult, op1=ALU.add).then_inc(h2_ready, 1)

                def norm(T, par):
                    dve.wait_ge(ss5, T + 1)
                    dve.tensor_scalar(st5[par][:, 1:2], st5[par][:, 0:1], 1.0 / D, EPS, ALU.mult, ALU.add).then_inc(var5, 1)
                    dve.wait_ge(nhi_ready, T + 1)
                    dve.tensor_tensor(out=n_lo[par][:].rearrange("p k n -> p (k n)"), in0=p_nt[:], in1=n_hi[par][:].rearrange("p k n -> p (k n)"),
                                      op=ALU.subtract).then_inc(nlo_ready, 1)
                    dve.wait_ge(plhi_ready, T + 1)
                    dve.tensor_tensor(out=pl_lo[par][:].rearrange("p k n -> p (k n)"), in0=p_plt[:, 0:PLE],
                                      in1=pl_hi[par][:].rearrange("p k n -> p (k n)"), op=ALU.subtract).then_inc(pllo_ready, 1)
                    dve.wait_ge(std5, T + 1)
                    dve.reciprocal(st5[par][:, 3:4], st5[par][:, 2:3]).then_inc(r5, 1)

                split_lo(0, range(4))
                combine(0, 0, 1)
                split_lo(0, range(4, 6))
                norm(0, 0)
                split_lo(0, range(6, KB))
                split_lo(1, range(KB))

                def tile(T, par, i=None):
                    if i is not None or T + 1 < T_ALL:
                        combine(T + 1, 1 - par, (T + 1) // 2 + 1 if i is None else i + 2)
                        norm(T + 1, 1 - par)
                    dve.wait_ge(s_o[par], loads(T, i, par) * 16)
                    for n in range(2):
                        cs = slice(n * CHUNK, (n + 1) * CHUNK)
                        dve.wait_ge(sg_ready, T * 2 + n + 1)
                        dve.tensor_tensor(out=o5[par][:, cs], in0=sg[:, cs], in1=p_pp[:, cs], op=ALU.mult).then_inc(gp_ready, 1)
                        dve.wait_ge(gp_ready, T * 2 + n + 1)
                        dve.tensor_tensor(out=o5[par][:, cs], in0=o5[par][:, cs], in1=h2[par][:, cs], op=ALU.add).then_inc(o_ready, 1)

                tiles(dve, tile)
        p5.close()
        late.close()


def constants():
    t = np.arange(P)
    band = np.zeros((P, NG, 5, P), np.float32)
    for g, w in enumerate(WINDOWS):
        s_, t_ = t[:, None], t[None, :]
        inside = (s_ <= t_) & (t_ - s_ < w)
        same = (s_ == t_).astype(np.float32)
        band[:, g, V_PREV] = (t_ + P - s_ < w) / w
        band[:, g, V_FIRST] = inside / np.minimum(t_ + 1, w) - same
        band[:, g, V_CUR] = inside / w - same
        for b in range(NS):
            for r in range(STATE):
                band[b * STATE + r, g, V_STATE, b] = (r >= STATE - (w - 1)) / w
            band[b, g, V_NEW, b] = 1.0 / w - 1.0
    r, c = np.arange(P)[:, None], np.arange(AW)[None, :]
    head_mask = (c // HD == r % H).astype(np.float32)
    sel = (r // H % NS == np.arange(NS)[None, :]).astype(np.float32)
    route = np.zeros((P, 272), np.float32)
    route[:, 0:128] = t
    route[:, 128:160] = np.arange(E_ALL)
    route[:, 160:160 + N_BLK] = np.arange(N_BLK)
    route[:, 208:216] = P * np.arange(1, 9)
    for T in range(T_ALL):
        route[:, 216 + T] = 1.0 if T else (t < NS)
        for c in range(2):
            route[:, 225 + c * 9 + T] = 2 * (T * P + t) + c + 1
        route[:, 243 + T] = T * P + t + 1
    route[:, 252:252 + N_OVER] = np.arange(N_OVER)
    return {
        "c_ident": np.eye(P, dtype=np.float32), "c_head_mask": head_mask, "c_sel": sel,
        "c_band": band, "c_route": route,
        "c_mask": np.where(t[None, :] >= t[:, None], np.float32(-240000.0), np.float32(0.0)),
        "c_tri": (t[:, None] < t[None, :]).astype(np.float32),
    }


def kernel(**inputs):
    import concourse.bacc as bacc
    from concourse.bass_utils import run_bass_kernel_spmd

    x = {k: np.asarray(v) for k, v in inputs.items()}

    def tiled(prompt, sample):
        out = np.zeros((ROWS, prompt.shape[-1]), prompt.dtype)
        out[0:NS] = sample.reshape(NS, -1)
        out[P:] = prompt.reshape(SEQ, -1)
        return out

    cols = np.zeros((P, 64), np.float32)
    for at, name in ((0, "g_mix"), (16, "g_ple")):
        cols[:, at:at + 8] = x[name][0].reshape(KD, P).T
    cols[:, 24:28] = x["s_pool"][0].reshape(NG, PW).T
    bias = x["b_sb"][0]
    cols[:, 36:44] = bias
    cols[0:NS * H, 45] = np.tile(bias, NS)
    state = np.zeros((P, AW), np.float32)
    state[0:NS * STATE] = x["state_pool"][0].reshape(NS * STATE, AW)
    x_all = tiled(x["x_prompt"], x["x_sample"])
    arrays = {
        "x_all": np.concatenate([x_all, x_all[P:2 * P]]),
        "p_all": tiled(x["p_prompt"][0], x["p_sample"][0]),
        "cache_k": x["cache_k"][0].reshape(-1, P, AW), "cache_v": x["cache_v"][0].reshape(-1, P, AW),
        "state_pool": x["state_pool"][0], "state_rows": state,
        "page_table": x["page_table"].reshape(1, -1),
        "w_in": x["w_in"][0], "w_out": x["w_out"][0],
        "w_pool": x["w_pool"][0].transpose(1, 0, 2),
        "g_qk": np.stack([np.broadcast_to(x["g_q"][0], (P, HD)), np.broadcast_to(x["g_k"][0], (P, HD))], axis=1),
        "c_cols": cols,
        "g_ffn_bc": np.broadcast_to(x["g_ffn"][0], (P, D)),
        "w_router": np.concatenate([x["w_router_group"][0], x["w_router_expert"][0]], axis=1).reshape(KD, P, NR).transpose(1, 0, 2),
        "b_router": np.broadcast_to(np.concatenate([x["b_router_group"][0], x["b_router_expert"][0]]), (P, NR)),
        "w_gate": x["w_gate"][0], "w_up": x["w_up"][0], "w_down": x["w_down"][0],
        "w_ple_gate": x["w_ple_gate"][0], "w_ple_proj": x["w_ple_proj"][0],
    }
    arrays.update(constants())
    arrays = {f"in_{k}": np.ascontiguousarray(v) for k, v in arrays.items()}
    nc = bacc.Bacc("TRN2", target_bir_lowering=False, num_devices=1)
    A = {k[3:]: nc.dram_tensor(k, v.shape, mybir.dt.from_np(v.dtype), kind="ExternalInput").ap() for k, v in arrays.items()}
    outs = {"y_all": (ROWS, D), "k_all": (ROWS, AW), "v_all": (ROWS, AW),
            "pool_prompt": (STATE, AW), "pool_sample": (NS, STATE, AW)}
    O = {k: nc.dram_tensor("out_" + k, s, F32, kind="ExternalOutput").ap() for k, s in outs.items()}
    build(nc, A, O)
    r = run_bass_kernel_spmd(nc, [arrays], core_ids=[0]).results[0]
    y, k, v = r["out_y_all"], r["out_k_all"], r["out_v_all"]
    return (y[P:].reshape(1, SEQ, D), y[0:NS].reshape(NS, 1, D),
            k[P:].reshape(1, 1, SEQ, H, HD), v[P:].reshape(1, 1, SEQ, H, HD), r["out_pool_prompt"].reshape(1, 1, STATE, AW),
            k[0:NS].reshape(1, NS, 1, H, HD), v[0:NS].reshape(1, NS, 1, H, HD), r["out_pool_sample"].reshape(1, NS, STATE, AW))
```
